# Optimizing a Trainium2 kernel written in Bass

```python
import jax, jax.numpy as jnp
from jax import lax
import numpy as np

D_MODEL = 1024
BATCH = 1
SEQ = 256
DEPTH = 2

HEAD_DIM = 64
N_HEADS_TOTAL = D_MODEL // HEAD_DIM
N_Q_HEADS = N_HEADS_TOTAL // 2
N_KV_HEADS = max(1, N_Q_HEADS // 4)
Q_PER_KV = N_Q_HEADS // N_KV_HEADS
ATTN_WIDTH = N_Q_HEADS * HEAD_DIM
KV_WIDTH = N_KV_HEADS * HEAD_DIM
N_SGU_GROUPS = N_HEADS_TOTAL - N_Q_HEADS
SGU_GROUP_DIM = HEAD_DIM
SGU_WIDTH = N_SGU_GROUPS * SGU_GROUP_DIM
MIX_WIDTH = ATTN_WIDTH + SGU_WIDTH
IN_WIDTH = ATTN_WIDTH + 2 * KV_WIDTH + 2 * SGU_WIDTH
WINDOW = 128
BLOCK = 128
SGU_CHUNK = 128
ROPE_THETA = 500000.0
ROPE_DIM = HEAD_DIM // 4
D_FF_DENSE = ((8 * D_MODEL // 3 + 255) // 256) * 256
N_EXPERTS = 8
TOP_K = 2
D_FF_EXPERT = 7 * D_MODEL // 2
EPS = 1e-6
N_DENSE = (DEPTH + 1) // 2
N_MOE = DEPTH // 2

kernel_name = "hybrid_swa_sink_sgu_moe_block"

def rmsnorm(x, g):
    xf = x.astype(jnp.float32)
    y = xf * lax.rsqrt(jnp.mean(xf * xf, axis=-1, keepdims=True) + EPS)
    return (y * g.astype(jnp.float32)).astype(x.dtype)

def partial_rope(t, positions):
    half = ROPE_DIM // 2
    inv_freq = jnp.power(jnp.float32(ROPE_THETA), -jnp.arange(0, ROPE_DIM, 2, dtype=jnp.float32) / ROPE_DIM)
    ang = positions.astype(jnp.float32)[..., None] * inv_freq
    cos = jnp.cos(ang)[:, :, None, :]
    sin = jnp.sin(ang)[:, :, None, :]
    tr = t[..., :ROPE_DIM].astype(jnp.float32)
    t1, t2 = tr[..., :half], tr[..., half:]
    rot = jnp.concatenate([t1 * cos - t2 * sin, t2 * cos + t1 * sin], axis=-1)
    return jnp.concatenate([rot.astype(t.dtype), t[..., ROPE_DIM:]], axis=-1)

def sliding_window_attention(q, k, v, sinks):
    B, S = q.shape[0], q.shape[1]
    nb = S // BLOCK
    qb = q.reshape(B, nb, BLOCK, N_KV_HEADS, Q_PER_KV, HEAD_DIM)

    def band(t):
        tb = t.reshape(B, nb, BLOCK, N_KV_HEADS, HEAD_DIM)
        prev = jnp.pad(tb, ((0, 0), (1, 0), (0, 0), (0, 0), (0, 0)))[:, :-1]
        return jnp.concatenate([prev, tb], axis=2)

    kb, vb = band(k), band(v)
    scores = jnp.einsum('bnqhgd,bnkhd->bnhgqk', qb, kb).astype(jnp.float32) * (HEAD_DIM ** -0.5)
    qi = jnp.arange(BLOCK)[:, None]
    kj = jnp.arange(2 * BLOCK)[None, :]
    dist = qi + BLOCK - kj
    in_window = (dist >= 0) & (dist < WINDOW)
    exists = (jnp.arange(nb)[:, None, None] > 0) | (kj >= BLOCK)[None]
    mask = in_window[None] & exists
    scores = jnp.where(mask[None, :, None, None], scores, -1e30)
    sink = sinks.astype(jnp.float32).reshape(N_KV_HEADS, Q_PER_KV)[None, None, :, :, None, None]
    sink = jnp.broadcast_to(sink, scores.shape[:-1] + (1,))
    probs = jax.nn.softmax(jnp.concatenate([scores, sink], axis=-1), axis=-1)[..., :-1]
    out = jnp.einsum('bnhgqk,bnkhd->bnqhgd', probs.astype(v.dtype), vb)
    return out.reshape(B, S, N_Q_HEADS * HEAD_DIM)

def spatial_gating(u, v, ln_g, ln_b, w_s, b_s):
    B, S = v.shape[0], v.shape[1]
    nc = S // SGU_CHUNK
    vg = v.reshape(B, S, N_SGU_GROUPS, SGU_GROUP_DIM).astype(jnp.float32)
    mu = jnp.mean(vg, axis=-1, keepdims=True)
    var = jnp.mean(jnp.square(vg - mu), axis=-1, keepdims=True)
    vn = (vg - mu) * lax.rsqrt(var + EPS)
    vn = vn * ln_g.astype(jnp.float32).reshape(N_SGU_GROUPS, SGU_GROUP_DIM) + ln_b.astype(jnp.float32).reshape(N_SGU_GROUPS, SGU_GROUP_DIM)
    vn = vn.astype(v.dtype).reshape(B, nc, SGU_CHUNK, N_SGU_GROUPS, SGU_GROUP_DIM)
    causal = jnp.tril(jnp.ones((SGU_CHUNK, SGU_CHUNK), dtype=bool))
    w = jnp.where(causal[None], w_s, jnp.zeros_like(w_s))
    mixed = jnp.einsum('gts,bcsgd->bctgd', w, vn) + b_s.T[None, None, :, :, None]
    ug = u.reshape(B, nc, SGU_CHUNK, N_SGU_GROUPS, SGU_GROUP_DIM)
    return (ug * mixed).reshape(B, S, SGU_WIDTH)

def swiglu(x, w_gate, w_up, w_down):
    return (jax.nn.silu(x @ w_gate) * (x @ w_up)) @ w_down

def moe_swiglu(x, w_router, e_gate, e_up, e_down):
    B, S, D = x.shape
    xt = x.reshape(B * S, D)
    logits = (xt @ w_router).astype(jnp.float32)
    top_vals, top_idx = lax.top_k(logits, TOP_K)
    top_w = jax.nn.softmax(top_vals, axis=-1)
    gates = jnp.sum(jax.nn.one_hot(top_idx, N_EXPERTS, dtype=jnp.float32) * top_w[..., None], axis=1)
    out = jnp.zeros((B * S, D), dtype=jnp.float32)
    for e in range(N_EXPERTS):
        h = jax.nn.silu(xt @ e_gate[e]) * (xt @ e_up[e])
        out = out + gates[:, e:e + 1] * (h @ e_down[e]).astype(jnp.float32)
    return out.astype(x.dtype).reshape(B, S, D)

def setup_inputs(seed: int = 0) -> dict:
    key = jax.random.key(seed)
    ks = jax.random.split(key, 24)
    f32 = jnp.float32

    def w(k, shape, fan_in):
        return jax.random.normal(k, shape, f32) * (fan_in ** -0.5)

    def gain(k, shape):
        return 1.0 + 0.1 * jax.random.normal(k, shape, f32)

    x = jax.random.normal(ks[0], (BATCH, SEQ, D_MODEL), f32)
    offset = jax.random.randint(ks[1], (BATCH, 1), 0, 1024, dtype=jnp.int32)
    positions = offset + jnp.arange(SEQ, dtype=jnp.int32)[None, :]
    return {
        "x": x,
        "positions": positions,
        "pre_mix_norm": gain(ks[2], (DEPTH, D_MODEL)),
        "w_in": w(ks[3], (DEPTH, D_MODEL, IN_WIDTH), D_MODEL),
        "attn_sinks": jax.random.normal(ks[4], (DEPTH, N_Q_HEADS), f32),
        "sgu_ln_g": gain(ks[5], (DEPTH, SGU_WIDTH)),
        "sgu_ln_b": 0.1 * jax.random.normal(ks[6], (DEPTH, SGU_WIDTH), f32),
        "sgu_w": w(ks[7], (DEPTH, N_SGU_GROUPS, SGU_CHUNK, SGU_CHUNK), SGU_CHUNK),
        "sgu_b": gain(ks[8], (DEPTH, N_SGU_GROUPS, SGU_CHUNK)),
        "attn_out_norm": gain(ks[9], (DEPTH, ATTN_WIDTH)),
        "sgu_out_norm": gain(ks[10], (DEPTH, SGU_WIDTH)),
        "w_out": w(ks[11], (DEPTH, MIX_WIDTH, D_MODEL), MIX_WIDTH),
        "post_mix_norm": gain(ks[12], (DEPTH, D_MODEL)),
        "pre_ffn_norm": gain(ks[13], (DEPTH, D_MODEL)),
        "post_ffn_norm": gain(ks[14], (DEPTH, D_MODEL)),
        "ffn_w_gate": w(ks[15], (N_DENSE, D_MODEL, D_FF_DENSE), D_MODEL),
        "ffn_w_up": w(ks[16], (N_DENSE, D_MODEL, D_FF_DENSE), D_MODEL),
        "ffn_w_down": w(ks[17], (N_DENSE, D_FF_DENSE, D_MODEL), D_FF_DENSE),
        "moe_router": w(ks[18], (N_MOE, D_MODEL, N_EXPERTS), D_MODEL),
        "moe_w_gate": w(ks[19], (N_MOE, N_EXPERTS, D_MODEL, D_FF_EXPERT), D_MODEL),
        "moe_w_up": w(ks[20], (N_MOE, N_EXPERTS, D_MODEL, D_FF_EXPERT), D_MODEL),
        "moe_w_down": w(ks[21], (N_MOE, N_EXPERTS, D_FF_EXPERT, D_MODEL), D_FF_EXPERT),
    }

def reference(x, positions, pre_mix_norm, w_in, attn_sinks, sgu_ln_g, sgu_ln_b, sgu_w, sgu_b,
              attn_out_norm, sgu_out_norm, w_out, post_mix_norm, pre_ffn_norm, post_ffn_norm,
              ffn_w_gate, ffn_w_up, ffn_w_down, moe_router, moe_w_gate, moe_w_up, moe_w_down):
    B, S, _ = x.shape
    cuts = [ATTN_WIDTH, ATTN_WIDTH + KV_WIDTH, ATTN_WIDTH + 2 * KV_WIDTH, ATTN_WIDTH + 2 * KV_WIDTH + SGU_WIDTH]
    h = x
    for layer in range(DEPTH):
        hn = rmsnorm(h, pre_mix_norm[layer])
        z = hn @ w_in[layer]
        q, k, v, zu, zv = jnp.split(z, cuts, axis=-1)
        q = partial_rope(q.reshape(B, S, N_Q_HEADS, HEAD_DIM), positions)
        k = partial_rope(k.reshape(B, S, N_KV_HEADS, HEAD_DIM), positions)
        v = v.reshape(B, S, N_KV_HEADS, HEAD_DIM)
        attn = sliding_window_attention(q, k, v, attn_sinks[layer])
        sgu = spatial_gating(jax.nn.gelu(zu), jax.nn.gelu(zv), sgu_ln_g[layer], sgu_ln_b[layer],
                             sgu_w[layer], sgu_b[layer])
        merged = jnp.concatenate([rmsnorm(attn, attn_out_norm[layer]),
                                  rmsnorm(sgu, sgu_out_norm[layer])], axis=-1)
        h = h + rmsnorm(merged @ w_out[layer], post_mix_norm[layer])
        y = rmsnorm(h, pre_ffn_norm[layer])
        if layer % 2 == 0:
            i = layer // 2
            f = swiglu(y, ffn_w_gate[i], ffn_w_up[i], ffn_w_down[i])
        else:
            i = layer // 2
            f = moe_swiglu(y, moe_router[i], moe_w_gate[i], moe_w_up[i], moe_w_down[i])
        h = h + rmsnorm(f, post_ffn_norm[layer])
    return h


_drawn_inputs = setup_inputs


def setup_inputs(seed=0):
    import zlib

    import numpy as np

    out = dict(_drawn_inputs(seed))
    spreads = {}
    factors = {}
    for name, (base, spread) in spreads.items():
        noise = np.random.default_rng([zlib.crc32(name.encode()), seed]).standard_normal(out[name].shape)
        drawn = base * np.exp(spread * noise) if base else spread * noise
        out[name] = __import__('jax').numpy.asarray(drawn.astype(out[name].dtype))
    for name, factor in factors.items():
        out[name] = (out[name] * factor).astype(out[name].dtype)
    return out
```

```python
from contextlib import ExitStack

import numpy as np

import concourse.bass as bass
from concourse import mybir

F32 = mybir.dt.float32
F32R = mybir.dt.float32r
I32 = mybir.dt.int32
ALU = mybir.AluOpType
ACT = mybir.ActivationFunctionType
AX = mybir.AxisListType

P = 128
D = 1024
S = 256
T = S // P
KC = D // P
DEPTH = 2
HD = 64
NQ, NKV = 8, 2
QPK = NQ // NKV
AW = NQ * HD
KVW = NKV * HD
NG = 8
GD = 64
SW = NG * GD
HALF = 8
THETA, ROPE_DIM = 500000.0, 16
FD = 2816
FE = 3584
NE = 8
EPS = 1e-6
NEG = -1e30
BANK = 512

UW = 1024
NRAW = 12
NSPL = 6
Z_UNITS, O_UNITS = 14, 8
MIX_UNITS = Z_UNITS + O_UNITS
GU_UNITS, DN_UNITS = 8, 4
BODY = GU_UNITS + DN_UNITS
DG = FD // BANK
EG = FE // BANK
DENSE0 = MIX_UNITS
DENSE_UNITS = DG * BODY + BODY // 2
MIX1 = DENSE0 + DENSE_UNITS
MOE0 = MIX1 + MIX_UNITS
EXPERT_UNITS = EG * BODY
assert NRAW == BODY and BODY % NSPL == 0 and FD % BANK == BANK // 2 and FE % BANK == 0


def trunk(nc, x, positions, pre_mix_norm, w_in, attn_sinks, sgu_ln_g, sgu_ln_b, sgu_w, sgu_b, attn_out_norm,
          sgu_out_norm, w_out, post_mix_norm, pre_ffn_norm, post_ffn_norm, ffn_w_gate, ffn_w_up, ffn_w_down,
          moe_router, moe_w_gate, moe_w_up, moe_w_down, out):
    ctx = ExitStack()
    with ctx:
        def sb(name, shape, dt=F32):
            return ctx.enter_context(nc.sbuf_tensor(name, shape, dt))

        def sem(name):
            return ctx.enter_context(nc.semaphore(name))

        raw = sb("raw", [P, NRAW, UW])
        w_hi = sb("w_hi", [P, NSPL, UW], F32R)
        w_lo = sb("w_lo", [P, NSPL, UW], F32R)
        h = sb("h", [P, T, D])
        tok = sb("tok", [P, T, D])
        act_hi = sb("act_hi", [P, KC, S], F32R)
        act_lo = sb("act_lo", [P, KC, S], F32R)
        g_pre = sb("g_pre", [P, D])
        g_out = sb("g_out", [P, D])
        g_post = sb("g_post", [P, D])
        g_ln = sb("g_ln", [P, 2, SW])
        qk = sb("qk", [P, T, NQ + NKV, HD])
        vv = sb("vv", [P, T, KVW])
        qk_t = sb("qk_t", [P, (NQ + NKV) // 2, S])
        ug = sb("ug", [P, T, SW])
        vg = sb("vg", [P, T, SW])
        ws_t = sb("ws_t", [P, NG, P])
        shared = sb("shared", [P, 6144])
        ht_hi = sb("ht_hi", [P, 4, T, P], F32R)
        ht_lo = sb("ht_lo", [P, 4, T, P], F32R)
        ident = sb("ident", [P, P])
        ones = sb("ones", [P, P])
        upper = sb("upper", [P, P])
        mask = sb("mask", [P, 2 * P])
        iota_i = sb("iota_i", [P, P], I32)
        iota = sb("iota", [P, P])
        inv_freq = sb("inv_freq", [P, HALF])
        pos_i = sb("pos_i", [P, T], I32)
        pos = sb("pos", [P, T])
        ang = sb("ang", [P, T, HALF])
        turns = sb("turns", [P, T, HALF])
        cos = sb("cos", [P, T, HALF])
        sin = sb("sin", [P, T, HALF])
        sinks = sb("sinks", [P, DEPTH, NQ])
        sb_rows = sb("sb_rows", [NG, P])
        sb_t = sb("sb_t", [P, NG])
        eps = sb("eps", [P, 1])
        half_pi = sb("half_pi", [P, 1])
        ssq = sb("ssq", [P, T, 2])
        std = sb("std", [P, T, 2])
        rstd = sb("rstd", [P, T, 2])
        ln_mu = sb("ln_mu", [P, T * NG])
        ln_var = sb("ln_var", [P, T * NG])
        ln_std = sb("ln_std", [P, T * NG])
        mx = sb("mx", [P, T, NQ])
        nmx = sb("nmx", [P, T, NQ])
        sink_d = sb("sink_d", [P, T, NQ])
        sink_e = sb("sink_e", [P, T, NQ])
        rsum = sb("rsum", [P, T, NQ])
        rinv = sb("rinv", [P, T, NQ])
        wr = sb("wr", [P, KC, NE])
        wr_hi = sb("wr_hi", [P, KC, NE], F32R)
        wr_lo = sb("wr_lo", [P, KC, NE], F32R)
        lg = sb("lg", [P, T, NE])
        pick = sb("pick", [P, 2, T, NE])
        cand = sb("cand", [P, T, NE])
        top = sb("top", [P, 2, T])
        at = sb("at", [P, T])
        e2 = sb("e2", [P, T])
        g12 = sb("g12", [P, 2, T])
        chosen = sb("chosen", [P, T, NE])
        gate = sb("gate", [P, T, 2 * NE])
        rank = sb("rank", [P, T, 2 * NE])
        cnt = sb("cnt", [P, 1])
        n_exp_f = sb("n_exp_f", [P, 1])
        n_exp = sb("n_exp", [P, 1], I32)

        sc = [shared[:, 0:1024].rearrange("p (h k) -> p h k", h=NQ),
              shared[:, 1024:3072].rearrange("p (h k) -> p h k", h=NQ)]
        pt = shared[:, 3072:6144].rearrange("p (b q) -> p b q", b=24)
        rot = shared[:, 0:4 * T * (NQ + NKV) * HALF].rearrange("p (r t h j) -> p r t h j", r=4, t=T, h=NQ + NKV)
        facc = shared[:, 0:2048].rearrange("p (t d) -> p t d", t=T)
        sil = shared[:, 2048:3072].rearrange("p (t f) -> p t f", t=T)
        hid = shared[:, 3072:4096].rearrange("p (t f) -> p t f", t=T)
        y = shared[:, 4096:5120]
        sel = shared[:, 5120:5376].rearrange("p (t j) -> p t j", t=T)
        sel_g = shared[:, 5376:5632].rearrange("p (t j) -> p t j", t=T)
        sel_t = shared[:, 5632:5888].rearrange("p (t j) -> p t j", t=T)
        sq = shared[:, 5120:6144]
        ws_raw = ug[:, :, :].rearrange("p t (g s) -> p (t g) s", s=P)
        ln_sq = tok[:, :, AW:AW + SW]
        xe_hi = act_hi[:, :, 0:P]
        xe_lo = act_lo[:, :, 0:P]

        ps = ctx.enter_context(nc.psum_tensor("ps", [P, 8, BANK], F32))

        raw_arrived = [sem(f"raw_arrived{i}") for i in range(NRAW)]
        hi_ready = sem("hi_ready")
        lo_ready = sem("lo_ready")
        unit_used = sem("unit_used")
        x_loaded = sem("x_loaded")
        small_loaded = sem("small_loaded")
        pre_loaded, out_loaded, post_loaded, ln_loaded = (sem(f"{n}_gain_loaded") for n in ("pre", "out", "post", "ln"))
        ws_loaded = sem("ws_loaded")
        sb_loaded = sem("sb_loaded")
        ws_masked = sem("ws_masked")
        consts_ready = sem("consts_ready")
        pool_step = sem("pool_step")
        act_step = sem("act_step")
        dve_step = sem("dve_step")
        angle_ready = sem("angle_ready")
        sincos_ready = sem("sincos_ready")
        std_ready = sem("std_ready")
        tok_ready = sem("tok_ready")
        tok_turned = sem("tok_turned")
        act_hi_ready = sem("act_hi_ready")
        act_lo_ready = sem("act_lo_ready")
        ws_turned = sem("ws_turned")
        ws_copied = sem("ws_copied")
        qkv_copied = sem("qkv_copied")
        qk_roped = sem("qk_roped")
        qk_turned = sem("qk_turned")
        qk_t_act = sem("qk_t_act")
        qk_t_dve = sem("qk_t_dve")
        gelu_done = sem("gelu_done")
        scores_done = sem("scores_done")
        max_ready = sem("max_ready")
        probs_ready = sem("probs_ready")
        sink_ready = sem("sink_ready")
        probs_turned = sem("probs_turned")
        pt_ready = sem("pt_ready")
        pv_done = sem("pv_done")
        attn_ready = sem("attn_ready")
        var_ready = sem("var_ready")
        ln_std_ready = sem("ln_std_ready")
        vn_ready = sem("vn_ready")
        sgu_done = sem("sgu_done")
        sgu_ready = sem("sgu_ready")
        h_updated = sem("h_updated")
        sil_ready = sem("sil_ready")
        hid_ready = sem("hid_ready")
        hid_turned = sem("hid_turned")
        ht_hi_ready = sem("ht_hi_ready")
        ht_lo_ready = sem("ht_lo_ready")
        part_done = sem("part_done")
        part_added = sem("part_added")
        logits_done = sem("logits_done")
        top_ready = sem("top_ready")
        e2_ready = sem("e2_ready")
        chosen_ready = sem("chosen_ready")
        counts_done = sem("counts_done")
        n_exp_ready = sem("n_exp_ready")
        sel_ready = sem("sel_ready")
        gathered = sem("gathered")
        xe_hi_ready = sem("xe_hi_ready")
        xe_lo_ready = sem("xe_lo_ready")
        sel_t_ready = sem("sel_t_ready")
        y_act = sem("y_act")
        y_dve = sem("y_dve")
        out_stored = sem("out_stored")

        DENSE_TILES = T * (DG + 1)
        DENSE_PARTS = 2 * T * (DG + 1)
        ADDED0 = 2 + DENSE_PARTS + 2

        def stacked(w):
            return w.rearrange("(k p) c -> p k c", p=P)

        def unit_view(ring, slot, k):
            return ring[:, slot, :].rearrange("p (k c) -> p k c", k=k)

        block = ctx.enter_context(nc.Block())

        @block.sync
        def _(sp):
            def load(m, src, k, loops=0):
                if m >= NRAW:
                    sp.wait_ge(lo_ready, m - NRAW + 1 + BODY * loops)
                sp.dma_start(unit_view(raw, m % NRAW, k), src).then_inc(raw_arrived[m % NRAW], 16)

            def mixer_units(layer, m):
                for c0, width in ((0, AW), (AW, 2 * KVW), (AW + 2 * KVW, SW), (AW + 2 * KVW + SW, SW)):
                    k = UW // width
                    for r in range(0, KC, k):
                        load(m, stacked(w_in[layer, r * P:(r + k) * P, c0:c0 + width]), k)
                        m += 1
                for r in range(0, KC, 2):
                    for c0 in (0, BANK):
                        load(m, stacked(w_out[layer, r * P:(r + 2) * P, c0:c0 + BANK]), 2)
                        m += 1

            def gate_up(m, w_gate, w_up, c0, loops=0):
                for w in (w_gate, w_up):
                    for r in range(0, KC, 2):
                        load(m, stacked(w[r * P:(r + 2) * P, bass.ds(c0, BANK)]), 2, loops)
                        m += 1

            def down(m, w_down, r0, loops=0, chunks=4):
                for c in range(chunks):
                    load(m, stacked(w_down[bass.ds(r0 + c * P, P), :]), 1, loops)
                    m += 1

            sp.dma_start(h[:, :, :], x[0].rearrange("(t p) d -> p t d", p=P)).then_inc(x_loaded, 16)
            mixer_units(0, 0)
            wg, wu, wd = ffn_w_gate[0], ffn_w_up[0], ffn_w_down[0]
            gate_up(DENSE0, wg, wu, 0)
            with sp.Fori(0, DG - 1) as g:
                gate_up(DENSE0 + GU_UNITS, wg, wu, (g + 1) * BANK, g)
                down(DENSE0 + BODY + DN_UNITS, wd, g * BANK, g)
            m = DENSE0 + GU_UNITS + (DG - 1) * BODY
            for w in (wg, wu):
                for r in (0, 4):
                    load(m, stacked(w[r * P:(r + 4) * P, DG * BANK:FD]), 4)
                    m += 1
            down(m, wd, (DG - 1) * BANK)
            down(m + DN_UNITS, wd, DG * BANK, chunks=2)
            mixer_units(1, MIX1)

            def experts(first_loop):
                with sp.Fori(0, NE) as e:
                    wg = moe_w_gate[0, bass.ds(e, 1)].rearrange("a d f -> (a d) f")
                    wu = moe_w_up[0, bass.ds(e, 1)].rearrange("a d f -> (a d) f")
                    wd = moe_w_down[0, bass.ds(e, 1)].rearrange("a f d -> (a f) d")
                    done = first_loop + EG * e
                    gate_up(MOE0, wg, wu, 0, done)
                    with sp.Fori(0, EG - 1) as g:
                        gate_up(MOE0 + GU_UNITS, wg, wu, (g + 1) * BANK, done + g)
                        down(MOE0 + 2 * GU_UNITS, wd, g * BANK, done + g)
                    down(MOE0 + GU_UNITS, wd, (EG - 1) * BANK, done + EG - 1)

            experts(0)
            sp.wait_ge(n_exp_ready, 1)
            n = sp.value_load(n_exp[0:1, 0:1], min_val=NE, max_val=2 * NE)
            with sp.If(n > NE):
                experts(EG * NE)
            sp.wait_ge(h_updated, 4 * DEPTH)
            sp.dma_start(out[0].rearrange("(t p) d -> p t d", p=P), h[:, :, :]).then_inc(out_stored, 16)
            sp.wait_ge(out_stored, 16)

        @block.gpsimd
        def _(pool):
            steps = [0]

            def link(ins):
                steps[0] += 1
                ins.then_inc(pool_step, 1)
                pool.wait_ge(pool_step, steps[0])

            def gain(dst, rows, loaded):
                for n, row in enumerate(rows):
                    width = row.shape[-1]
                    pool.dma_start(dst[:, n * width:(n + 1) * width],
                                   row.to_broadcast([P, width])).then_inc(loaded, 16)

            def gating_weights(layer):
                pool.dma_start(ws_raw, sgu_w[layer].rearrange("g t s -> t g s")).then_inc(ws_loaded, 16)
                pool.dma_start(sb_rows[:, :], sgu_b[layer]).then_inc(sb_loaded, 16)
                pool.wait_ge(ws_loaded, 16 * (layer + 1))
                nc.gpsimd.affine_select(out=ws_raw, in_=ws_raw, compare_op=ALU.is_ge, fill=0.0, base=0,
                                        pattern=[[0, NG], [-1, P]], channel_multiplier=1).then_inc(ws_masked, 1)

            with nc.allow_non_contiguous_dma(reason="256 positions, one per partition"):
                pool.dma_start(pos_i[:, :], positions.rearrange("o (t p) -> p (o t)", p=P)).then_inc(small_loaded, 16)
            pool.dma_start(sinks[:, :, :].rearrange("p l h -> p (l h)"),
                           attn_sinks.rearrange("l h -> (l h)").unsqueeze(0).to_broadcast([P, DEPTH * NQ])
                           ).then_inc(small_loaded, 16)
            pool.dma_start(wr[:, :, :], stacked(moe_router[0])).then_inc(small_loaded, 16)
            gain(g_pre, [pre_mix_norm[0:1, :]], pre_loaded)
            nc.gpsimd.memset(eps[:, :], EPS)
            nc.gpsimd.memset(half_pi[:, :], float(np.pi / 2))
            for j in range(HALF):
                f = np.power(np.float32(THETA), -np.float32(2 * j) / np.float32(ROPE_DIM), dtype=np.float32)
                nc.gpsimd.memset(inv_freq[:, j:j + 1], float(f))
            nc.gpsimd.memset(ones[:, :], 1.0)
            nc.gpsimd.memset(ident[:, :], 0.0)
            nc.gpsimd.memset(upper[:, :], 1.0)
            nc.gpsimd.iota(iota_i[:, :], pattern=[[1, P]], base=0, channel_multiplier=0)
            link(nc.gpsimd.memset(mask[:, :], 0.0))
            nc.gpsimd.affine_select(out=ident[:, :], in_=ident[:, :], compare_op=ALU.not_equal, fill=1.0, base=0,
                                    pattern=[[-1, P]], channel_multiplier=1)
            nc.gpsimd.affine_select(out=upper[:, :], in_=upper[:, :], compare_op=ALU.is_ge, fill=0.0, base=0,
                                    pattern=[[1, P]], channel_multiplier=-1)
            nc.gpsimd.affine_select(out=mask[:, 0:P], in_=mask[:, 0:P], compare_op=ALU.is_ge, fill=NEG, base=-1,
                                    pattern=[[1, P]], channel_multiplier=-1)
            nc.gpsimd.affine_select(out=mask[:, P:2 * P], in_=mask[:, P:2 * P], compare_op=ALU.is_ge, fill=NEG,
                                    base=0, pattern=[[-1, P]], channel_multiplier=1).then_inc(consts_ready, 1)
            gating_weights(0)
            gain(g_ln[:, :, :].rearrange("p a c -> p (a c)"), [sgu_ln_g[0:1, :], sgu_ln_b[0:1, :]], ln_loaded)
            gain(g_out, [attn_out_norm[0:1, :], sgu_out_norm[0:1, :]], out_loaded)
            gain(g_post, [post_mix_norm[0:1, :]], post_loaded)
            for layer in range(DEPTH):
                pool.wait_ge(tok_ready, 6 * layer + 2)
                gain(g_pre, [pre_ffn_norm[layer:layer + 1, :]], pre_loaded)
                if layer + 1 < DEPTH:
                    nxt = slice(layer + 1, layer + 2)
                    pool.wait_ge(vn_ready, layer + 1)
                    gain(g_ln[:, :, :].rearrange("p a c -> p (a c)"), [sgu_ln_g[nxt, :], sgu_ln_b[nxt, :]], ln_loaded)
                    pool.wait_ge(sgu_ready, 2 * (layer + 1))
                    gating_weights(layer + 1)
                    pool.wait_ge(tok_ready, 6 * layer + 4)
                    gain(g_out, [attn_out_norm[nxt, :], sgu_out_norm[nxt, :]], out_loaded)
                pool.wait_ge(h_updated, 4 * layer + 2)
                gain(g_post, [post_ffn_norm[layer:layer + 1, :]], post_loaded)
                if layer + 1 < DEPTH:
                    pool.wait_ge(tok_ready, 6 * layer + 6)
                    gain(g_pre, [pre_mix_norm[nxt, :]], pre_loaded)
                    pool.wait_ge(h_updated, 4 * layer + 4)
                    gain(g_post, [post_mix_norm[nxt, :]], post_loaded)

        @block.scalar
        def _(act):
            steps = [0]
            A = nc.scalar.activation

            def link(ins):
                steps[0] += 1
                ins.then_inc(act_step, 1)
                act.wait_ge(act_step, steps[0])

            def split(m, loops=0):
                act.wait_ge(raw_arrived[m % NRAW], 16 * (m // NRAW + 1) + 16 * loops)
                if m >= NSPL:
                    act.wait_ge(unit_used, m - NSPL + 1 + BODY * loops)
                A(w_hi[:, m % NSPL, :], raw[:, m % NRAW, :], ACT.Copy).then_inc(hi_ready, 1)

            def splits(a, b, loops=0):
                for m in range(a, b):
                    split(m, loops)

            def root(n_parts, width):
                A(std[:, :, 0:n_parts], ssq[:, :, 0:n_parts], ACT.Sqrt, bias=eps[:, :],
                  scale=1.0 / width).then_inc(std_ready, 1)

            def squares(srcs, width):
                for t, part, src in srcs:
                    link(A(sq[:, 0:width], src, ACT.Square, accum_out=ssq[:, t, part:part + 1]))

            def pre_norm():
                squares([(t, 0, h[:, t, :]) for t in range(T)], D)
                root(1, D)

            def act_high(s):
                for b in range(4):
                    act.wait_ge(tok_turned, 4 * s + b + 1)
                    A(act_hi[:, 2 * b:2 * b + 2, :], ps[:, b, :].rearrange("p (k t) -> p k t", k=2),
                      ACT.Copy).then_inc(act_hi_ready, 1)

            def mixer(layer, m):
                if layer:
                    act.wait_ge(h_updated, 4 * layer)
                else:
                    act.wait_ge(consts_ready, 1)
                    act.wait_ge(x_loaded, 16)
                pre_norm()
                act_high(3 * layer)
                splits(m + 6, m + 12)
                act.wait_ge(unit_used, m + 4)
                for t in range(T):
                    A(qk[:, t, 0:NQ, :].rearrange("p (i j) d -> p j i d", j=NKV),
                      ps[:, 4 + t, :].rearrange("p (j i d) -> p j i d", j=NKV, i=QPK), ACT.Copy,
                      scale=HD ** -0.5).then_inc(qkv_copied, 1)
                act.wait_ge(unit_used, m + 6)
                A(qk[:, :, NQ:, :].rearrange("p t j d -> p t (j d)"), ps[:, 6:8, 0:KVW], ACT.Copy).then_inc(qkv_copied, 1)
                A(vv[:, :, :], ps[:, 6:8, KVW:2 * KVW], ACT.Copy).then_inc(qkv_copied, 1)
                splits(m + 12, m + 16)
                act.wait_ge(unit_used, m + 10)
                for t in range(T):
                    A(ug[:, t, :], ps[:, t, :], ACT.Gelu_apprx_tanh).then_inc(gelu_done, 1)
                splits(m + 16, m + 18)
                for b in (0, 2):
                    act.wait_ge(qk_turned, 3 * layer + b + 1)
                    n = 2 if b == 0 else 1
                    A(qk_t[:, 2 * b:2 * b + n, :], ps[:, 4 + b, 0:n * S].rearrange("p (k t) -> p k t", k=n),
                      ACT.Copy).then_inc(qk_t_act, 1)
                act.wait_ge(unit_used, m + 14)
                for t in range(T):
                    A(vg[:, t, :], ps[:, 2 + t, :], ACT.Gelu_apprx_tanh).then_inc(gelu_done, 1)
                splits(m + 18, m + 20)
                for t in range(T):
                    act.wait_ge(max_ready, T * layer + t + 1)
                    for hh in range(NQ):
                        A(sc[t][:, hh, :], sc[t][:, hh, :], ACT.Exp, bias=nmx[:, t, hh:hh + 1],
                          accum_out=rsum[:, t, hh:hh + 1]).then_inc(probs_ready, 1)
                A(sink_e[:, :, :], sink_d[:, :, :], ACT.Exp).then_inc(sink_ready, 1)
                act.wait_ge(var_ready, layer + 1)
                A(ln_std[:, :], ln_var[:, :], ACT.Sqrt, bias=eps[:, :], scale=1.0 / GD).then_inc(ln_std_ready, 1)
                for b, bank in enumerate((4, 5, 0, 1, 2, 3)):
                    act.wait_ge(probs_turned, 6 * layer + b + 1)
                    A(pt[:, 4 * b:4 * b + 4, :], ps[:, bank, :].rearrange("p (n q) -> p n q", n=4),
                      ACT.Copy).then_inc(pt_ready, 1)
                act.wait_ge(attn_ready, T * (layer + 1))
                squares([(t, 0, tok[:, t, 0:AW]) for t in range(T)], AW)
                act.wait_ge(sgu_ready, 2 * (layer + 1))
                squares([(t, 1, tok[:, t, AW:]) for t in range(T)], SW)
                root(2, AW)
                act_high(3 * layer + 1)
                splits(m + 20, m + 22)
                act.wait_ge(unit_used, m + MIX_UNITS)
                squares([(t, 0, ps[:, 4 + 2 * t:6 + 2 * t, :].rearrange("p b c -> p (b c)")) for t in range(T)], D)
                root(1, D)
                splits(m + 22, m + 28)
                act.wait_ge(h_updated, 4 * layer + 2)
                pre_norm()
                act_high(3 * layer + 2)

            def silu(units, n, tiles, width=BANK, split_banks=False):
                act.wait_ge(unit_used, units)
                for t in range(tiles):
                    A(sil[:, t, 0:width], ps[:, 2 * t, 0:width], ACT.Silu).then_inc(sil_ready, 1)

            def turned(n, tiles, chunks=4):
                for t in range(tiles):
                    act.wait_ge(hid_turned, n + t + 1)
                    A(ht_hi[:, 0:chunks, t, :], ps[:, 6 + t, 0:chunks * P].rearrange("p (c j) -> p c j", c=chunks),
                      ACT.Copy).then_inc(ht_hi_ready, 1)

            act.wait_ge(angle_ready, 1)
            act.wait_ge(consts_ready, 1)
            A(sin[:, :, :], ang[:, :, :], ACT.Sin).then_inc(sincos_ready, 1)
            A(cos[:, :, :], turns[:, :, :], ACT.Sin, scale=-1.0, bias=half_pi[:, :]).then_inc(sincos_ready, 1)
            A(wr_hi[:, :, :], wr[:, :, :], ACT.Copy).then_inc(sincos_ready, 1)

            splits(0, 6)
            mixer(0, 0)

            m = DENSE0
            splits(m + 6, m + 12)
            silu(m + 8, 0, T)
            splits(m + 12, m + 14)
            turned(0, T)
            m = DENSE0 + GU_UNITS
            with act.Fori(0, DG - 1) as g:
                splits(m + 6, m + 14, g)
                silu(m + 8 + BODY * g, 0, T)
                splits(m + 14, m + 16, g)
                turned(T * (g + 1), T)
                splits(m + 16, m + 18, g)
            m += BODY * (DG - 1)
            splits(m + 6, m + 10)
            silu(m + 4, 0, T, BANK // 2)
            turned(T * DG, T, 2)
            splits(MIX1, MIX1 + 6)
            act.wait_ge(part_added, 2 + DENSE_PARTS)
            squares([(t, 0, facc[:, t, :]) for t in range(T)], D)
            root(1, D)

            mixer(1, MIX1)

            act.wait_ge(top_ready, 1)
            A(e2[:, :], e2[:, :], ACT.Exp).then_inc(e2_ready, 1)
            act.wait_ge(n_exp_ready, 1)
            n = act.value_load(n_exp[0:1, 0:1], min_val=NE, max_val=2 * NE)
            with act.Fori(0, n) as e:
                done = EG * e
                for b in range(2):
                    act.wait_ge(gathered, 3 * e + b + 1)
                    A(xe_hi[:, 4 * b:4 * b + 4, :], ps[:, (7, 2)[b], :].rearrange("p (k j) -> p k j", k=4),
                      ACT.Copy).then_inc(xe_hi_ready, 1)
                with act.If(e > 0):
                    splits(MOE0, MOE0 + 6, done)
                splits(MOE0 + 6, MOE0 + 12, done)
                silu(MOE0 + 8 + BODY * done, 0, 1)
                splits(MOE0 + 12, MOE0 + 14, done)
                turned(DENSE_TILES + done, 1)
                m = MOE0 + GU_UNITS
                with act.Fori(0, EG - 2) as g:
                    splits(m + 6, m + 14, done + g)
                    silu(m + 8 + BODY * (done + g), 0, 1)
                    splits(m + 14, m + 18, done + g)
                    turned(DENSE_TILES + done + g + 1, 1)
                last = done + EG - 2
                splits(m + 6, m + 14, last)
                silu(m + 8 + BODY * last, 0, 1)
                splits(m + 14, m + 16, last)
                turned(DENSE_TILES + last + 1, 1)
                act.wait_ge(unit_used, MOE0 + EXPERT_UNITS + BODY * done)
                A(y[:, 0:BANK], ps[:, 4, :], ACT.Copy).then_inc(y_act, 1)
            act.wait_ge(part_added, ADDED0 + 4 * n)
            squares([(t, 0, facc[:, t, :]) for t in range(T)], D)
            root(1, D)

        @block.vector
        def _(dve):
            steps = [0]
            V = nc.vector

            def link(ins):
                steps[0] += 1
                ins.then_inc(dve_step, 1)
                dve.wait_ge(dve_step, steps[0])

            def split(m, loops=0):
                dve.wait_ge(hi_ready, m + 1 + BODY * loops)
                V.tensor_tensor(w_lo[:, m % NSPL, :], raw[:, m % NRAW, :], w_hi[:, m % NSPL, :].bitcast(F32),
                                ALU.subtract).then_inc(lo_ready, 1)

            def splits(a, b, loops=0):
                for m in range(a, b):
                    split(m, loops)

            stds = [0]

            def inverse(n_parts=1):
                stds[0] += 1
                dve.wait_ge(std_ready, stds[0])
                link(V.reciprocal(rstd[:, :, 0:n_parts], std[:, :, 0:n_parts]))

            def pre_norm(k):
                dve.wait_ge(pre_loaded, 16 * (k + 1))
                inverse()
                for t in range(T):
                    V.scalar_tensor_tensor(out=tok[:, t, :], in0=h[:, t, :], scalar=rstd[:, t, 0:1],
                                           in1=g_pre[:, :], op0=ALU.mult, op1=ALU.mult).then_inc(tok_ready, 1)

            def post_norm(k, srcs):
                dve.wait_ge(post_loaded, 16 * (k + 1))
                inverse()
                for t, src in enumerate(srcs):
                    link(V.scalar_tensor_tensor(out=tok[:, t, :], in0=src, scalar=rstd[:, t, 0:1],
                                                in1=g_post[:, :], op0=ALU.mult, op1=ALU.mult))
                    V.tensor_tensor(h[:, t, :], h[:, t, :], tok[:, t, :], ALU.add).then_inc(h_updated, 1)

            def act_low(s):
                for b in range(4):
                    dve.wait_ge(act_hi_ready, 4 * s + b + 1)
                    c = slice(2 * b, 2 * b + 2)
                    V.tensor_tensor(act_lo[:, c, :], ps[:, b, :].rearrange("p (k t) -> p k t", k=2),
                                    act_hi[:, c, :].bitcast(F32), ALU.subtract).then_inc(act_lo_ready, 1)

            def rope(layer):
                dve.wait_ge(qkv_copied, 4 * (layer + 1))
                H = NQ + NKV
                a, b = qk[:, :, :, 0:HALF], qk[:, :, :, HALF:2 * HALF]

                def bc(f):
                    return f[:, :, :].unsqueeze(2).to_broadcast([P, T, H, HALF])
                for t in range(T):
                    a, b = qk[:, t, :, 0:HALF], qk[:, t, :, HALF:2 * HALF]
                    c = cos[:, t, :].unsqueeze(1).to_broadcast([P, H, HALF])
                    s = sin[:, t, :].unsqueeze(1).to_broadcast([P, H, HALF])
                    V.tensor_tensor(rot[:, 0, t], a, c, ALU.mult)
                    V.tensor_tensor(rot[:, 1, t], b, s, ALU.mult)
                    V.tensor_tensor(rot[:, 2, t], b, c, ALU.mult)
                    link(V.tensor_tensor(rot[:, 3, t], a, s, ALU.mult))
                    V.tensor_tensor(a, rot[:, 0, t], rot[:, 1, t], ALU.subtract)
                    V.tensor_tensor(b, rot[:, 2, t], rot[:, 3, t], ALU.add).then_inc(qk_roped, 1)

            def mixer(layer, m):
                for b in range(2):
                    dve.wait_ge(ws_turned, 3 * layer + b + 1)
                    V.tensor_copy(ws_t[:, 4 * b:4 * b + 4, :],
                                  ps[:, 4 + b, :].rearrange("p (g t) -> p g t", g=4)).then_inc(ws_copied, 1)
                dve.wait_ge(ws_turned, 3 * layer + 3)
                V.tensor_copy(sb_t[:, :], ps[:, 6, 0:NG]).then_inc(ws_copied, 1)
                pre_norm(2 * layer)
                act_low(3 * layer)
                splits(m + 6, m + 12)
                rope(layer)
                splits(m + 12, m + 18)
                dve.wait_ge(qk_turned, 3 * layer + 2)
                V.tensor_copy(qk_t[:, 2:4, :], ps[:, 5, :].rearrange("p (k t) -> p k t", k=2)).then_inc(qk_t_dve, 1)
                splits(m + 18, m + 20)
                for t in range(T):
                    keys = (t + 1) * P
                    per = BANK // keys
                    own = mask[:, (T - 1 - t) * P:].unsqueeze(1).to_broadcast([P, per, keys])
                    for b in range(NQ // per):
                        dve.wait_ge(scores_done, 6 * layer + 2 * t + b + 1)
                        bank = (4 if t == 0 else 0) + b
                        ins = V.tensor_tensor(sc[t][:, per * b:per * (b + 1), :],
                                              ps[:, bank, :].rearrange("p (h k) -> p h k", h=per), own, ALU.add)
                    link(ins)
                    link(V.tensor_reduce(mx[:, t, :], sc[t], AX.X, ALU.max))
                    link(V.tensor_tensor(mx[:, t, :], mx[:, t, :], sinks[:, layer, :], ALU.max))
                    link(V.tensor_tensor(sink_d[:, t, :], sinks[:, layer, :], mx[:, t, :], ALU.subtract))
                    V.tensor_scalar(nmx[:, t, :], mx[:, t, :], -1.0, None, ALU.mult).then_inc(max_ready, 1)
                dve.wait_ge(gelu_done, 4 * (layer + 1))
                v3 = vg[:, :, :].rearrange("p t (g d) -> p (t g) d", g=NG)
                for t in range(T):
                    vt = vg[:, t, :].rearrange("p (g d) -> p g d", g=NG)
                    ins = V.tensor_reduce(ln_mu[:, t * NG:(t + 1) * NG], vt, AX.X, ALU.add)
                link(ins)
                link(V.tensor_scalar(ln_mu[:, :], ln_mu[:, :], 1.0 / GD, None, ALU.mult))
                link(V.tensor_tensor(v3, v3, ln_mu[:, :].unsqueeze(2).to_broadcast([P, T * NG, GD]), ALU.subtract))
                link(V.tensor_tensor(ln_sq, vg[:, :, :], vg[:, :, :], ALU.mult))
                for t in range(T):
                    ins = V.tensor_reduce(ln_var[:, t * NG:(t + 1) * NG],
                                          ln_sq[:, t, :].rearrange("p (g d) -> p g d", g=NG), AX.X, ALU.add)
                ins.then_inc(var_ready, 1)
                dve.wait_ge(ln_std_ready, layer + 1)
                link(V.reciprocal(ln_std[:, :], ln_std[:, :]))
                link(V.tensor_tensor(v3, v3, ln_std[:, :].unsqueeze(2).to_broadcast([P, T * NG, GD]), ALU.mult))
                dve.wait_ge(ln_loaded, 32 * (layer + 1))
                link(V.tensor_tensor(vg[:, :, :], vg[:, :, :], g_ln[:, 0:1, :].to_broadcast([P, T, SW]), ALU.mult))
                V.tensor_tensor(vg[:, :, :], vg[:, :, :], g_ln[:, 1:2, :].to_broadcast([P, T, SW]),
                                ALU.add).then_inc(vn_ready, 1)
                dve.wait_ge(sink_ready, layer + 1)
                link(V.tensor_tensor(rsum[:, :, :], rsum[:, :, :], sink_e[:, :, :], ALU.add))
                link(V.reciprocal(rinv[:, :, :], rsum[:, :, :]))
                for t in range(T):
                    dve.wait_ge(pv_done, T * layer + t + 1)
                    V.tensor_tensor(tok[:, t, 0:AW].rearrange("p (h d) -> p h d", h=NQ),
                                    ps[:, 4 + t, :].rearrange("p (h d) -> p h d", h=NQ),
                                    rinv[:, t, :].unsqueeze(2).to_broadcast([P, NQ, HD]), ALU.mult
                                    ).then_inc(attn_ready, 1)
                for b in range(2):
                    dve.wait_ge(sgu_done, 2 * layer + b + 1)
                    for i in range(4):
                        g = 4 * b + i
                        ins = V.scalar_tensor_tensor(
                            out=tok[:, :, AW + g * GD:AW + (g + 1) * GD],
                            in0=ps[:, 6 + b, i * P:(i + 1) * P].rearrange("p (t d) -> p t d", t=T),
                            scalar=sb_t[:, g:g + 1], in1=ug[:, :, g * GD:(g + 1) * GD], op0=ALU.add, op1=ALU.mult)
                    ins.then_inc(sgu_ready, 1)
                dve.wait_ge(out_loaded, 32 * (layer + 1))
                inverse(2)
                for t in range(T):
                    link(V.scalar_tensor_tensor(out=tok[:, t, 0:AW], in0=tok[:, t, 0:AW], scalar=rstd[:, t, 0:1],
                                                in1=g_out[:, 0:AW], op0=ALU.mult, op1=ALU.mult))
                    V.scalar_tensor_tensor(out=tok[:, t, AW:], in0=tok[:, t, AW:], scalar=rstd[:, t, 1:2],
                                           in1=g_out[:, AW:], op0=ALU.mult, op1=ALU.mult).then_inc(tok_ready, 1)
                act_low(3 * layer + 1)
                splits(m + 20, m + 22)
                post_norm(2 * layer, [ps[:, 4 + 2 * t:6 + 2 * t, :].rearrange("p b c -> p (b c)") for t in range(T)])
                splits(m + 22, m + 28)
                pre_norm(2 * layer + 1)
                act_low(3 * layer + 2)

            def hidden(n, tiles, width=BANK):
                for t in range(tiles):
                    dve.wait_ge(sil_ready, n + t + 1)
                    V.tensor_tensor(hid[:, t, 0:width], sil[:, t, 0:width], ps[:, 2 * t + 1, 0:width],
                                    ALU.mult).then_inc(hid_ready, 1)

            def turned(n, tiles, chunks=4):
                for t in range(tiles):
                    dve.wait_ge(ht_hi_ready, n + t + 1)
                    V.tensor_tensor(ht_lo[:, 0:chunks, t, :],
                                    ps[:, 6 + t, 0:chunks * P].rearrange("p (c j) -> p c j", c=chunks),
                                    ht_hi[:, 0:chunks, t, :].bitcast(F32), ALU.subtract).then_inc(ht_lo_ready, 1)

            def add_parts(n, banks, units=None):
                for t in range(T):
                    for half in range(2):
                        if units is not None and (t, half) == (T - 1, 1):
                            dve.wait_ge(unit_used, units)
                        else:
                            dve.wait_ge(part_done, n + 2 * t + half + 1)
                        cols = slice(half * BANK, (half + 1) * BANK)
                        V.tensor_tensor(facc[:, t, cols], facc[:, t, cols], ps[:, banks[half], :],
                                        ALU.add).then_inc(part_added, 1)

            def clear_sums():
                for t in range(T):
                    V.memset(facc[:, t, :], 0.0).then_inc(part_added, 1)

            dve.wait_ge(consts_ready, 1)
            dve.wait_ge(small_loaded, 48)
            V.tensor_copy(iota[:, :], iota_i[:, :])
            link(V.tensor_copy(pos[:, :], pos_i[:, :]))
            for t in range(T):
                ins = V.tensor_scalar(ang[:, t, :], inv_freq[:, :], pos[:, t:t + 1], None, ALU.mult)
            link(ins)
            big = 1.5 * 2 ** 23
            link(V.tensor_scalar(turns[:, :, :], ang[:, :, :], 1 / (2 * np.pi), big, ALU.mult, ALU.add))
            link(V.tensor_scalar(turns[:, :, :], turns[:, :, :], -big, None, ALU.add))
            c1 = 6.28125
            c2 = float(np.float32(np.round((2 * np.pi - c1) * 2 ** 20) / 2 ** 20))
            for c in (c1, c2, 2 * np.pi - c1 - c2):
                link(V.scalar_tensor_tensor(out=ang[:, :, :], in0=turns[:, :, :], scalar=-float(c), in1=ang[:, :, :],
                                            op0=ALU.mult, op1=ALU.add))
            link(V.tensor_scalar(ang[:, :, :], ang[:, :, :], 3.1415925, -3.1415925, ALU.min, ALU.max))
            V.scalar_tensor_tensor(out=turns[:, :, :], in0=ang[:, :, :], scalar=-1.0, in1=ang[:, :, :],
                                   op0=ALU.mult, op1=ALU.max).then_inc(angle_ready, 1)

            splits(0, 6)
            dve.wait_ge(sincos_ready, 3)
            link(V.tensor_tensor(wr_lo[:, :, :], wr[:, :, :], wr_hi[:, :, :].bitcast(F32), ALU.subtract))
            mixer(0, 0)

            clear_sums()
            m = DENSE0
            splits(m + 6, m + 12)
            hidden(0, T)
            splits(m + 12, m + 14)
            turned(0, T)
            m = DENSE0 + GU_UNITS
            with dve.Fori(0, DG - 1) as g:
                splits(m + 6, m + 14, g)
                hidden(T * (g + 1), T)
                add_parts(3 * g, (4, 5), m + BODY * (g + 1))
                splits(m + 14, m + 16, g)
                turned(T * (g + 1), T)
                splits(m + 16, m + 18, g)
            m += BODY * (DG - 1)
            splits(m + 6, m + 10)
            hidden(T * DG, T, BANK // 2)
            add_parts(3 * (DG - 1), (4, 5), m + BODY - 4)
            turned(T * DG, T, 2)
            add_parts(3 * DG, (4, 5), MIX1)
            splits(MIX1, MIX1 + 6)
            post_norm(1, [facc[:, t, :] for t in range(T)])

            mixer(1, MIX1)

            clear_sums()
            dve.wait_ge(logits_done, 1)
            link(V.tensor_copy(lg[:, :, :], ps[:, 6, 0:T * NE].rearrange("p (t e) -> p t e", t=T)))
            experts_iota = iota[:, 0:NE].unsqueeze(1).to_broadcast([P, T, NE])

            def wide(a):
                return a.unsqueeze(2).to_broadcast([P, T, NE])

            for r in range(2):
                link(V.tensor_reduce(top[:, r, :], lg[:, :, :], AX.X, ALU.max))
                link(V.tensor_tensor(cand[:, :, :], lg[:, :, :], wide(top[:, r, :]), ALU.is_lt))
                link(V.scalar_tensor_tensor(out=cand[:, :, :], in0=cand[:, :, :], scalar=100.0, in1=experts_iota,
                                            op0=ALU.mult, op1=ALU.add))
                link(V.tensor_reduce(at[:, :], cand[:, :, :], AX.X, ALU.min))
                link(V.tensor_tensor(pick[:, r], experts_iota, wide(at[:, :]), ALU.is_equal))
                if r == 0:
                    link(V.scalar_tensor_tensor(out=lg[:, :, :], in0=pick[:, 0], scalar=-3e38, in1=lg[:, :, :],
                                                op0=ALU.mult, op1=ALU.add))
            link(V.tensor_tensor(chosen[:, :, :], pick[:, 0], pick[:, 1], ALU.add))
            V.tensor_tensor(e2[:, :], top[:, 1, :], top[:, 0, :], ALU.subtract).then_inc(top_ready, 1)
            dve.wait_ge(e2_ready, 1)
            link(V.tensor_scalar(g12[:, 0, :], e2[:, :], 1.0, None, ALU.add))
            link(V.reciprocal(g12[:, 0, :], g12[:, 0, :]))
            link(V.tensor_tensor(g12[:, 1, :], g12[:, 0, :], e2[:, :], ALU.mult))
            for r in range(2):
                link(V.tensor_tensor(pick[:, r], pick[:, r], wide(g12[:, r, :]), ALU.mult))
            for r in range(2):
                V.tensor_tensor(gate[:, :, r * NE:(r + 1) * NE], pick[:, 0], pick[:, 1], ALU.add)
            dve.wait_ge(counts_done, 1)
            link(V.tensor_tensor(rank[:, :, 0:NE], ps[:, 7, 0:T * NE].rearrange("p (t e) -> p t e", t=T),
                                 chosen[:, :, :], ALU.mult))
            link(V.tensor_scalar(rank[:, :, 0:NE], rank[:, :, 0:NE], -1.0, None, ALU.add))
            link(V.tensor_scalar(rank[:, :, NE:], rank[:, :, 0:NE], -float(P), None, ALU.add))
            link(V.tensor_reduce(cnt[:, :], ps[:, 7, T * NE:(T + 1) * NE], AX.X, ALU.max))
            link(V.tensor_scalar(n_exp_f[:, :], cnt[:, :], P + 0.5, float(NE), ALU.is_gt, ALU.mult))
            link(V.tensor_scalar(n_exp_f[:, :], n_exp_f[:, :], float(NE), None, ALU.add))
            V.tensor_copy(n_exp[:, :], n_exp_f[:, :]).then_inc(n_exp_ready, 1)
            dve.wait_ge(n_exp_ready, 1)
            n = dve.value_load(n_exp[0:1, 0:1], min_val=NE, max_val=2 * NE)
            with dve.Fori(0, n) as e:
                done = EG * e
                for t in range(T):
                    r_e, g_e = rank[:, t, bass.ds(e, 1)], gate[:, t, bass.ds(e, 1)]
                    V.tensor_scalar(sel[:, t, :], iota[:, :], r_e, None, ALU.is_equal).then_inc(sel_ready, 1)
                    V.tensor_scalar(sel_g[:, t, :], iota[:, :], r_e, g_e, ALU.is_equal, ALU.mult).then_inc(sel_ready, 1)
                for b in range(2):
                    dve.wait_ge(xe_hi_ready, 2 * e + b + 1)
                    c = slice(4 * b, 4 * b + 4)
                    V.tensor_tensor(xe_lo[:, c, :], ps[:, (7, 2)[b], :].rearrange("p (k j) -> p k j", k=4),
                                    xe_hi[:, c, :].bitcast(F32), ALU.subtract).then_inc(xe_lo_ready, 1)
                with dve.If(e > 0):
                    splits(MOE0, MOE0 + 6, done)
                dve.wait_ge(gathered, 3 * e + 3)
                V.tensor_copy(sel_t, ps[:, 3, 0:S].rearrange("p (t j) -> p t j", t=T)).then_inc(sel_t_ready, 1)
                splits(MOE0 + 6, MOE0 + 12, done)
                hidden(DENSE_TILES + done, 1)
                splits(MOE0 + 12, MOE0 + 14, done)
                turned(DENSE_TILES + done, 1)
                m = MOE0 + GU_UNITS
                with dve.Fori(0, EG - 2) as g:
                    splits(m + 6, m + 14, done + g)
                    hidden(DENSE_TILES + done + g + 1, 1)
                    splits(m + 14, m + 18, done + g)
                    turned(DENSE_TILES + done + g + 1, 1)
                last = done + EG - 2
                splits(m + 6, m + 14, last)
                hidden(DENSE_TILES + last + 1, 1)
                splits(m + 14, m + 16, last)
                turned(DENSE_TILES + last + 1, 1)
                dve.wait_ge(unit_used, MOE0 + EXPERT_UNITS + BODY * done)
                V.tensor_copy(y[:, BANK:], ps[:, 5, :]).then_inc(y_dve, 1)
                add_parts(3 * (DG + 1) + 4 * e, (2, 3))
            post_norm(3, [facc[:, t, :] for t in range(T)])

        @block.tensor
        def _(pe):
            mm = nc.tensor.matmul

            def product(o, a_hi, a_lo, b_hi, b_lo, first, last):
                mm(o, a_hi, b_hi, start=first, stop=False)
                mm(o, a_lo, b_hi, start=False, stop=False)
                return mm(o, a_hi, b_lo, start=False, stop=last)

            def unit(m, k, loops=0):
                pe.wait_ge(lo_ready, m + 1 + BODY * loops)
                return unit_view(w_hi, m % NSPL, k), unit_view(w_lo, m % NSPL, k)

            def turn(s):
                for b in range(4):
                    for c in range(2):
                        for t in range(T):
                            if b == c == 0:
                                pe.wait_ge(tok_ready, T * s + t + 1)
                            k = 2 * b + c
                            ins = nc.tensor.transpose(ps[:, b, c * S + t * P:c * S + (t + 1) * P],
                                                      tok[:, t, k * P:(k + 1) * P], ident[:, :])
                    ins.then_inc(tok_turned, 1)

            def columns(m, n, k, banks, width, first_row=0, rows=KC):
                done = 0
                for u in range(n):
                    hi, lo = unit(m + u, k)
                    for t in range(T):
                        tt = slice(t * P, (t + 1) * P)
                        for i in range(k):
                            r = u * k + i
                            ins = product(ps[:, banks[t], 0:width], act_hi[:, r, tt], act_lo[:, r, tt],
                                          hi[:, i, :], lo[:, i, :], r == 0, r == KC - 1)
                    ins.then_inc(unit_used, 1)

            def mixer(layer, m):
                pe.wait_ge(ws_masked, layer + 1)
                pe.wait_ge(sb_loaded, 16 * (layer + 1))
                if layer == 0:
                    pe.wait_ge(consts_ready, 1)
                else:
                    pe.wait_ge(part_added, 2 + DENSE_PARTS)
                for b in range(2):
                    for i in range(4):
                        ins = nc.tensor.transpose(ps[:, 4 + b, i * P:(i + 1) * P], ws_raw[:, 4 * b + i, :], ident[:, :])
                    ins.then_inc(ws_turned, 1)
                nc.tensor.transpose(ps[:, 6, 0:NG], sb_rows[:, :], ident[0:NG, 0:NG]).then_inc(ws_turned, 1)
                turn(3 * layer)
                pe.wait_ge(act_lo_ready, 4 * (3 * layer + 1))
                pe.wait_ge(ws_copied, 3 * (layer + 1))
                columns(m, 4, 2, (4, 5), BANK)
                columns(m + 4, 2, 4, (6, 7), 2 * KVW)
                columns(m + 6, 4, 2, (0, 1), BANK)
                columns(m + 10, 4, 2, (2, 3), BANK)
                pe.wait_ge(qk_roped, T * (layer + 1))
                for c in range((NQ + NKV) // 2):
                    for t in range(T):
                        ins = nc.tensor.transpose(ps[:, 4 + c // 2, (c % 2) * S + t * P:(c % 2) * S + (t + 1) * P],
                                                  qk[:, t, 2 * c:2 * c + 2, :].rearrange("p j d -> p (j d)"),
                                                  ident[:, :])
                    if c in (1, 3, 4):
                        ins.then_inc(qk_turned, 1)
                pe.wait_ge(qk_t_act, 2 * (layer + 1))
                pe.wait_ge(qk_t_dve, layer + 1)
                for t in range(T):
                    if t == 1:
                        pe.wait_ge(gelu_done, 4 * (layer + 1))
                    keys = (t + 1) * P
                    per = BANK // keys
                    for hh in range(NQ):
                        j, i = hh // QPK, hh % QPK
                        rows = slice(HD * j, HD * (j + 1))
                        bank = (4 if t == 0 else 0) + hh // per
                        ins = mm(ps[:, bank, (hh % per) * keys:(hh % per + 1) * keys],
                                 qk_t[rows, i, t * P:(t + 1) * P], qk_t[rows, QPK, 0:keys], start=True, stop=True)
                        if hh % per == per - 1:
                            ins.then_inc(scores_done, 1)
                for b, bank in enumerate((4, 5, 0, 1, 2, 3)):
                    for i in range(4):
                        n = 4 * b + i
                        if n < NQ:
                            pe.wait_ge(probs_ready, T * NQ * layer + n + 1)
                            src = sc[0][:, n, :]
                        else:
                            hh, blk = (n - NQ) // 2, n % 2
                            pe.wait_ge(probs_ready, T * NQ * layer + NQ + hh + 1)
                            src = sc[1][:, hh, blk * P:(blk + 1) * P]
                        ins = nc.tensor.transpose(ps[:, bank, i * P:(i + 1) * P], src, ident[:, :])
                    ins.then_inc(probs_turned, 1)
                for t in range(T):
                    pe.wait_ge(pt_ready, 6 * layer + (2 if t == 0 else 6))
                    for hh in range(NQ):
                        j = hh // QPK
                        for blk in range(t + 1):
                            n = hh if t == 0 else NQ + 2 * hh + blk
                            ins = mm(ps[:, 4 + t, hh * HD:(hh + 1) * HD], pt[:, n, :],
                                     vv[:, blk, j * HD:(j + 1) * HD], start=(blk == 0), stop=(blk == t))
                    ins.then_inc(pv_done, 1)
                pe.wait_ge(vn_ready, layer + 1)
                for g in range(NG):
                    ins = mm(ps[:, 6 + g // 4, (g % 4) * P:(g % 4 + 1) * P].rearrange("p (t d) -> p t d", t=T),
                             ws_t[:, g, :], vg[:, :, g * GD:(g + 1) * GD], start=True, stop=True)
                    if g % 4 == 3:
                        ins.then_inc(sgu_done, 1)
                turn(3 * layer + 1)
                for q in range(4):
                    pe.wait_ge(act_lo_ready, 4 * (3 * layer + 1) + q + 1)
                    for half in range(2):
                        hi, lo = unit(m + Z_UNITS + 2 * q + half, 2)
                        for t in range(T):
                            tt = slice(t * P, (t + 1) * P)
                            for i in range(2):
                                r = 2 * q + i
                                ins = product(ps[:, 4 + 2 * t + half, :], act_hi[:, r, tt], act_lo[:, r, tt],
                                              hi[:, i, :], lo[:, i, :], r == 0, r == KC - 1)
                        ins.then_inc(unit_used, 1)
                turn(3 * layer + 2)
                pe.wait_ge(act_lo_ready, 4 * (3 * layer + 3))

            def gate_up(m, a_hi, a_lo, tiles, loops=0, width=BANK):
                k = UW // width
                per = KC // k
                for w in range(2):
                    for u in range(per):
                        hi, lo = unit(m + w * per + u, k, loops)
                        for t in range(tiles):
                            tt = slice(t * P, (t + 1) * P)
                            for i in range(k):
                                r = u * k + i
                                ins = product(ps[:, 2 * t + w, 0:width], a_hi[:, r, tt], a_lo[:, r, tt],
                                              hi[:, i, :], lo[:, i, :], r == 0, r == KC - 1)
                        ins.then_inc(unit_used, 1)

            def turn_hidden(n, tiles, chunks=4):
                for t in range(tiles):
                    pe.wait_ge(hid_ready, n + t + 1)
                    for c in range(chunks):
                        ins = nc.tensor.transpose(ps[:, 6 + t, c * P:(c + 1) * P], hid[:, t, c * P:(c + 1) * P],
                                                  ident[:, :])
                    ins.then_inc(hid_turned, 1)

            def dense_down(m, n, parts, loops=0, chunks=4):
                pe.wait_ge(ht_lo_ready, n)
                hl = [unit(m + c, 1, loops) for c in range(chunks)]
                for t in range(T):
                    for half in range(2):
                        pe.wait_ge(part_added, parts + 2 * t + half + 1)
                        for c in range(chunks):
                            cols = slice(half * BANK, (half + 1) * BANK)
                            ins = product(ps[:, 4 + half, :], ht_hi[:, c, t, :], ht_lo[:, c, t, :],
                                          hl[c][0][:, 0, cols], hl[c][1][:, 0, cols], c == 0, c == chunks - 1)
                            if (t, half) == (T - 1, 1):
                                ins.then_inc(unit_used, 1)
                        if (t, half) != (T - 1, 1):
                            ins.then_inc(part_done, 1)

            def expert_down(m, n, first, last, loops=0):
                pe.wait_ge(ht_lo_ready, n)
                for c in range(4):
                    hi, lo = unit(m + c, 1, loops)
                    for half in range(2):
                        cols = slice(half * BANK, (half + 1) * BANK)
                        ins = product(ps[:, 4 + half, :], ht_hi[:, c, 0, :], ht_lo[:, c, 0, :],
                                      hi[:, 0, cols], lo[:, 0, cols], first and c == 0, last and c == 3)
                    ins.then_inc(unit_used, 1)

            mixer(0, 0)
            gate_up(DENSE0, act_hi, act_lo, T)
            turn_hidden(0, T)
            m = DENSE0 + GU_UNITS
            with pe.Fori(0, DG - 1) as g:
                gate_up(m, act_hi, act_lo, T, g)
                dense_down(m + GU_UNITS, T * (g + 1), 4 * g, g)
                turn_hidden(T * (g + 1), T)
            m += BODY * (DG - 1)
            gate_up(m, act_hi, act_lo, T, width=BANK // 2)
            dense_down(m + 4, T * DG, 4 * (DG - 1))
            turn_hidden(T * DG, T, 2)
            dense_down(m + 8, T * (DG + 1), 4 * DG, chunks=2)

            mixer(1, MIX1)

            for t in range(T):
                tt = slice(t * P, (t + 1) * P)
                for k in range(KC):
                    o = ps[:, 6, t * NE:(t + 1) * NE]
                    product(o, act_hi[:, k, tt], act_lo[:, k, tt], wr_hi[:, k, :], wr_lo[:, k, :], k == 0, False)
                    ins = mm(o, act_lo[:, k, tt], wr_lo[:, k, :], start=False, stop=(k == KC - 1))
            ins.then_inc(logits_done, 1)
            pe.wait_ge(top_ready, 1)
            c0, c1 = chosen[:, 0, :], chosen[:, 1, :]
            mm(ps[:, 7, 0:NE], upper[:, :], c0, start=True, stop=True)
            mm(ps[:, 7, NE:2 * NE], ones[:, :], c0, start=True, stop=False)
            mm(ps[:, 7, NE:2 * NE], upper[:, :], c1, start=False, stop=True)
            mm(ps[:, 7, 2 * NE:3 * NE], ones[:, :], c0, start=True, stop=False)
            mm(ps[:, 7, 2 * NE:3 * NE], ones[:, :], c1, start=False, stop=True).then_inc(counts_done, 1)
            pe.wait_ge(n_exp_ready, 1)
            n = pe.value_load(n_exp[0:1, 0:1], min_val=NE, max_val=2 * NE)
            with pe.Fori(0, n) as e:
                done = EG * e
                pe.wait_ge(sel_ready, 4 * (e + 1))
                for b in range(2):
                    for i in range(4):
                        k = 4 * b + i
                        for t in range(T):
                            ins = mm(ps[:, (7, 2)[b], i * P:(i + 1) * P], tok[:, t, k * P:(k + 1) * P], sel[:, t, :],
                                     start=(t == 0), stop=(t == T - 1))
                    ins.then_inc(gathered, 1)
                for t in range(T):
                    ins = nc.tensor.transpose(ps[:, 3, t * P:(t + 1) * P], sel_g[:, t, :], ident[:, :])
                ins.then_inc(gathered, 1)
                pe.wait_ge(xe_lo_ready, 2 * (e + 1))
                gate_up(MOE0, xe_hi, xe_lo, 1, done)
                turn_hidden(DENSE_TILES + done, 1)
                m = MOE0 + GU_UNITS
                gate_up(m, xe_hi, xe_lo, 1, done)
                expert_down(m + GU_UNITS, DENSE_TILES + done + 1, True, False, done)
                turn_hidden(DENSE_TILES + done + 1, 1)
                with pe.Fori(1, EG - 1) as g:
                    gate_up(m, xe_hi, xe_lo, 1, done + g)
                    expert_down(m + GU_UNITS, DENSE_TILES + done + g + 1, False, False, done + g)
                    turn_hidden(DENSE_TILES + done + g + 1, 1)
                expert_down(m, DENSE_TILES + done + EG, False, True, done + EG - 1)
                pe.wait_ge(sel_t_ready, e + 1)
                pe.wait_ge(y_act, e + 1)
                pe.wait_ge(y_dve, e + 1)
                for t in range(T):
                    for half in range(2):
                        pe.wait_ge(part_added, ADDED0 - 1 + 4 * e + 2 * t + half)
                        mm(ps[:, 2 + half, :], sel_t[:, t, :], y[:, half * BANK:(half + 1) * BANK], start=True,
                           stop=True).then_inc(part_done, 1)


_INS = ["x", "positions", "pre_mix_norm", "w_in", "attn_sinks", "sgu_ln_g", "sgu_ln_b", "sgu_w", "sgu_b",
        "attn_out_norm", "sgu_out_norm", "w_out", "post_mix_norm", "pre_ffn_norm", "post_ffn_norm", "ffn_w_gate",
        "ffn_w_up", "ffn_w_down", "moe_router", "moe_w_gate", "moe_w_up", "moe_w_down"]


def kernel(**inputs):
    import numpy as _np
    import concourse.bacc as _bacc
    from concourse import mybir as _mybir
    from concourse.bass_utils import run_bass_kernel_spmd as _run

    nc = _bacc.Bacc("TRN2", target_bir_lowering=False, num_devices=1)
    arrays, args = {}, []
    for name in _INS:
        a = _np.ascontiguousarray(inputs[name])
        arrays[f"in_{name}"] = a
        args.append(nc.dram_tensor(f"in_{name}", a.shape, _mybir.dt.from_np(a.dtype), kind="ExternalInput").ap())
    out = nc.dram_tensor("out_0", (1, S, D), _mybir.dt.float32, kind="ExternalOutput").ap()
    trunk(nc, *args, out)
    r = _run(nc, [arrays], core_ids=[0])
    return r.results[0]["out_0"]
```

```python
from contextlib import ExitStack

import numpy as np

import concourse.bass as bass
from concourse import mybir

F32 = mybir.dt.float32
F32R = mybir.dt.float32r
I32 = mybir.dt.int32
ALU = mybir.AluOpType
ACT = mybir.ActivationFunctionType
AX = mybir.AxisListType

P = 128
D = 1024
S = 256
T = S // P
KC = D // P
DEPTH = 2
HD = 64
NQ, NKV = 8, 2
QPK = NQ // NKV
AW = NQ * HD
KVW = NKV * HD
NG = 8
GD = 64
SW = NG * GD
HALF = 8
THETA, ROPE_DIM = 500000.0, 16
FD = 2816
FE = 3584
NE = 8
EPS = 1e-6
NEG = -1e30
BANK = 512

UW = 1024
NRAW = 12
NSPL = 6
Z_UNITS, O_UNITS = 14, 8
MIX_UNITS = Z_UNITS + O_UNITS
GU_UNITS, DN_UNITS = 8, 4
BODY = GU_UNITS + DN_UNITS
DG = FD // BANK
EG = FE // BANK
DENSE0 = MIX_UNITS
DENSE_UNITS = DG * BODY + BODY // 2
MIX1 = DENSE0 + DENSE_UNITS
MOE0 = MIX1 + MIX_UNITS
EXPERT_UNITS = EG * BODY
assert NRAW == BODY and BODY % NSPL == 0 and FD % BANK == BANK // 2 and FE % BANK == 0


def trunk(nc, x, positions, pre_mix_norm, w_in, attn_sinks, sgu_ln_g, sgu_ln_b, sgu_w, sgu_b, attn_out_norm,
          sgu_out_norm, w_out, post_mix_norm, pre_ffn_norm, post_ffn_norm, ffn_w_gate, ffn_w_up, ffn_w_down,
          moe_router, moe_w_gate, moe_w_up, moe_w_down, out):
    ctx = ExitStack()
    with ctx:
        def sb(name, shape, dt=F32):
            return ctx.enter_context(nc.sbuf_tensor(name, shape, dt))

        def sem(name):
            return ctx.enter_context(nc.semaphore(name))

        raw = sb("raw", [P, NRAW, UW])
        w_hi = sb("w_hi", [P, NSPL, UW], F32R)
        w_lo = sb("w_lo", [P, NSPL, UW], F32R)
        h = sb("h", [P, T, D])
        tok = sb("tok", [P, T, D])
        act_hi = sb("act_hi", [P, KC, S], F32R)
        act_lo = sb("act_lo", [P, KC, S], F32R)
        g_pre = sb("g_pre", [P, D])
        g_out = sb("g_out", [P, D])
        g_post = sb("g_post", [P, D])
        g_ln = sb("g_ln", [P, 2, SW])
        qk = sb("qk", [P, T, NQ + NKV, HD])
        vv = sb("vv", [P, T, KVW])
        qk_t = sb("qk_t", [P, (NQ + NKV) // 2, S])
        ug = sb("ug", [P, T, SW])
        vg = sb("vg", [P, T, SW])
        ws_t = sb("ws_t", [P, NG, P])
        shared = sb("shared", [P, 6144])
        ht_hi = sb("ht_hi", [P, 4, T, P], F32R)
        ht_lo = sb("ht_lo", [P, 4, T, P], F32R)
        ident = sb("ident", [P, P])
        ones = sb("ones", [P, P])
        upper = sb("upper", [P, P])
        mask = sb("mask", [P, 2 * P])
        iota_i = sb("iota_i", [P, P], I32)
        iota = sb("iota", [P, P])
        inv_freq = sb("inv_freq", [P, HALF])
        pos_i = sb("pos_i", [P, T], I32)
        pos = sb("pos", [P, T])
        ang = sb("ang", [P, T, HALF])
        turns = sb("turns", [P, T, HALF])
        cos = sb("cos", [P, T, HALF])
        sin = sb("sin", [P, T, HALF])
        sinks = sb("sinks", [P, DEPTH, NQ])
        sb_rows = sb("sb_rows", [NG, P])
        sb_t = sb("sb_t", [P, NG])
        eps = sb("eps", [P, 1])
        half_pi = sb("half_pi", [P, 1])
        ssq = sb("ssq", [P, 4 * T])
        std = sb("std", [P, 4 * T])
        rstd = sb("rstd", [P, 4 * T])
        half_ssq = sb("half_ssq", [P, T, 3])
        q_scale = sb("q_scale", [P, T])
        ln_mu = sb("ln_mu", [P, T * NG])
        ln_var = sb("ln_var", [P, T * NG])
        ln_std = sb("ln_std", [P, T * NG])
        mx = sb("mx", [P, T, NQ])
        nmx = sb("nmx", [P, T, NQ])
        sink_d = sb("sink_d", [P, T, NQ])
        sink_e = sb("sink_e", [P, T, NQ])
        rsum = sb("rsum", [P, T, NQ])
        rinv = sb("rinv", [P, T, NQ])
        wr = sb("wr", [P, KC, NE])
        wr_hi = sb("wr_hi", [P, KC, NE], F32R)
        wr_lo = sb("wr_lo", [P, KC, NE], F32R)
        lg = sb("lg", [P, T, NE])
        pick = sb("pick", [P, 2, T, NE])
        cand = sb("cand", [P, T, NE])
        top = sb("top", [P, 2, T])
        at = sb("at", [P, T])
        e2 = sb("e2", [P, T])
        g12 = sb("g12", [P, 2, T])
        chosen = sb("chosen", [P, T, NE])
        gate = sb("gate", [P, T, 2 * NE])
        rank = sb("rank", [P, T, 2 * NE + 1])
        cnt = sb("cnt", [P, 1])
        n_exp_f = sb("n_exp_f", [P, 1])
        n_exp = sb("n_exp", [P, 1], I32)

        sc = [shared[:, 0:1024].rearrange("p (h k) -> p h k", h=NQ),
              shared[:, 1024:3072].rearrange("p (h k) -> p h k", h=NQ)]
        pt = shared[:, 3072:6144].rearrange("p (b q) -> p b q", b=24)
        rot = shared[:, 0:4 * T * (NQ + NKV) * HALF].rearrange("p (r t h j) -> p r t h j", r=4, t=T, h=NQ + NKV)
        facc = shared[:, 0:2048].rearrange("p (t d) -> p t d", t=T)
        sil = shared[:, 2048:3072].rearrange("p (t f) -> p t f", t=T)
        hid = shared[:, 3072:4096].rearrange("p (t f) -> p t f", t=T)
        y = shared[:, 4096:5120]
        sel = shared[:, 5120:5376].rearrange("p (t j) -> p t j", t=T)
        sel_g = shared[:, 5376:5632].rearrange("p (t j) -> p t j", t=T)
        sel_t = shared[:, 5632:5888].rearrange("p (t j) -> p t j", t=T)
        sq = shared[:, 5120:6144]
        sq_mix = shared[:, 0:AW]
        ws_raw = ug[:, :, :].rearrange("p t (g s) -> p (t g) s", s=P)
        ln_sq = tok[:, :, AW:AW + SW]
        xe_hi = act_hi[:, :, 0:P]
        xe_lo = act_lo[:, :, 0:P]

        PROB_BANKS = (4, 5, 6, 7, 0, 1)
        ps = ctx.enter_context(nc.psum_tensor("ps", [P, 8, BANK], F32))

        raw_arrived = [sem(f"raw_arrived{i}") for i in range(NRAW)]
        hi_ready = sem("hi_ready")
        lo_ready = sem("lo_ready")
        unit_used = sem("unit_used")
        x_loaded = sem("x_loaded")
        small_loaded = sem("small_loaded")
        pre_loaded, out_loaded, post_loaded, ln_loaded = (sem(f"{n}_gain_loaded") for n in ("pre", "out", "post", "ln"))
        ws_loaded = sem("ws_loaded")
        sb_loaded = sem("sb_loaded")
        ws_masked = sem("ws_masked")
        consts_ready = sem("consts_ready")
        pool_step = sem("pool_step")
        act_step = sem("act_step")
        dve_step = sem("dve_step")
        angle_ready = sem("angle_ready")
        sincos_ready = sem("sincos_ready")
        std_ready = sem("std_ready")
        rstd_ready = sem("rstd_ready")
        mix_done = sem("mix_done")
        half_squared = sem("half_squared")
        tokens_ready = sem("tokens_ready")
        tok_ready = sem("tok_ready")
        tok_turned = sem("tok_turned")
        act_hi_ready = sem("act_hi_ready")
        act_lo_ready = sem("act_lo_ready")
        ws_turned = sem("ws_turned")
        ws_copied = sem("ws_copied")
        qkv_copied = sem("qkv_copied")
        qk_roped = sem("qk_roped")
        qk_turned = sem("qk_turned")
        qk_t_act = sem("qk_t_act")
        qk_t_dve = sem("qk_t_dve")
        gelu_done = sem("gelu_done")
        scores_done = sem("scores_done")
        max_ready = sem("max_ready")
        probs_ready = sem("probs_ready")
        sink_ready = sem("sink_ready")
        probs_turned = sem("probs_turned")
        pt_ready = sem("pt_ready")
        pv_done = sem("pv_done")
        attn_ready = sem("attn_ready")
        var_ready = sem("var_ready")
        ln_std_ready = sem("ln_std_ready")
        vn_ready = sem("vn_ready")
        sgu_done = sem("sgu_done")
        sgu_ready = sem("sgu_ready")
        h_updated = sem("h_updated")
        sil_ready = sem("sil_ready")
        hid_ready = sem("hid_ready")
        hid_turned = sem("hid_turned")
        ht_hi_ready = sem("ht_hi_ready")
        ht_lo_ready = sem("ht_lo_ready")
        part_done = sem("part_done")
        part_added = sem("part_added")
        logits_done = sem("logits_done")
        top_ready = sem("top_ready")
        e2_ready = sem("e2_ready")
        chosen_ready = sem("chosen_ready")
        counts_done = sem("counts_done")
        n_exp_ready = sem("n_exp_ready")
        sel_ready = sem("sel_ready")
        gathered = sem("gathered")
        xe_hi_ready = sem("xe_hi_ready")
        xe_lo_ready = sem("xe_lo_ready")
        sel_t_ready = sem("sel_t_ready")
        y_act = sem("y_act")
        y_dve = sem("y_dve")
        out_stored = sem("out_stored")

        DENSE_TILES = T * (DG + 1)
        DENSE_PARTS = 2 * T * (DG + 1)
        ADDED0 = 2 + DENSE_PARTS + 2
        PRE, ATTN, SGU, POST = 0, T, 2 * T, 3 * T
        TURNS = ([(2 * t + b, slice(4 * b, 4 * b + 4), t) for t in range(T) for b in range(2)]
                 + [(t, slice(0, 4), t) for t in range(T)] + [(t, slice(4, 8), t) for t in range(T)]
                 + [(2 * t + b, slice(4 * b, 4 * b + 4), t) for t in range(T) for b in range(2)])
        PRE_MIX, ATTN_HALF, SGU_HALF, PRE_FFN = 0, 4, 6, 8
        N_TURNS = len(TURNS)

        def mixed(t):
            return [ps[:, 4 + 2 * t + half, :] for half in range(2)]

        def summed(t):
            return [facc[:, t, half * BANK:(half + 1) * BANK] for half in range(2)]

        def stacked(w):
            return w.rearrange("(k p) c -> p k c", p=P)

        def unit_view(ring, slot, k):
            return ring[:, slot, :].rearrange("p (k c) -> p k c", k=k)

        block = ctx.enter_context(nc.Block())

        @block.sync
        def _(sp):
            def load(m, src, k, loops=0):
                if m >= NRAW:
                    sp.wait_ge(lo_ready, m - NRAW + 1 + BODY * loops)
                sp.dma_start(unit_view(raw, m % NRAW, k), src).then_inc(raw_arrived[m % NRAW], 16)

            def mixer_units(layer, m):
                for c0, width in ((0, AW), (AW, 2 * KVW), (AW + 2 * KVW + SW, SW), (AW + 2 * KVW, SW)):
                    k = UW // width
                    for r in range(0, KC, k):
                        load(m, stacked(w_in[layer, r * P:(r + k) * P, c0:c0 + width]), k)
                        m += 1
                for r in range(0, KC, 2):
                    for c0 in (0, BANK):
                        load(m, stacked(w_out[layer, r * P:(r + 2) * P, c0:c0 + BANK]), 2)
                        m += 1

            def gate_up(m, w_gate, w_up, c0, loops=0):
                for w in (w_gate, w_up):
                    for r in range(0, KC, 2):
                        load(m, stacked(w[r * P:(r + 2) * P, bass.ds(c0, BANK)]), 2, loops)
                        m += 1

            def down(m, w_down, r0, loops=0, chunks=4):
                for c in range(chunks):
                    load(m, stacked(w_down[bass.ds(r0 + c * P, P), :]), 1, loops)
                    m += 1

            sp.dma_start(h[:, :, :], x[0].rearrange("(t p) d -> p t d", p=P)).then_inc(x_loaded, 16)
            mixer_units(0, 0)
            wg, wu, wd = ffn_w_gate[0], ffn_w_up[0], ffn_w_down[0]
            gate_up(DENSE0, wg, wu, 0)
            with sp.Fori(0, DG - 1) as g:
                gate_up(DENSE0 + GU_UNITS, wg, wu, (g + 1) * BANK, g)
                down(DENSE0 + BODY + DN_UNITS, wd, g * BANK, g)
            m = DENSE0 + GU_UNITS + (DG - 1) * BODY
            for w in (wg, wu):
                for r in (0, 4):
                    load(m, stacked(w[r * P:(r + 4) * P, DG * BANK:FD]), 4)
                    m += 1
            down(m, wd, (DG - 1) * BANK)
            down(m + DN_UNITS, wd, DG * BANK, chunks=2)
            mixer_units(1, MIX1)

            def experts(first_loop):
                with sp.Fori(0, NE) as e:
                    wg = moe_w_gate[0, bass.ds(e, 1)].rearrange("a d f -> (a d) f")
                    wu = moe_w_up[0, bass.ds(e, 1)].rearrange("a d f -> (a d) f")
                    wd = moe_w_down[0, bass.ds(e, 1)].rearrange("a f d -> (a f) d")
                    done = first_loop + EG * e
                    gate_up(MOE0, wg, wu, 0, done)
                    with sp.Fori(0, EG - 1) as g:
                        gate_up(MOE0 + GU_UNITS, wg, wu, (g + 1) * BANK, done + g)
                        down(MOE0 + 2 * GU_UNITS, wd, g * BANK, done + g)
                    down(MOE0 + GU_UNITS, wd, (EG - 1) * BANK, done + EG - 1)

            experts(0)
            sp.wait_ge(n_exp_ready, 1)
            n = sp.value_load(n_exp[0:1, 0:1], min_val=NE, max_val=2 * NE)
            with sp.If(n > NE):
                experts(EG * NE)
            sp.wait_ge(h_updated, 4 * DEPTH)
            sp.dma_start(out[0].rearrange("(t p) d -> p t d", p=P), h[:, :, :]).then_inc(out_stored, 16)
            sp.wait_ge(out_stored, 16)

        @block.gpsimd
        def _(pool):
            steps = [0]

            def link(ins):
                steps[0] += 1
                ins.then_inc(pool_step, 1)
                pool.wait_ge(pool_step, steps[0])

            def gain(dst, rows, loaded):
                for n, row in enumerate(rows):
                    width = row.shape[-1]
                    pool.dma_start(dst[:, n * width:(n + 1) * width],
                                   row.to_broadcast([P, width])).then_inc(loaded, 16)

            def gating_weights(layer):
                pool.dma_start(ws_raw, sgu_w[layer].rearrange("g t s -> t g s")).then_inc(ws_loaded, 16)
                pool.dma_start(sb_rows[:, :], sgu_b[layer]).then_inc(sb_loaded, 16)
                pool.wait_ge(ws_loaded, 16 * (layer + 1))
                nc.gpsimd.affine_select(out=ws_raw, in_=ws_raw, compare_op=ALU.is_ge, fill=0.0, base=0,
                                        pattern=[[0, NG], [-1, P]], channel_multiplier=1).then_inc(ws_masked, 1)

            with nc.allow_non_contiguous_dma(reason="256 positions, one per partition"):
                pool.dma_start(pos_i[:, :], positions.rearrange("o (t p) -> p (o t)", p=P)).then_inc(small_loaded, 16)
            pool.dma_start(sinks[:, :, :].rearrange("p l h -> p (l h)"),
                           attn_sinks.rearrange("l h -> (l h)").unsqueeze(0).to_broadcast([P, DEPTH * NQ])
                           ).then_inc(small_loaded, 16)
            pool.dma_start(wr[:, :, :], stacked(moe_router[0])).then_inc(small_loaded, 16)
            gain(g_pre, [pre_mix_norm[0:1, :]], pre_loaded)
            nc.gpsimd.memset(eps[:, :], EPS)
            nc.gpsimd.memset(half_pi[:, :], float(np.pi / 2))
            for j in range(HALF):
                f = np.power(np.float32(THETA), -np.float32(2 * j) / np.float32(ROPE_DIM), dtype=np.float32)
                nc.gpsimd.memset(inv_freq[:, j:j + 1], float(f))
            nc.gpsimd.memset(ones[:, :], 1.0)
            nc.gpsimd.memset(ident[:, :], 0.0)
            nc.gpsimd.memset(upper[:, :], 1.0)
            nc.gpsimd.iota(iota_i[:, :], pattern=[[1, P]], base=0, channel_multiplier=0)
            link(nc.gpsimd.memset(mask[:, :], 0.0))
            nc.gpsimd.affine_select(out=ident[:, :], in_=ident[:, :], compare_op=ALU.not_equal, fill=1.0, base=0,
                                    pattern=[[-1, P]], channel_multiplier=1)
            nc.gpsimd.affine_select(out=upper[:, :], in_=upper[:, :], compare_op=ALU.is_ge, fill=0.0, base=0,
                                    pattern=[[1, P]], channel_multiplier=-1)
            nc.gpsimd.affine_select(out=mask[:, 0:P], in_=mask[:, 0:P], compare_op=ALU.is_ge, fill=NEG, base=-1,
                                    pattern=[[1, P]], channel_multiplier=-1)
            nc.gpsimd.affine_select(out=mask[:, P:2 * P], in_=mask[:, P:2 * P], compare_op=ALU.is_ge, fill=NEG,
                                    base=0, pattern=[[-1, P]], channel_multiplier=1).then_inc(consts_ready, 1)
            gating_weights(0)
            gain(g_ln[:, :, :].rearrange("p a c -> p (a c)"), [sgu_ln_g[0:1, :], sgu_ln_b[0:1, :]], ln_loaded)
            gain(g_out, [attn_out_norm[0:1, :], sgu_out_norm[0:1, :]], out_loaded)
            gain(g_post, [post_mix_norm[0:1, :]], post_loaded)
            for layer in range(DEPTH):
                pool.wait_ge(tok_ready, 8 * layer + 2)
                gain(g_pre, [pre_ffn_norm[layer:layer + 1, :]], pre_loaded)
                if layer + 1 < DEPTH:
                    nxt = slice(layer + 1, layer + 2)
                    pool.wait_ge(vn_ready, layer + 1)
                    gain(g_ln[:, :, :].rearrange("p a c -> p (a c)"), [sgu_ln_g[nxt, :], sgu_ln_b[nxt, :]], ln_loaded)
                    pool.wait_ge(sgu_ready, 2 * (layer + 1))
                    gating_weights(layer + 1)
                    pool.wait_ge(tok_ready, 8 * layer + 6)
                    gain(g_out, [attn_out_norm[nxt, :], sgu_out_norm[nxt, :]], out_loaded)
                pool.wait_ge(h_updated, 4 * layer + 2)
                gain(g_post, [post_ffn_norm[layer:layer + 1, :]], post_loaded)
                if layer + 1 < DEPTH:
                    pool.wait_ge(tok_ready, 8 * layer + 8)
                    gain(g_pre, [pre_mix_norm[nxt, :]], pre_loaded)
                    pool.wait_ge(h_updated, 4 * layer + 4)
                    gain(g_post, [post_mix_norm[nxt, :]], post_loaded)

        @block.scalar
        def _(act):
            steps = [0]
            A = nc.scalar.activation

            def link(ins):
                steps[0] += 1
                ins.then_inc(act_step, 1)
                act.wait_ge(act_step, steps[0])

            def split(m, loops=0):
                act.wait_ge(raw_arrived[m % NRAW], 16 * (m // NRAW + 1) + 16 * loops)
                if m >= NSPL:
                    act.wait_ge(unit_used, m - NSPL + 1 + BODY * loops)
                A(w_hi[:, m % NSPL, :], raw[:, m % NRAW, :], ACT.Copy).then_inc(hi_ready, 1)

            def splits(a, b, loops=0):
                for m in range(a, b):
                    split(m, loops)

            def square(col, src, width, sq=sq):
                if steps[0]:
                    act.wait_ge(act_step, steps[0])
                A(sq[:, 0:width], src, ACT.Square, accum_out=ssq[:, col:col + 1]).then_inc(act_step, 1)
                steps[0] += 1

            def root(col, n, width):
                act.wait_ge(act_step, steps[0])
                A(std[:, col:col + n], ssq[:, col:col + n], ACT.Sqrt, bias=eps[:, :],
                  scale=1.0 / width).then_inc(std_ready, 1)

            def act_high(layer, first, n):
                for i in range(first, first + n):
                    bank, chunks, t = TURNS[i]
                    act.wait_ge(tok_turned, N_TURNS * layer + i + 1)
                    A(act_hi[:, chunks, t * P:(t + 1) * P], ps[:, bank, :].rearrange("p (k t) -> p k t", k=4),
                      ACT.Copy).then_inc(act_hi_ready, 1)

            def entry(layer, first, m, early):
                splits(m + early, m + 2)
                act_high(layer, first, 2)
                splits(max(m + 2, m + early), m + 4)
                act_high(layer, first + 2, 2)
                splits(m + 4, m + 6)
                for t in range(T):
                    if layer or first:
                        act.wait_ge(h_updated, 4 * layer - (0 if first else 2) + t + 1)
                    square(PRE + t, h[:, t, :], D)
                root(PRE, T, D)

            def post_squares(k, t, halves):
                act.wait_ge(act_step, steps[0])
                for half, src in enumerate(halves):
                    before = 2 * T * k + 2 * t + half
                    if before:
                        act.wait_ge(half_squared, before)
                    A(sq[:, 0:BANK], src, ACT.Square, accum_out=half_ssq[:, t, half:half + 1]).then_inc(half_squared, 1)
                act.wait_ge(half_squared, 2 * T * k + 2 * t + 2)
                link(A(half_ssq[:, t, 2:3], half_ssq[:, t, 1:2], ACT.Identity, bias=eps[:, :], scale=1.0 / D))
                A(std[:, POST + t:POST + t + 1], half_ssq[:, t, 0:1], ACT.Sqrt, bias=half_ssq[:, t, 2:3],
                  scale=1.0 / D).then_inc(std_ready, 1)

            def mixer(layer, m, early):
                entry(layer, PRE_MIX, m, early)
                if layer == 0:
                    act.wait_ge(angle_ready, 1)
                    A(sin[:, :, :], ang[:, :, :], ACT.Sin).then_inc(sincos_ready, 1)
                    A(cos[:, :, :], turns[:, :, :], ACT.Sin, scale=-1.0, bias=half_pi[:, :]).then_inc(sincos_ready, 1)
                splits(m + 6, m + 10)
                act.wait_ge(rstd_ready, 2 * layer + 1)
                act.wait_ge(unit_used, m + 4)
                for t in range(T):
                    A(qk[:, t, 0:NQ, :].rearrange("p (i j) d -> p j i d", j=NKV),
                      ps[:, 4 + t, :].rearrange("p (j i d) -> p j i d", j=NKV, i=QPK), ACT.Identity,
                      scale=q_scale[:, t:t + 1]).then_inc(qkv_copied, 1)
                splits(m + 10, m + 12)
                act.wait_ge(unit_used, m + 6)
                for t in range(T):
                    scale = rstd[:, PRE + t:PRE + t + 1]
                    A(qk[:, t, NQ:, :].rearrange("p j d -> p (j d)"), ps[:, 6 + t, 0:KVW], ACT.Identity,
                      scale=scale).then_inc(qkv_copied, 1)
                    A(vv[:, t, :], ps[:, 6 + t, KVW:2 * KVW], ACT.Identity, scale=scale).then_inc(qkv_copied, 1)
                splits(m + 12, m + 15)
                for b in (0, 2):
                    act.wait_ge(qk_turned, 3 * layer + b + 1)
                    n = 2 if b == 0 else 1
                    A(qk_t[:, 2 * b:2 * b + n, :], ps[:, 4 + b, 0:n * S].rearrange("p (k t) -> p k t", k=n),
                      ACT.Copy).then_inc(qk_t_act, 1)
                act.wait_ge(unit_used, m + 10)
                for t in range(T):
                    A(vg[:, t, :], ps[:, 2 + t, :], ACT.Gelu_apprx_tanh,
                      scale=rstd[:, PRE + t:PRE + t + 1]).then_inc(gelu_done, 1)
                split(m + 15)
                for t in range(T):
                    act.wait_ge(max_ready, T * layer + t + 1)
                    for hh in range(NQ):
                        A(sc[t][:, hh, :], sc[t][:, hh, :], ACT.Exp, bias=nmx[:, t, hh:hh + 1],
                          accum_out=rsum[:, t, hh:hh + 1]).then_inc(probs_ready, 1)
                A(sink_e[:, :, :], sink_d[:, :, :], ACT.Exp).then_inc(sink_ready, 1)
                act.wait_ge(var_ready, layer + 1)
                A(ln_std[:, :], ln_var[:, :], ACT.Sqrt, bias=eps[:, :], scale=1.0 / GD).then_inc(ln_std_ready, 1)
                splits(m + 16, m + 18)
                for b, bank in enumerate(PROB_BANKS):
                    act.wait_ge(probs_turned, 6 * layer + b + 1)
                    A(pt[:, 4 * b:4 * b + 4, :], ps[:, bank, :].rearrange("p (n q) -> p n q", n=4),
                      ACT.Copy).then_inc(pt_ready, 1)
                act.wait_ge(unit_used, m + 14)
                for t in range(T):
                    A(ug[:, t, :], ps[:, 2 + t, :], ACT.Gelu_apprx_tanh,
                      scale=rstd[:, PRE + t:PRE + t + 1]).then_inc(gelu_done, 1)
                for t in range(T):
                    act.wait_ge(attn_ready, T * layer + t + 1)
                    square(ATTN + t, tok[:, t, 0:AW], AW, sq_mix)
                root(ATTN, T, AW)
                act_high(layer, ATTN_HALF, 2)
                splits(m + 18, m + 20)
                act.wait_ge(sgu_ready, 2 * (layer + 1))
                for t in range(T):
                    square(SGU + t, tok[:, t, AW:], SW, sq_mix)
                root(SGU, T, SW)
                act_high(layer, SGU_HALF, 2)
                splits(m + 20, m + 24)
                for t in range(T):
                    if t == 0:
                        act.wait_ge(mix_done, layer + 1)
                    else:
                        act.wait_ge(unit_used, m + MIX_UNITS)
                    post_squares(2 * layer, t, mixed(t))
                entry(layer, PRE_FFN, m + MIX_UNITS, 2)

            def silu(units, tiles, width=BANK, scaled=True):
                act.wait_ge(unit_used, units)
                for t in range(tiles):
                    scale = rstd[:, PRE + t:PRE + t + 1] if scaled else 1.0
                    A(sil[:, t, 0:width], ps[:, 2 * t, 0:width], ACT.Silu, scale=scale).then_inc(sil_ready, 1)

            def turned(n, tiles, chunks=4):
                for t in range(tiles):
                    act.wait_ge(hid_turned, n + t + 1)
                    A(ht_hi[:, 0:chunks, t, :], ps[:, 6 + t, 0:chunks * P].rearrange("p (c j) -> p c j", c=chunks),
                      ACT.Copy).then_inc(ht_hi_ready, 1)

            act.wait_ge(consts_ready, 1)
            act.wait_ge(x_loaded, 16)
            mixer(0, 0, 0)

            m = DENSE0
            splits(m + 6, m + 12)
            act.wait_ge(rstd_ready, 2)
            silu(m + 8, T)
            splits(m + 12, m + 14)
            turned(0, T)
            m = DENSE0 + GU_UNITS
            with act.Fori(0, DG - 1) as g:
                splits(m + 6, m + 14, g)
                silu(m + 8 + BODY * g, T)
                splits(m + 14, m + 16, g)
                turned(T * (g + 1), T)
                splits(m + 16, m + 18, g)
            m += BODY * (DG - 1)
            splits(m + 6, m + 10)
            silu(m + 4, T, BANK // 2)
            turned(T * DG, T, 2)
            splits(MIX1, MIX1 + 4)
            for t in range(T):
                act.wait_ge(part_added, 2 + DENSE_PARTS - 2 * (T - 1 - t))
                post_squares(1, t, summed(t))

            mixer(1, MIX1, 4)

            act.wait_ge(small_loaded, 48)
            A(wr_hi[:, :, :], wr[:, :, :], ACT.Copy).then_inc(sincos_ready, 1)

            def gathered_high(b, count):
                act.wait_ge(gathered, count)
                A(xe_hi[:, 4 * b:4 * b + 4, :], ps[:, (7, 2)[b], :].rearrange("p (k j) -> p k j", k=4),
                  ACT.Copy).then_inc(xe_hi_ready, 1)

            def output(e):
                act.wait_ge(unit_used, MOE0 + EXPERT_UNITS * e)
                A(y[:, 0:BANK], ps[:, 4, :], ACT.Copy).then_inc(y_act, 1)

            act.wait_ge(top_ready, 1)
            A(e2[:, :], e2[:, :], ACT.Exp).then_inc(e2_ready, 1)
            act.wait_ge(n_exp_ready, 1)
            n = act.value_load(n_exp[0:1, 0:1], min_val=NE, max_val=2 * NE)
            for b in range(2):
                gathered_high(b, b + 1)
            with act.Fori(0, n) as e:
                done = EG * e
                with act.If(e > 0):
                    splits(MOE0, MOE0 + 4, done)
                    output(e)
                    splits(MOE0 + 4, MOE0 + 6, done)
                splits(MOE0 + 6, MOE0 + 12, done)
                silu(MOE0 + 8 + BODY * done, 1, scaled=False)
                splits(MOE0 + 12, MOE0 + 14, done)
                turned(DENSE_TILES + done, 1)
                m = MOE0 + GU_UNITS
                with act.Fori(0, EG - 2) as g:
                    splits(m + 6, m + 14, done + g)
                    silu(m + 8 + BODY * (done + g), 1, scaled=False)
                    splits(m + 14, m + 18, done + g)
                    turned(DENSE_TILES + done + g + 1, 1)
                last = done + EG - 2
                splits(m + 6, m + 14, last)
                silu(m + 8 + BODY * last, 1, scaled=False)
                splits(m + 14, m + 16, last)
                turned(DENSE_TILES + last + 1, 1)
                for b in range(2):
                    gathered_high(b, 3 * e + b + 4)
            output(n)
            for t in range(T):
                act.wait_ge(part_added, ADDED0 + 4 * n - 2 * (T - 1 - t))
                post_squares(3, t, summed(t))

        @block.vector
        def _(dve):
            steps = [0]
            V = nc.vector

            def link(ins):
                steps[0] += 1
                ins.then_inc(dve_step, 1)
                dve.wait_ge(dve_step, steps[0])

            def split(m, loops=0):
                dve.wait_ge(hi_ready, m + 1 + BODY * loops)
                V.tensor_tensor(w_lo[:, m % NSPL, :], raw[:, m % NRAW, :], w_hi[:, m % NSPL, :].bitcast(F32),
                                ALU.subtract).then_inc(lo_ready, 1)

            def splits(a, b, loops=0):
                for m in range(a, b):
                    split(m, loops)

            stds = [0]

            def inverse(col, n):
                stds[0] += 1
                dve.wait_ge(std_ready, stds[0])
                link(V.reciprocal(rstd[:, col:col + n], std[:, col:col + n]))

            def act_low(layer, first, n):
                for i in range(first, first + n):
                    bank, chunks, t = TURNS[i]
                    tt = slice(t * P, (t + 1) * P)
                    dve.wait_ge(act_hi_ready, N_TURNS * layer + i + 1)
                    V.tensor_tensor(act_lo[:, chunks, tt], ps[:, bank, :].rearrange("p (k t) -> p k t", k=4),
                                    act_hi[:, chunks, tt].bitcast(F32), ALU.subtract).then_inc(act_lo_ready, 1)

            def gained(t):
                V.tensor_tensor(tok[:, t, :], h[:, t, :], g_pre[:, :], ALU.mult).then_inc(tok_ready, 1)

            def post(k, t, halves):
                dve.wait_ge(post_loaded, 16 * (k + 1))
                for half, src in enumerate(halves):
                    c = slice(half * BANK, (half + 1) * BANK)
                    dve.wait_ge(half_squared, 2 * T * k + 2 * t + half + 1)
                    ins = V.tensor_tensor(tok[:, t, c], src, g_post[:, c], ALU.mult)
                link(ins)
                inverse(POST + t, 1)
                V.scalar_tensor_tensor(out=h[:, t, :], in0=tok[:, t, :], scalar=rstd[:, POST + t:POST + t + 1],
                                       in1=h[:, t, :], op0=ALU.mult, op1=ALU.add).then_inc(h_updated, 1)
                if k < 2 * DEPTH - 1:
                    dve.wait_ge(h_updated, T * k + t + 1)
                    dve.wait_ge(pre_loaded, 16 * (k + 2))
                    gained(t)

            def entry(layer, first, m, early):
                splits(m + early, m + 2)
                act_low(layer, first, 2)
                splits(max(m + 2, m + early), m + 4)
                act_low(layer, first + 2, 2)
                splits(m + 4, m + 6)
                inverse(PRE, T)
                V.tensor_scalar(q_scale[:, :], rstd[:, PRE:PRE + T], HD ** -0.5, None, ALU.mult).then_inc(rstd_ready, 1)

            def rope(layer):
                dve.wait_ge(qkv_copied, 3 * T * (layer + 1))
                H = NQ + NKV
                a, b = qk[:, :, :, 0:HALF], qk[:, :, :, HALF:2 * HALF]

                def bc(f):
                    return f[:, :, :].unsqueeze(2).to_broadcast([P, T, H, HALF])
                for t in range(T):
                    a, b = qk[:, t, :, 0:HALF], qk[:, t, :, HALF:2 * HALF]
                    c = cos[:, t, :].unsqueeze(1).to_broadcast([P, H, HALF])
                    s = sin[:, t, :].unsqueeze(1).to_broadcast([P, H, HALF])
                    V.tensor_tensor(rot[:, 0, t], a, c, ALU.mult)
                    V.tensor_tensor(rot[:, 1, t], b, s, ALU.mult)
                    V.tensor_tensor(rot[:, 2, t], b, c, ALU.mult)
                    link(V.tensor_tensor(rot[:, 3, t], a, s, ALU.mult))
                    V.tensor_tensor(a, rot[:, 0, t], rot[:, 1, t], ALU.subtract)
                    V.tensor_tensor(b, rot[:, 2, t], rot[:, 3, t], ALU.add).then_inc(qk_roped, 1)

            def mixer(layer, m, early):
                entry(layer, PRE_MIX, m, early)
                splits(m + 6, m + 10)
                for b in range(2):
                    dve.wait_ge(ws_turned, 3 * layer + b + 1)
                    V.tensor_copy(ws_t[:, 4 * b:4 * b + 4, :],
                                  ps[:, b, :].rearrange("p (g t) -> p g t", g=4)).then_inc(ws_copied, 1)
                dve.wait_ge(ws_turned, 3 * layer + 3)
                V.tensor_copy(sb_t[:, :], ps[:, 2, 0:NG]).then_inc(ws_copied, 1)
                splits(m + 10, m + 12)
                if layer == 0:
                    dve.wait_ge(sincos_ready, 2)
                rope(layer)
                splits(m + 12, m + 15)
                dve.wait_ge(qk_turned, 3 * layer + 2)
                V.tensor_copy(qk_t[:, 2:4, :], ps[:, 5, :].rearrange("p (k t) -> p k t", k=2)).then_inc(qk_t_dve, 1)
                split(m + 15)
                for t in range(T):
                    keys = (t + 1) * P
                    per = BANK // keys
                    own = mask[:, (T - 1 - t) * P:].unsqueeze(1).to_broadcast([P, per, keys])
                    for b in range(NQ // per):
                        dve.wait_ge(scores_done, 6 * layer + 2 * t + b + 1)
                        ins = V.tensor_tensor(sc[t][:, per * b:per * (b + 1), :],
                                              ps[:, PROB_BANKS[2 * t + b], :].rearrange("p (h k) -> p h k", h=per),
                                              own, ALU.add)
                    link(ins)
                    link(V.tensor_reduce(mx[:, t, :], sc[t], AX.X, ALU.max))
                    link(V.tensor_tensor(mx[:, t, :], mx[:, t, :], sinks[:, layer, :], ALU.max))
                    link(V.tensor_tensor(sink_d[:, t, :], sinks[:, layer, :], mx[:, t, :], ALU.subtract))
                    V.tensor_scalar(nmx[:, t, :], mx[:, t, :], -1.0, None, ALU.mult).then_inc(max_ready, 1)
                dve.wait_ge(gelu_done, 4 * layer + 2)
                v3 = vg[:, :, :].rearrange("p t (g d) -> p (t g) d", g=NG)
                for t in range(T):
                    vt = vg[:, t, :].rearrange("p (g d) -> p g d", g=NG)
                    ins = V.tensor_reduce(ln_mu[:, t * NG:(t + 1) * NG], vt, AX.X, ALU.add)
                link(ins)
                link(V.tensor_scalar(ln_mu[:, :], ln_mu[:, :], 1.0 / GD, None, ALU.mult))
                link(V.tensor_tensor(v3, v3, ln_mu[:, :].unsqueeze(2).to_broadcast([P, T * NG, GD]), ALU.subtract))
                link(V.tensor_tensor(ln_sq, vg[:, :, :], vg[:, :, :], ALU.mult))
                for t in range(T):
                    ins = V.tensor_reduce(ln_var[:, t * NG:(t + 1) * NG],
                                          ln_sq[:, t, :].rearrange("p (g d) -> p g d", g=NG), AX.X, ALU.add)
                ins.then_inc(var_ready, 1)
                splits(m + 16, m + 18)
                dve.wait_ge(ln_std_ready, layer + 1)
                link(V.reciprocal(ln_std[:, :], ln_std[:, :]))
                link(V.tensor_tensor(v3, v3, ln_std[:, :].unsqueeze(2).to_broadcast([P, T * NG, GD]), ALU.mult))
                dve.wait_ge(ln_loaded, 32 * (layer + 1))
                link(V.tensor_tensor(vg[:, :, :], vg[:, :, :], g_ln[:, 0:1, :].to_broadcast([P, T, SW]), ALU.mult))
                V.tensor_tensor(vg[:, :, :], vg[:, :, :], g_ln[:, 1:2, :].to_broadcast([P, T, SW]),
                                ALU.add).then_inc(vn_ready, 1)
                dve.wait_ge(sink_ready, layer + 1)
                link(V.tensor_tensor(rsum[:, :, :], rsum[:, :, :], sink_e[:, :, :], ALU.add))
                link(V.reciprocal(rinv[:, :, :], rsum[:, :, :]))
                for t in range(T):
                    dve.wait_ge(pv_done, T * layer + t + 1)
                    V.tensor_tensor(tok[:, t, 0:AW].rearrange("p (h d) -> p h d", h=NQ),
                                    ps[:, 4 + t, :].rearrange("p (h d) -> p h d", h=NQ),
                                    rinv[:, t, :].unsqueeze(2).to_broadcast([P, NQ, HD]), ALU.mult
                                    ).then_inc(attn_ready, 1)

                def out_norm(col, c0, loaded):
                    dve.wait_ge(out_loaded, 32 * (layer + 1))
                    inverse(col, T)
                    for t in range(T):
                        V.scalar_tensor_tensor(out=tok[:, t, c0:c0 + AW], in0=tok[:, t, c0:c0 + AW],
                                               scalar=rstd[:, col + t:col + t + 1], in1=g_out[:, c0:c0 + AW],
                                               op0=ALU.mult, op1=ALU.mult).then_inc(tok_ready, 1)

                dve.wait_ge(attn_ready, T * (layer + 1))
                out_norm(ATTN, 0, 1)
                act_low(layer, ATTN_HALF, 2)
                splits(m + 18, m + 20)
                for b in range(2):
                    dve.wait_ge(sgu_done, 2 * layer + b + 1)
                    for i in range(4):
                        g = 4 * b + i
                        ins = V.scalar_tensor_tensor(
                            out=tok[:, :, AW + g * GD:AW + (g + 1) * GD],
                            in0=ps[:, 2 + b, i * P:(i + 1) * P].rearrange("p (t d) -> p t d", t=T),
                            scalar=sb_t[:, g:g + 1], in1=ug[:, :, g * GD:(g + 1) * GD], op0=ALU.add, op1=ALU.mult)
                    ins.then_inc(sgu_ready, 1)
                dve.wait_ge(sgu_ready, 2 * (layer + 1))
                out_norm(SGU, AW, 2)
                act_low(layer, SGU_HALF, 2)
                splits(m + 20, m + 24)
                for t in range(T):
                    if t == 0:
                        dve.wait_ge(mix_done, layer + 1)
                    else:
                        dve.wait_ge(unit_used, m + MIX_UNITS)
                    post(2 * layer, t, mixed(t))
                entry(layer, PRE_FFN, m + MIX_UNITS, 2)

            def hidden(n, tiles, width=BANK, scaled=True):
                for t in range(tiles):
                    dve.wait_ge(sil_ready, n + t + 1)
                    up = ps[:, 2 * t + 1, 0:width]
                    if scaled:
                        V.scalar_tensor_tensor(out=hid[:, t, 0:width], in0=up, scalar=rstd[:, PRE + t:PRE + t + 1],
                                               in1=sil[:, t, 0:width], op0=ALU.mult, op1=ALU.mult
                                               ).then_inc(hid_ready, 1)
                    else:
                        V.tensor_tensor(hid[:, t, 0:width], sil[:, t, 0:width], up, ALU.mult).then_inc(hid_ready, 1)

            def turned(n, tiles, chunks=4):
                for t in range(tiles):
                    dve.wait_ge(ht_hi_ready, n + t + 1)
                    V.tensor_tensor(ht_lo[:, 0:chunks, t, :],
                                    ps[:, 6 + t, 0:chunks * P].rearrange("p (c j) -> p c j", c=chunks),
                                    ht_hi[:, 0:chunks, t, :].bitcast(F32), ALU.subtract).then_inc(ht_lo_ready, 1)

            def add_parts(n, banks, units=None, tiles=range(T)):
                for t in tiles:
                    for half in range(2):
                        if units is not None and (t, half) == (T - 1, 1):
                            dve.wait_ge(unit_used, units)
                        else:
                            dve.wait_ge(part_done, n + 2 * t + half + 1)
                        cols = slice(half * BANK, (half + 1) * BANK)
                        V.tensor_tensor(facc[:, t, cols], facc[:, t, cols], ps[:, banks[half], :],
                                        ALU.add).then_inc(part_added, 1)

            def clear_sums():
                for t in range(T):
                    V.memset(facc[:, t, :], 0.0).then_inc(part_added, 1)

            dve.wait_ge(consts_ready, 1)
            dve.wait_ge(x_loaded, 16)
            dve.wait_ge(pre_loaded, 16)
            for t in range(T):
                gained(t)
            dve.wait_ge(small_loaded, 48)
            V.tensor_copy(iota[:, :], iota_i[:, :])
            link(V.tensor_copy(pos[:, :], pos_i[:, :]))
            for t in range(T):
                ins = V.tensor_scalar(ang[:, t, :], inv_freq[:, :], pos[:, t:t + 1], None, ALU.mult)
            link(ins)
            big = 1.5 * 2 ** 23
            link(V.tensor_scalar(turns[:, :, :], ang[:, :, :], 1 / (2 * np.pi), big, ALU.mult, ALU.add))
            link(V.tensor_scalar(turns[:, :, :], turns[:, :, :], -big, None, ALU.add))
            c1 = 6.28125
            c2 = float(np.float32(np.round((2 * np.pi - c1) * 2 ** 20) / 2 ** 20))
            for c in (c1, c2, 2 * np.pi - c1 - c2):
                link(V.scalar_tensor_tensor(out=ang[:, :, :], in0=turns[:, :, :], scalar=-float(c), in1=ang[:, :, :],
                                            op0=ALU.mult, op1=ALU.add))
            link(V.tensor_scalar(ang[:, :, :], ang[:, :, :], 3.1415925, -3.1415925, ALU.min, ALU.max))
            V.scalar_tensor_tensor(out=turns[:, :, :], in0=ang[:, :, :], scalar=-1.0, in1=ang[:, :, :],
                                   op0=ALU.mult, op1=ALU.max).then_inc(angle_ready, 1)

            mixer(0, 0, 0)

            clear_sums()
            m = DENSE0
            splits(m + 6, m + 12)
            hidden(0, T)
            splits(m + 12, m + 14)
            turned(0, T)
            m = DENSE0 + GU_UNITS
            with dve.Fori(0, DG - 1) as g:
                splits(m + 6, m + 14, g)
                hidden(T * (g + 1), T)
                add_parts(3 * g, (4, 5), m + BODY * (g + 1))
                splits(m + 14, m + 16, g)
                turned(T * (g + 1), T)
                splits(m + 16, m + 18, g)
            m += BODY * (DG - 1)
            splits(m + 6, m + 10)
            hidden(T * DG, T, BANK // 2)
            add_parts(3 * (DG - 1), (4, 5), m + BODY - 4)
            turned(T * DG, T, 2)
            splits(MIX1, MIX1 + 4)
            for t in range(T):
                add_parts(3 * DG, (4, 5), MIX1, (t,))
                dve.wait_ge(part_added, 2 + DENSE_PARTS - 2 * (T - 1 - t))
                post(1, t, summed(t))

            mixer(1, MIX1, 4)

            dve.wait_ge(sincos_ready, 3)
            V.tensor_tensor(wr_lo[:, :, :], wr[:, :, :], wr_hi[:, :, :].bitcast(F32), ALU.subtract
                            ).then_inc(tokens_ready, 1)
            dve.wait_ge(tok_turned, N_TURNS * DEPTH)
            for t in range(T):
                V.tensor_scalar(tok[:, t, :], tok[:, t, :], rstd[:, PRE + t:PRE + t + 1], None,
                                ALU.mult).then_inc(tokens_ready, 1)
            clear_sums()
            dve.wait_ge(logits_done, 1)
            for t in range(T):
                ins = V.tensor_scalar(lg[:, t, :], ps[:, 6, t * NE:(t + 1) * NE], rstd[:, PRE + t:PRE + t + 1], None,
                                      ALU.mult)
            link(ins)
            experts_iota = iota[:, 0:NE].unsqueeze(1).to_broadcast([P, T, NE])

            def wide(a):
                return a.unsqueeze(2).to_broadcast([P, T, NE])

            for r in range(2):
                link(V.tensor_reduce(top[:, r, :], lg[:, :, :], AX.X, ALU.max))
                link(V.tensor_tensor(cand[:, :, :], lg[:, :, :], wide(top[:, r, :]), ALU.is_lt))
                link(V.scalar_tensor_tensor(out=cand[:, :, :], in0=cand[:, :, :], scalar=100.0, in1=experts_iota,
                                            op0=ALU.mult, op1=ALU.add))
                link(V.tensor_reduce(at[:, :], cand[:, :, :], AX.X, ALU.min))
                link(V.tensor_tensor(pick[:, r], experts_iota, wide(at[:, :]), ALU.is_equal))
                if r == 0:
                    link(V.scalar_tensor_tensor(out=lg[:, :, :], in0=pick[:, 0], scalar=-3e38, in1=lg[:, :, :],
                                                op0=ALU.mult, op1=ALU.add))
            link(V.tensor_tensor(chosen[:, :, :], pick[:, 0], pick[:, 1], ALU.add))
            V.tensor_tensor(e2[:, :], top[:, 1, :], top[:, 0, :], ALU.subtract).then_inc(top_ready, 1)
            dve.wait_ge(e2_ready, 1)
            link(V.tensor_scalar(g12[:, 0, :], e2[:, :], 1.0, None, ALU.add))
            link(V.reciprocal(g12[:, 0, :], g12[:, 0, :]))
            link(V.tensor_tensor(g12[:, 1, :], g12[:, 0, :], e2[:, :], ALU.mult))
            for r in range(2):
                link(V.tensor_tensor(pick[:, r], pick[:, r], wide(g12[:, r, :]), ALU.mult))
            for r in range(2):
                V.tensor_tensor(gate[:, :, r * NE:(r + 1) * NE], pick[:, 0], pick[:, 1], ALU.add)
            dve.wait_ge(counts_done, 1)
            link(V.tensor_tensor(rank[:, :, 0:NE], ps[:, 7, 0:T * NE].rearrange("p (t e) -> p t e", t=T),
                                 chosen[:, :, :], ALU.mult))
            link(V.tensor_scalar(rank[:, :, 0:NE], rank[:, :, 0:NE], -1.0, None, ALU.add))
            V.memset(rank[:, :, 2 * NE:], -1.0)
            link(V.tensor_scalar(rank[:, :, NE:2 * NE], rank[:, :, 0:NE], -float(P), None, ALU.add))
            link(V.tensor_reduce(cnt[:, :], ps[:, 7, T * NE:(T + 1) * NE], AX.X, ALU.max))
            link(V.tensor_scalar(n_exp_f[:, :], cnt[:, :], P + 0.5, float(NE), ALU.is_gt, ALU.mult))
            link(V.tensor_scalar(n_exp_f[:, :], n_exp_f[:, :], float(NE), None, ALU.add))
            V.tensor_copy(n_exp[:, :], n_exp_f[:, :]).then_inc(n_exp_ready, 1)
            dve.wait_ge(n_exp_ready, 1)
            n = dve.value_load(n_exp[0:1, 0:1], min_val=NE, max_val=2 * NE)

            def select(e):
                for t in range(T):
                    V.tensor_scalar(sel[:, t, :], iota[:, :], rank[:, t, bass.ds(e, 1)], None,
                                    ALU.is_equal).then_inc(sel_ready, 1)

            def gathered_low(b, count):
                dve.wait_ge(xe_hi_ready, count)
                c = slice(4 * b, 4 * b + 4)
                V.tensor_tensor(xe_lo[:, c, :], ps[:, (7, 2)[b], :].rearrange("p (k j) -> p k j", k=4),
                                xe_hi[:, c, :].bitcast(F32), ALU.subtract).then_inc(xe_lo_ready, 1)

            def output(e):
                dve.wait_ge(unit_used, MOE0 + EXPERT_UNITS * e)
                V.tensor_copy(y[:, BANK:], ps[:, 5, :]).then_inc(y_dve, 1)

            select(0)
            for b in range(2):
                gathered_low(b, b + 1)
            with dve.Fori(0, n) as e:
                done = EG * e
                with dve.If(e > 0):
                    splits(MOE0, MOE0 + 4, done)
                    output(e)
                    splits(MOE0 + 4, MOE0 + 6, done)
                splits(MOE0 + 6, MOE0 + 12, done)
                hidden(DENSE_TILES + done, 1, scaled=False)
                with dve.If(e > 0):
                    add_parts(3 * (DG + 1) + 4 * (e - 1), (2, 3))
                splits(MOE0 + 12, MOE0 + 14, done)
                turned(DENSE_TILES + done, 1)
                select(e + 1)
                for t in range(T):
                    V.tensor_scalar(sel_g[:, t, :], iota[:, :], rank[:, t, bass.ds(e, 1)], gate[:, t, bass.ds(e, 1)],
                                    ALU.is_equal, ALU.mult).then_inc(sel_ready, 1)
                m = MOE0 + GU_UNITS
                with dve.Fori(0, EG - 2) as g:
                    splits(m + 6, m + 14, done + g)
                    hidden(DENSE_TILES + done + g + 1, 1, scaled=False)
                    splits(m + 14, m + 18, done + g)
                    turned(DENSE_TILES + done + g + 1, 1)
                last = done + EG - 2
                splits(m + 6, m + 14, last)
                hidden(DENSE_TILES + last + 1, 1, scaled=False)
                splits(m + 14, m + 16, last)
                turned(DENSE_TILES + last + 1, 1)
                dve.wait_ge(gathered, 3 * e + 3)
                V.tensor_copy(sel_t, ps[:, 3, 0:S].rearrange("p (t j) -> p t j", t=T)).then_inc(sel_t_ready, 1)
                for b in range(2):
                    gathered_low(b, 2 * e + b + 3)
            output(n)
            for t in range(T):
                add_parts(3 * (DG + 1) + 4 * (n - 1), (2, 3), None, (t,))
                dve.wait_ge(part_added, ADDED0 + 4 * n - 2 * (T - 1 - t))
                post(3, t, summed(t))

        @block.tensor
        def _(pe):
            mm = nc.tensor.matmul

            def product(o, a_hi, a_lo, b_hi, b_lo, first, last):
                mm(o, a_hi, b_hi, start=first, stop=False)
                mm(o, a_lo, b_hi, start=False, stop=False)
                return mm(o, a_hi, b_lo, start=False, stop=last)

            def unit(m, k, loops=0):
                pe.wait_ge(lo_ready, m + 1 + BODY * loops)
                return unit_view(w_hi, m % NSPL, k), unit_view(w_lo, m % NSPL, k)

            def turn(layer, first, n, per_tile):
                for i in range(first, first + n):
                    bank, chunks, t = TURNS[i]
                    if (i - first) % per_tile == 0:
                        ready = {PRE_MIX: 0, ATTN_HALF: 2, SGU_HALF: 4, PRE_FFN: 6}[first]
                        pe.wait_ge(tok_ready, 8 * layer + ready + t + 1)
                    for c in range(4):
                        k = chunks.start + c
                        ins = nc.tensor.transpose(ps[:, bank, c * P:(c + 1) * P], tok[:, t, k * P:(k + 1) * P],
                                                  ident[:, :])
                    ins.then_inc(tok_turned, 1)

            def group(units, k, width, tiles=T, loops=0, a=(act_hi, act_lo), before=None, after=None):
                a_hi, a_lo = a
                for t in range(tiles):
                    if before is not None:
                        before(t)
                    tt = slice(t * P, (t + 1) * P)
                    for m, row, bank in units:
                        if t == 0:
                            pe.wait_ge(lo_ready, m + 1 + BODY * loops)
                        hi, lo = unit_view(w_hi, m % NSPL, k), unit_view(w_lo, m % NSPL, k)
                        for i in range(k):
                            r = row + i
                            ins = product(ps[:, bank(t), 0:width], a_hi[:, r, tt], a_lo[:, r, tt],
                                          hi[:, i, :], lo[:, i, :], r == 0, r == KC - 1)
                        if t == tiles - 1:
                            ins.then_inc(unit_used, 1)
                    if after is not None and t < tiles - 1:
                        ins.then_inc(after, 1)

            def columns(m, n, k, bank0, width, before=None):
                group([(m + u, u * k, lambda t: bank0 + t) for u in range(n)], k, width, before=before)

            def lows(layer, first, per_tile):
                return lambda t: pe.wait_ge(act_lo_ready, N_TURNS * layer + first + per_tile * (t + 1))

            def mixer(layer, m):
                turn(layer, PRE_MIX, 4, 2)
                columns(m, 4, 2, 4, BANK, lows(layer, PRE_MIX, 2))
                pe.wait_ge(ws_masked, layer + 1)
                pe.wait_ge(sb_loaded, 16 * (layer + 1))
                for b in range(2):
                    for i in range(4):
                        ins = nc.tensor.transpose(ps[:, b, i * P:(i + 1) * P], ws_raw[:, 4 * b + i, :], ident[:, :])
                    ins.then_inc(ws_turned, 1)
                nc.tensor.transpose(ps[:, 2, 0:NG], sb_rows[:, :], ident[0:NG, 0:NG]).then_inc(ws_turned, 1)
                columns(m + 4, 2, 4, 6, 2 * KVW)
                pe.wait_ge(ws_copied, 3 * (layer + 1))
                columns(m + 6, 4, 2, 2, BANK)
                pe.wait_ge(qk_roped, T * (layer + 1))
                for c in range((NQ + NKV) // 2):
                    for t in range(T):
                        ins = nc.tensor.transpose(ps[:, 4 + c // 2, (c % 2) * S + t * P:(c % 2) * S + (t + 1) * P],
                                                  qk[:, t, 2 * c:2 * c + 2, :].rearrange("p j d -> p (j d)"),
                                                  ident[:, :])
                    if c in (1, 3, 4):
                        ins.then_inc(qk_turned, 1)
                pe.wait_ge(qk_t_act, 2 * (layer + 1))
                pe.wait_ge(qk_t_dve, layer + 1)
                for t in range(T):
                    keys = (t + 1) * P
                    per = BANK // keys
                    for hh in range(NQ):
                        j, i = hh // QPK, hh % QPK
                        rows = slice(HD * j, HD * (j + 1))
                        bank = PROB_BANKS[2 * t + hh // per]
                        ins = mm(ps[:, bank, (hh % per) * keys:(hh % per + 1) * keys],
                                 qk_t[rows, i, t * P:(t + 1) * P], qk_t[rows, QPK, 0:keys], start=True, stop=True)
                        if hh % per == per - 1:
                            ins.then_inc(scores_done, 1)
                pe.wait_ge(gelu_done, 4 * layer + 2)
                columns(m + 10, 4, 2, 2, BANK)
                for b, bank in enumerate(PROB_BANKS):
                    for i in range(4):
                        n = 4 * b + i
                        if n < NQ:
                            pe.wait_ge(probs_ready, T * NQ * layer + n + 1)
                            src = sc[0][:, n, :]
                        else:
                            hh, blk = (n - NQ) // 2, n % 2
                            pe.wait_ge(probs_ready, T * NQ * layer + NQ + hh + 1)
                            src = sc[1][:, hh, blk * P:(blk + 1) * P]
                        ins = nc.tensor.transpose(ps[:, bank, i * P:(i + 1) * P], src, ident[:, :])
                    ins.then_inc(probs_turned, 1)
                for t in range(T):
                    pe.wait_ge(pt_ready, 6 * layer + (2 if t == 0 else 6))
                    for hh in range(NQ):
                        j = hh // QPK
                        for blk in range(t + 1):
                            n = hh if t == 0 else NQ + 2 * hh + blk
                            ins = mm(ps[:, 4 + t, hh * HD:(hh + 1) * HD], pt[:, n, :],
                                     vv[:, blk, j * HD:(j + 1) * HD], start=(blk == 0), stop=(blk == t))
                    ins.then_inc(pv_done, 1)
                pe.wait_ge(vn_ready, layer + 1)
                pe.wait_ge(gelu_done, 4 * (layer + 1))
                for g in range(NG):
                    ins = mm(ps[:, 2 + g // 4, (g % 4) * P:(g % 4 + 1) * P].rearrange("p (t d) -> p t d", t=T),
                             ws_t[:, g, :], vg[:, :, g * GD:(g + 1) * GD], start=True, stop=True)
                    if g % 4 == 3:
                        ins.then_inc(sgu_done, 1)
                turn(layer, ATTN_HALF, 2, 1)
                for part, first in enumerate((ATTN_HALF, SGU_HALF)):
                    units = [(m + Z_UNITS + 4 * part + 2 * q + half, 4 * part + 2 * q,
                              lambda t, half=half: 4 + 2 * t + half) for q in range(2) for half in range(2)]
                    if part:
                        turn(layer, SGU_HALF, 2, 1)
                    group(units, 2, BANK, before=lows(layer, first, 1), after=mix_done if part else None)
                turn(layer, PRE_FFN, 4, 2)

            def gate_up(m, a, tiles, loops=0, width=BANK, before=None):
                k = UW // width
                per = KC // k
                for w in range(2):
                    group([(m + w * per + u, u * k, lambda t, w=w: 2 * t + w) for u in range(per)], k, width, tiles,
                          loops, a, before if w == 0 else None)

            def turn_hidden(n, tiles, chunks=4):
                for t in range(tiles):
                    pe.wait_ge(hid_ready, n + t + 1)
                    for c in range(chunks):
                        ins = nc.tensor.transpose(ps[:, 6 + t, c * P:(c + 1) * P], hid[:, t, c * P:(c + 1) * P],
                                                  ident[:, :])
                    ins.then_inc(hid_turned, 1)

            def dense_down(m, n, parts, loops=0, chunks=4):
                pe.wait_ge(ht_lo_ready, n)
                hl = [unit(m + c, 1, loops) for c in range(chunks)]
                for t in range(T):
                    for half in range(2):
                        pe.wait_ge(part_added, parts + 2 * t + half + 1)
                        for c in range(chunks):
                            cols = slice(half * BANK, (half + 1) * BANK)
                            ins = product(ps[:, 4 + half, :], ht_hi[:, c, t, :], ht_lo[:, c, t, :],
                                          hl[c][0][:, 0, cols], hl[c][1][:, 0, cols], c == 0, c == chunks - 1)
                            if (t, half) == (T - 1, 1):
                                ins.then_inc(unit_used, 1)
                        if (t, half) != (T - 1, 1):
                            ins.then_inc(part_done, 1)

            def expert_down(m, n, first, last, loops=0):
                pe.wait_ge(ht_lo_ready, n)
                for c in range(4):
                    hi, lo = unit(m + c, 1, loops)
                    for half in range(2):
                        cols = slice(half * BANK, (half + 1) * BANK)
                        ins = product(ps[:, 4 + half, :], ht_hi[:, c, 0, :], ht_lo[:, c, 0, :],
                                      hi[:, 0, cols], lo[:, 0, cols], first and c == 0, last and c == 3)
                    ins.then_inc(unit_used, 1)

            mixer(0, 0)
            dense = (act_hi, act_lo)
            gate_up(DENSE0, dense, T, before=lows(0, PRE_FFN, 2))
            turn_hidden(0, T)
            m = DENSE0 + GU_UNITS
            with pe.Fori(0, DG - 1) as g:
                gate_up(m, dense, T, g)
                dense_down(m + GU_UNITS, T * (g + 1), 4 * g, g)
                turn_hidden(T * (g + 1), T)
            m += BODY * (DG - 1)
            gate_up(m, dense, T, width=BANK // 2)
            dense_down(m + 4, T * DG, 4 * (DG - 1))
            turn_hidden(T * DG, T, 2)
            dense_down(m + 8, T * (DG + 1), 4 * DG, chunks=2)

            mixer(1, MIX1)

            lows(1, PRE_FFN, 2)(T - 1)
            pe.wait_ge(tokens_ready, 1)
            for t in range(T):
                tt = slice(t * P, (t + 1) * P)
                for k in range(KC):
                    o = ps[:, 6, t * NE:(t + 1) * NE]
                    product(o, act_hi[:, k, tt], act_lo[:, k, tt], wr_hi[:, k, :], wr_lo[:, k, :], k == 0, False)
                    ins = mm(o, act_lo[:, k, tt], wr_lo[:, k, :], start=False, stop=(k == KC - 1))
            ins.then_inc(logits_done, 1)
            pe.wait_ge(top_ready, 1)
            c0, c1 = chosen[:, 0, :], chosen[:, 1, :]
            mm(ps[:, 7, 0:NE], upper[:, :], c0, start=True, stop=True)
            mm(ps[:, 7, NE:2 * NE], ones[:, :], c0, start=True, stop=False)
            mm(ps[:, 7, NE:2 * NE], upper[:, :], c1, start=False, stop=True)
            mm(ps[:, 7, 2 * NE:3 * NE], ones[:, :], c0, start=True, stop=False)
            mm(ps[:, 7, 2 * NE:3 * NE], ones[:, :], c1, start=False, stop=True).then_inc(counts_done, 1)
            pe.wait_ge(n_exp_ready, 1)
            n = pe.value_load(n_exp[0:1, 0:1], min_val=NE, max_val=2 * NE)

            def gather():
                for b in range(2):
                    for i in range(4):
                        k = 4 * b + i
                        for t in range(T):
                            ins = mm(ps[:, (7, 2)[b], i * P:(i + 1) * P], tok[:, t, k * P:(k + 1) * P], sel[:, t, :],
                                     start=(t == 0), stop=(t == T - 1))
                    ins.then_inc(gathered, 1)

            def scatter(e):
                pe.wait_ge(sel_t_ready, e)
                pe.wait_ge(y_act, e)
                pe.wait_ge(y_dve, e)
                for t in range(T):
                    for half in range(2):
                        pe.wait_ge(part_added, ADDED0 - 5 + 4 * e + 2 * t + half)
                        mm(ps[:, 2 + half, :], sel_t[:, t, :], y[:, half * BANK:(half + 1) * BANK], start=True,
                           stop=True).then_inc(part_done, 1)

            pe.wait_ge(tokens_ready, 1 + T)
            pe.wait_ge(sel_ready, T)
            gather()
            picked = (xe_hi, xe_lo)
            with pe.Fori(0, n) as e:
                done = EG * e
                pe.wait_ge(xe_lo_ready, 2 * (e + 1))
                gate_up(MOE0, picked, 1, done)
                with pe.If(e > 0):
                    scatter(e)
                turn_hidden(DENSE_TILES + done, 1)
                m = MOE0 + GU_UNITS
                gate_up(m, picked, 1, done)
                expert_down(m + GU_UNITS, DENSE_TILES + done + 1, True, False, done)
                turn_hidden(DENSE_TILES + done + 1, 1)
                with pe.Fori(1, EG - 1) as g:
                    gate_up(m, picked, 1, done + g)
                    expert_down(m + GU_UNITS, DENSE_TILES + done + g + 1, False, False, done + g)
                    turn_hidden(DENSE_TILES + done + g + 1, 1)
                pe.wait_ge(sel_ready, T + 2 * T * (e + 1))
                for t in range(T):
                    ins = nc.tensor.transpose(ps[:, 3, t * P:(t + 1) * P], sel_g[:, t, :], ident[:, :])
                ins.then_inc(gathered, 1)
                gather()
                expert_down(m, DENSE_TILES + done + EG, False, True, done + EG - 1)
            scatter(n)


_INS = ["x", "positions", "pre_mix_norm", "w_in", "attn_sinks", "sgu_ln_g", "sgu_ln_b", "sgu_w", "sgu_b",
        "attn_out_norm", "sgu_out_norm", "w_out", "post_mix_norm", "pre_ffn_norm", "post_ffn_norm", "ffn_w_gate",
        "ffn_w_up", "ffn_w_down", "moe_router", "moe_w_gate", "moe_w_up", "moe_w_down"]


def kernel(**inputs):
    import numpy as _np
    import concourse.bacc as _bacc
    from concourse import mybir as _mybir
    from concourse.bass_utils import run_bass_kernel_spmd as _run

    nc = _bacc.Bacc("TRN2", target_bir_lowering=False, num_devices=1)
    arrays, args = {}, []
    for name in _INS:
        a = _np.ascontiguousarray(inputs[name])
        arrays[f"in_{name}"] = a
        args.append(nc.dram_tensor(f"in_{name}", a.shape, _mybir.dt.from_np(a.dtype), kind="ExternalInput").ap())
    out = nc.dram_tensor("out_0", (1, S, D), _mybir.dt.float32, kind="ExternalOutput").ap()
    trunk(nc, *args, out)
    r = _run(nc, [arrays], core_ids=[0])
    return r.results[0]["out_0"]
```

```python
from contextlib import ExitStack

import numpy as np

import concourse.bass as bass
from concourse import mybir

F32 = mybir.dt.float32
F32R = mybir.dt.float32r
I32 = mybir.dt.int32
ALU = mybir.AluOpType
ACT = mybir.ActivationFunctionType
AX = mybir.AxisListType

P = 128
D = 1024
S = 256
T = S // P
KC = D // P
DEPTH = 2
HD = 64
NQ, NKV = 8, 2
QPK = NQ // NKV
AW = NQ * HD
KVW = NKV * HD
NG = 8
GD = 64
SW = NG * GD
HALF = 8
THETA, ROPE_DIM = 500000.0, 16
FD = 2816
FE = 3584
NE = 8
EPS = 1e-6
NEG = -1e30
BANK = 512

UW = 1024
NRAW = 12
NSPL = 6
Z_UNITS, O_UNITS = 14, 8
MIX_UNITS = Z_UNITS + O_UNITS
GU_UNITS, DN_UNITS = 8, 4
BODY = GU_UNITS + DN_UNITS
DG = FD // BANK
EG = FE // BANK
DENSE0 = MIX_UNITS
DENSE_UNITS = DG * BODY + BODY // 2
MIX1 = DENSE0 + DENSE_UNITS
MOE0 = MIX1 + MIX_UNITS
EXPERT_UNITS = EG * BODY
assert NRAW == BODY and BODY % NSPL == 0 and FD % BANK == BANK // 2 and FE % BANK == 0


def trunk(nc, x, positions, pre_mix_norm, w_in, attn_sinks, sgu_ln_g, sgu_ln_b, sgu_w, sgu_b, attn_out_norm,
          sgu_out_norm, w_out, post_mix_norm, pre_ffn_norm, post_ffn_norm, ffn_w_gate, ffn_w_up, ffn_w_down,
          moe_router, moe_w_gate, moe_w_up, moe_w_down, out):
    ctx = ExitStack()
    with ctx:
        def sb(name, shape, dt=F32):
            return ctx.enter_context(nc.sbuf_tensor(name, shape, dt))

        def sem(name):
            return ctx.enter_context(nc.semaphore(name))

        raw = sb("raw", [P, NRAW, UW])
        w_hi = sb("w_hi", [P, NSPL, UW], F32R)
        w_lo = sb("w_lo", [P, NSPL, UW], F32R)
        h = sb("h", [P, T, D])
        tok = sb("tok", [P, T, D])
        act_hi = sb("act_hi", [P, KC, S], F32R)
        act_lo = sb("act_lo", [P, KC, S], F32R)
        g_post = sb("g_post", [P, D])
        mixers = sb("mixers", [P, 2 * T * SW + NG * P + 2 * SW + 2 * D + (NQ + NKV) * HD * 2 * T])
        taken = [0]

        def of_mixers(pattern, **sizes):
            columns = int(np.prod(list(sizes.values())))
            taken[0] += columns
            view = mixers[:, taken[0] - columns:taken[0]]
            return view.rearrange(f"p ({pattern}) -> p {pattern}", **sizes) if len(sizes) > 1 else view

        vg = of_mixers("t c", t=T, c=SW)
        ws_t = of_mixers("g t", g=NG, t=P)
        g_ln = of_mixers("a c", a=2, c=SW)
        ug = of_mixers("t c", t=T, c=SW)
        g_out = of_mixers("c", c=D)
        g_pre = of_mixers("c", c=D)
        qk_t = of_mixers("c s", c=(NQ + NKV) // 2, s=S)
        qk = of_mixers("t h d", t=T, h=NQ + NKV, d=HD)
        vv = sb("vv", [P, T, KVW])
        shared = sb("shared", [P, 6144])
        ht_hi = sb("ht_hi", [P, 4, T, P], F32R)
        ht_lo = sb("ht_lo", [P, 4, T, P], F32R)
        ident = sb("ident", [P, P])
        ones = sb("ones", [P, P])
        upper = sb("upper", [P, P])
        mask = sb("mask", [P, 2 * P])
        iota_i = sb("iota_i", [P, P], I32)
        iota = sb("iota", [P, P])
        inv_freq = sb("inv_freq", [P, HALF])
        pos_i = sb("pos_i", [P, T], I32)
        pos = sb("pos", [P, T])
        ang = sb("ang", [P, T, HALF])
        turns = sb("turns", [P, T, HALF])
        cos = sb("cos", [P, T, HALF])
        sin = sb("sin", [P, T, HALF])
        sinks = sb("sinks", [P, DEPTH, NQ])
        sb_rows = sb("sb_rows", [NG, P])
        sb_t = sb("sb_t", [P, NG])
        eps = sb("eps", [P, 1])
        half_pi = sb("half_pi", [P, 1])
        ssq = sb("ssq", [P, 4 * T])
        std = sb("std", [P, 4 * T])
        rstd = sb("rstd", [P, 4 * T])
        half_ssq = sb("half_ssq", [P, T, 3])
        q_scale = sb("q_scale", [P, T])
        ln_mu = sb("ln_mu", [P, T * NG])
        ln_var = sb("ln_var", [P, T * NG])
        ln_std = sb("ln_std", [P, T * NG])
        mx = sb("mx", [P, T, NQ])
        nmx = sb("nmx", [P, T, NQ])
        sink_d = sb("sink_d", [P, T, NQ])
        sink_e = sb("sink_e", [P, T, NQ])
        rsum = sb("rsum", [P, T, NQ])
        rinv = sb("rinv", [P, T, NQ])
        wr = sb("wr", [P, KC, NE])
        wr_split = sb("wr_split", [P, KC, 2, NE], F32R)
        fold = sb("fold", [2 * NE, NE])
        lg = sb("lg", [P, T, NE])
        pick = sb("pick", [P, 2, T, NE])
        cand = sb("cand", [P, T, NE])
        top = sb("top", [P, 2, T])
        at = sb("at", [P, T])
        e2 = sb("e2", [P, T])
        g12 = sb("g12", [P, 2, T])
        chosen = sb("chosen", [P, T, NE])
        gate = sb("gate", [P, T, 2 * NE])
        rank = sb("rank", [P, T, 2 * NE + 1])
        cnt = sb("cnt", [P, 1])
        n_exp_f = sb("n_exp_f", [P, 1])
        n_exp = sb("n_exp", [P, 1], I32)

        sc = [shared[:, 0:1024].rearrange("p (h k) -> p h k", h=NQ),
              shared[:, 1024:3072].rearrange("p (h k) -> p h k", h=NQ)]
        pt = shared[:, 3072:6144].rearrange("p (b q) -> p b q", b=24)
        rot = shared[:, 0:4 * T * (NQ + NKV) * HALF].rearrange("p (r t h j) -> p r t h j", r=4, t=T, h=NQ + NKV)
        facc = shared[:, 0:2048].rearrange("p (t d) -> p t d", t=T)
        sil = shared[:, 2048:3072].rearrange("p (t f) -> p t f", t=T)
        hid = shared[:, 3072:4096].rearrange("p (t f) -> p t f", t=T)
        y = shared[:, 4096:5120]
        sel = shared[:, 5120:5376].rearrange("p (t j) -> p t j", t=T)
        sel_g = shared[:, 5376:5632].rearrange("p (t j) -> p t j", t=T)
        sel_t = shared[:, 5632:5888].rearrange("p (t j) -> p t j", t=T)
        lg_parts = shared[0:2 * NE, 5376:5632]
        sq = shared[:, 5120:6144]
        sq_mix = shared[:, 0:AW]
        ws_raw = ug[:, :, :].rearrange("p t (g s) -> p (t g) s", s=P)
        ln_sq = tok[:, :, AW:AW + SW]
        late_hi, late_lo = (a.rearrange("p k (t j) -> p k t j", t=T) for a in (act_hi, act_lo))
        xe_hi = act_hi[:, :, 0:P]
        xe_lo = act_lo[:, :, 0:P]

        assert NE * UW <= taken[0]
        passed = sb("passed", [1, NE])

        PROB_BANKS = (4, 5, 6, 7, 0, 1)
        PART_BANKS = (2, 3, 4, 5)
        ps = ctx.enter_context(nc.psum_tensor("ps", [P, 8, BANK], F32))

        raw_arrived = [sem(f"raw_arrived{i}") for i in range(NRAW)]
        held_arrived = sem("held_arrived")
        hi_ready = sem("hi_ready")
        lo_ready = sem("lo_ready")
        unit_used = sem("unit_used")
        x_loaded = [sem(f"x_loaded{t}") for t in range(T)]
        first_gain_loaded = sem("first_gain_loaded")
        router_rounded = sem("router_rounded")
        router_split = sem("router_split")
        small_loaded = sem("small_loaded")
        pre_loaded, out_loaded, post_loaded, ln_loaded = (sem(f"{n}_gain_loaded") for n in ("pre", "out", "post", "ln"))
        ws_loaded = sem("ws_loaded")
        sb_loaded = sem("sb_loaded")
        ws_masked = sem("ws_masked")
        ident_ready = sem("ident_ready")
        consts_ready = sem("consts_ready")
        pool_step = sem("pool_step")
        act_step = sem("act_step")
        dve_step = sem("dve_step")
        angle_ready = sem("angle_ready")
        sincos_ready = sem("sincos_ready")
        std_ready = sem("std_ready")
        rstd_ready = sem("rstd_ready")
        first_tile_done = sem("first_tile_done")
        half_squared = sem("half_squared")
        tokens_ready = sem("tokens_ready")
        tok_ready = sem("tok_ready")
        tok_turned = sem("tok_turned")
        act_hi_ready = sem("act_hi_ready")
        act_lo_ready = sem("act_lo_ready")
        ws_turned = sem("ws_turned")
        ws_copied = sem("ws_copied")
        qkv_copied = sem("qkv_copied")
        qk_roped = sem("qk_roped")
        qk_turned = sem("qk_turned")
        qk_t_act = sem("qk_t_act")
        qk_t_dve = sem("qk_t_dve")
        gelu_done = sem("gelu_done")
        scores_done = sem("scores_done")
        max_ready = sem("max_ready")
        probs_ready = sem("probs_ready")
        sink_ready = sem("sink_ready")
        probs_turned = sem("probs_turned")
        pt_ready = sem("pt_ready")
        pv_done = sem("pv_done")
        attn_ready = sem("attn_ready")
        var_ready = sem("var_ready")
        ln_std_ready = sem("ln_std_ready")
        vn_ready = sem("vn_ready")
        sgu_done = sem("sgu_done")
        sgu_ready = sem("sgu_ready")
        h_updated = sem("h_updated")
        sil_ready = sem("sil_ready")
        hid_ready = sem("hid_ready")
        hid_turned = sem("hid_turned")
        ht_hi_ready = sem("ht_hi_ready")
        ht_lo_ready = sem("ht_lo_ready")
        part_done = sem("part_done")
        part_added = sem("part_added")
        lg_parts_done = sem("lg_parts_done")
        lg_parts_ready = sem("lg_parts_ready")
        logits_done = sem("logits_done")
        top_ready = sem("top_ready")
        e2_ready = sem("e2_ready")
        chosen_ready = sem("chosen_ready")
        counts_done = sem("counts_done")
        totals_done = sem("totals_done")
        n_exp_ready = sem("n_exp_ready")
        sel_ready = sem("sel_ready")
        gathered = sem("gathered")
        xe_hi_ready = sem("xe_hi_ready")
        xe_lo_ready = sem("xe_lo_ready")
        sel_t_ready = sem("sel_t_ready")
        y_act = sem("y_act")
        y_dve = sem("y_dve")
        out_stored = sem("out_stored")

        DENSE_TILES = T * (DG + 1)
        DENSE_PARTS = 2 * T * DG
        DENSE_SIGNALLED = 3 * (DG - 1) + 2
        ADDED0 = 2 + DENSE_PARTS + 2
        PRE, ATTN, SGU, POST = 0, T, 2 * T, 3 * T
        TURNS = ([(2 * t + b, slice(4 * b, 4 * b + 4), t) for t in range(T) for b in range(2)]
                 + [(6 + t, slice(0, 4), t) for t in range(T)] + [(2 + t, slice(4, 8), t) for t in range(T)]
                 + [(2 * t + b, slice(4 * b, 4 * b + 4), t) for t in range(T) for b in range(2)])
        PRE_MIX, ATTN_HALF, SGU_HALF, PRE_FFN = 0, 4, 6, 8
        N_TURNS = len(TURNS)
        OUT_ORDER = [(0, 0), (0, BANK), (2, 0), (2, BANK), (4, 0), (6, 0), (4, BANK), (6, BANK)]

        HELD = MOE0 + EXPERT_UNITS - 2
        HELD_CHUNK = (EG - 1) * 4 + 2

        def mixed(t):
            return [ps[:, 4 + 2 * t + half, :] for half in range(2)]

        def summed(t):
            return [facc[:, t, half * BANK:(half + 1) * BANK] for half in range(2)]

        def stacked(w):
            return w.rearrange("(k p) c -> p k c", p=P)

        def unit_view(ring, slot, k):
            return ring[:, slot, :].rearrange("p (k c) -> p k c", k=k)

        block = ctx.enter_context(nc.Block())

        @block.sync
        def _(sp):
            def load(m, src, k, loops=0):
                if m >= NRAW:
                    sp.wait_ge(lo_ready, m - NRAW + 1 + BODY * loops)
                sp.dma_start(unit_view(raw, m % NRAW, k), src).then_inc(raw_arrived[m % NRAW], 16)

            def mixer_units(layer, m):
                for c0, width in ((0, AW), (AW, 2 * KVW), (AW + 2 * KVW + SW, SW), (AW + 2 * KVW, SW)):
                    k = UW // width
                    for r in range(0, KC, k):
                        load(m, stacked(w_in[layer, r * P:(r + k) * P, c0:c0 + width]), k)
                        if m == 0:
                            load_x(1)
                        m += 1
                for r, c0 in OUT_ORDER:
                    load(m, stacked(w_out[layer, r * P:(r + 2) * P, c0:c0 + BANK]), 2)
                    m += 1

            def gate_up(m, w_gate, w_up, c0, loops=0):
                for w in (w_gate, w_up):
                    for r in range(0, KC, 2):
                        load(m, stacked(w[r * P:(r + 2) * P, bass.ds(c0, BANK)]), 2, loops)
                        m += 1

            def down(m, w_down, r0, loops=0, chunks=4):
                for c in range(chunks):
                    load(m, stacked(w_down[bass.ds(r0 + c * P, P), :]), 1, loops)
                    m += 1

            def load_x(t):
                sp.dma_start(h[:, t, :], x[0, t * P:(t + 1) * P, :]).then_inc(x_loaded[t], 16)

            load_x(0)
            sp.dma_start(g_pre[:, :], pre_mix_norm[0:1, :].to_broadcast([P, D])).then_inc(first_gain_loaded, 16)
            mixer_units(0, 0)
            wg, wu, wd = ffn_w_gate[0], ffn_w_up[0], ffn_w_down[0]
            gate_up(DENSE0, wg, wu, 0)
            with sp.Fori(0, DG - 1) as g:
                gate_up(DENSE0 + GU_UNITS, wg, wu, (g + 1) * BANK, g)
                down(DENSE0 + BODY + DN_UNITS, wd, g * BANK, g)
            m = DENSE0 + GU_UNITS + (DG - 1) * BODY
            for w in (wg, wu):
                for r in (0, 4):
                    load(m, stacked(w[r * P:(r + 4) * P, DG * BANK:FD]), 4)
                    m += 1
            down(m, wd, (DG - 1) * BANK)
            down(m + DN_UNITS, wd, DG * BANK, chunks=2)
            mixer_units(1, MIX1)

            def experts(first_loop):
                with sp.Fori(0, NE) as e:
                    wg = moe_w_gate[0, bass.ds(e, 1)].rearrange("a d f -> (a d) f")
                    wu = moe_w_up[0, bass.ds(e, 1)].rearrange("a d f -> (a d) f")
                    wd = moe_w_down[0, bass.ds(e, 1)].rearrange("a f d -> (a f) d")
                    done = first_loop + EG * e
                    gate_up(MOE0, wg, wu, 0, done)
                    with sp.Fori(0, EG - 1) as g:
                        gate_up(MOE0 + GU_UNITS, wg, wu, (g + 1) * BANK, done + g)
                        down(MOE0 + 2 * GU_UNITS, wd, g * BANK, done + g)
                    down(MOE0 + GU_UNITS, wd, (EG - 1) * BANK, done + EG - 1, chunks=2)
                    sp.wait_ge(lo_ready, MOE0 + GU_UNITS + 2 - NRAW + 1 + BODY * (done + EG - 1))
                    sp.dma_start(passed[:, bass.ds(e, 1)], moe_router[0, 0:1, 0:1]
                                 ).then_inc(raw_arrived[HELD % NRAW], 16)
                    down(MOE0 + GU_UNITS + 3, wd, (EG - 1) * BANK + 3 * P, done + EG - 1, chunks=1)
                sp.wait_ge(raw_arrived[HELD % NRAW], 16 * (HELD // NRAW + 1 + EG * (NE - 1) + first_loop))

            experts(0)
            sp.wait_ge(n_exp_ready, 1)
            n = sp.value_load(n_exp[0:1, 0:1], min_val=NE, max_val=2 * NE)
            with sp.If(n > NE):
                experts(EG * NE)
            for t in range(T):
                for half in range(2):
                    sp.wait_ge(h_updated, 8 * DEPTH - 2 * (T - t) + half + 1)
                    c = slice(half * BANK, (half + 1) * BANK)
                    sp.dma_start(out[0, t * P:(t + 1) * P, c], h[:, t, c]).then_inc(out_stored, 16)
            sp.wait_ge(out_stored, 16 * 2 * T)

        @block.gpsimd
        def _(pool):
            steps = [0]

            def link(ins):
                steps[0] += 1
                ins.then_inc(pool_step, 1)
                pool.wait_ge(pool_step, steps[0])

            def gain(dst, rows, loaded):
                for n, row in enumerate(rows):
                    width = row.shape[-1]
                    pool.dma_start(dst[:, n * width:(n + 1) * width],
                                   row.to_broadcast([P, width])).then_inc(loaded, 16)

            def load_held(e):
                pool.dma_start(mixers[:, e * UW:(e + 1) * UW],
                               moe_w_down[0, e, HELD_CHUNK * P:(HELD_CHUNK + 1) * P, :]).then_inc(held_arrived, 16)

            def gating_weights(layer):
                pool.dma_start(ws_raw, sgu_w[layer].rearrange("g t s -> t g s")).then_inc(ws_loaded, 16)
                pool.dma_start(sb_rows[:, :], sgu_b[layer]).then_inc(sb_loaded, 16)
                pool.wait_ge(ws_loaded, 16 * (layer + 1))
                nc.gpsimd.affine_select(out=ws_raw, in_=ws_raw, compare_op=ALU.is_ge, fill=0.0, base=0,
                                        pattern=[[0, NG], [-1, P]], channel_multiplier=1).then_inc(ws_masked, 1)

            nc.gpsimd.memset(eps[:, :], EPS)
            link(nc.gpsimd.memset(ident[:, :], 0.0))
            nc.gpsimd.affine_select(out=ident[:, :], in_=ident[:, :], compare_op=ALU.not_equal, fill=1.0, base=0,
                                    pattern=[[-1, P]], channel_multiplier=1).then_inc(ident_ready, 1)
            with nc.allow_non_contiguous_dma(reason="256 positions, one per partition"):
                pool.dma_start(pos_i[:, :], positions.rearrange("o (t p) -> p (o t)", p=P)).then_inc(small_loaded, 16)
            pool.dma_start(sinks[:, :, :].rearrange("p l h -> p (l h)"),
                           attn_sinks.rearrange("l h -> (l h)").unsqueeze(0).to_broadcast([P, DEPTH * NQ])
                           ).then_inc(small_loaded, 16)
            pool.dma_start(wr[:, :, :], stacked(moe_router[0])).then_inc(small_loaded, 16)
            nc.gpsimd.memset(half_pi[:, :], float(np.pi / 2))
            for j in range(HALF):
                f = np.power(np.float32(THETA), -np.float32(2 * j) / np.float32(ROPE_DIM), dtype=np.float32)
                nc.gpsimd.memset(inv_freq[:, j:j + 1], float(f))
            nc.gpsimd.memset(ones[:, :], 1.0)
            nc.gpsimd.memset(upper[:, :], 1.0)
            nc.gpsimd.iota(iota_i[:, :], pattern=[[1, P]], base=0, channel_multiplier=0)
            link(nc.gpsimd.memset(mask[:, :], 0.0))
            nc.gpsimd.affine_select(out=upper[:, :], in_=upper[:, :], compare_op=ALU.is_ge, fill=0.0, base=0,
                                    pattern=[[1, P]], channel_multiplier=-1)
            nc.gpsimd.affine_select(out=mask[:, 0:P], in_=mask[:, 0:P], compare_op=ALU.is_ge, fill=NEG, base=-1,
                                    pattern=[[1, P]], channel_multiplier=-1)
            nc.gpsimd.affine_select(out=mask[:, P:2 * P], in_=mask[:, P:2 * P], compare_op=ALU.is_ge, fill=NEG,
                                    base=0, pattern=[[-1, P]], channel_multiplier=1).then_inc(consts_ready, 1)
            gating_weights(0)
            pool.wait_ge(hi_ready, NRAW)
            gain(g_ln[:, :, :].rearrange("p a c -> p (a c)"), [sgu_ln_g[0:1, :], sgu_ln_b[0:1, :]], ln_loaded)
            gain(g_out, [attn_out_norm[0:1, :], sgu_out_norm[0:1, :]], out_loaded)
            gain(g_post, [post_mix_norm[0:1, :]], post_loaded)
            for layer in range(DEPTH):
                pool.wait_ge(tok_ready, N_TURNS * layer + ATTN_HALF)
                gain(g_pre, [pre_ffn_norm[layer:layer + 1, :]], pre_loaded)
                if layer + 1 < DEPTH:
                    nxt = slice(layer + 1, layer + 2)
                    pool.wait_ge(vn_ready, layer + 1)
                    gain(g_ln[:, :, :].rearrange("p a c -> p (a c)"), [sgu_ln_g[nxt, :], sgu_ln_b[nxt, :]], ln_loaded)
                    pool.wait_ge(sgu_ready, 2 * (layer + 1))
                    gating_weights(layer + 1)
                    pool.wait_ge(tok_ready, N_TURNS * layer + PRE_FFN)
                    gain(g_out, [attn_out_norm[nxt, :], sgu_out_norm[nxt, :]], out_loaded)
                else:
                    pool.wait_ge(scores_done, 6 * DEPTH)
                    load_held(6)
                    load_held(7)
                    pool.wait_ge(vn_ready, DEPTH)
                    load_held(2)
                    pool.wait_ge(sgu_done, 2 * DEPTH)
                    load_held(0)
                    load_held(1)
                    pool.wait_ge(sgu_ready, 2 * DEPTH)
                    load_held(3)
                    pool.wait_ge(tok_ready, N_TURNS * layer + PRE_FFN)
                    load_held(4)
                pool.wait_ge(h_updated, 8 * layer + 4)
                gain(g_post, [post_ffn_norm[layer:layer + 1, :]], post_loaded)
                if layer + 1 < DEPTH:
                    pool.wait_ge(tok_ready, N_TURNS * (layer + 1))
                    gain(g_pre, [pre_mix_norm[nxt, :]], pre_loaded)
                    pool.wait_ge(h_updated, 8 * layer + 8)
                    gain(g_post, [post_mix_norm[nxt, :]], post_loaded)
                else:
                    pool.wait_ge(tok_ready, N_TURNS * DEPTH)
                    load_held(5)

        @block.scalar
        def _(act):
            steps = [0]
            A = nc.scalar.activation

            def link(ins):
                steps[0] += 1
                ins.then_inc(act_step, 1)
                act.wait_ge(act_step, steps[0])

            def split(m, loops=0):
                act.wait_ge(raw_arrived[m % NRAW], 16 * (m // NRAW + 1) + 16 * loops)
                if m >= NSPL:
                    act.wait_ge(unit_used, m - NSPL + 1 + BODY * loops)
                A(w_hi[:, m % NSPL, :], raw[:, m % NRAW, :], ACT.Copy).then_inc(hi_ready, 1)

            def splits(a, b, loops=0):
                for m in range(a, b):
                    split(m, loops)

            def split_held(e):
                act.wait_ge(held_arrived, 16 * NE)
                act.wait_ge(unit_used, HELD - NSPL + 1 + EXPERT_UNITS * e)
                A(w_hi[:, HELD % NSPL, :], mixers[:, bass.ds(e % NE * UW, UW)], ACT.Copy).then_inc(hi_ready, 1)

            def square(col, src, width, sq=sq):
                if steps[0]:
                    act.wait_ge(act_step, steps[0])
                A(sq[:, 0:width], src, ACT.Square, accum_out=ssq[:, col:col + 1]).then_inc(act_step, 1)
                steps[0] += 1

            def root(col, n, width):
                act.wait_ge(act_step, steps[0])
                A(std[:, col:col + n], ssq[:, col:col + n], ACT.Sqrt, bias=eps[:, :],
                  scale=1.0 / width).then_inc(std_ready, 1)

            def act_high(layer, first, n):
                for i in range(first, first + n):
                    bank, chunks, t = TURNS[i]
                    act.wait_ge(tok_turned, N_TURNS * layer + i + 1)
                    A(act_hi[:, chunks, t * P:(t + 1) * P], ps[:, bank, :].rearrange("p (k t) -> p k t", k=4),
                      ACT.Copy).then_inc(act_hi_ready, 1)

            def entry_squares(layer, first, t):
                if layer or first:
                    act.wait_ge(h_updated, 8 * layer - (0 if first else 4) + 2 * t + 2)
                else:
                    act.wait_ge(x_loaded[t], 16)
                square(PRE + t, h[:, t, :], D)

            def entry(layer, first, m, early, source):
                source(0)
                if early:
                    splits(m + early, m + 3)
                    act_high(layer, first, 2)
                else:
                    splits(m, m + 2)
                    act_high(layer, first, 2)
                    split(m + 2)
                source(1)
                split(m + 3)
                act_high(layer, first + 2, 2)
                splits(m + 4, m + 6)
                for t in range(T):
                    entry_squares(layer, first, t)
                root(PRE, T, D)

            def load_root_table():
                link(A(half_ssq[:, 0, 2:3], eps[:, :], ACT.Sqrt))

            def post_squares(k, t, halves, left_units=None, units=None):
                act.wait_ge(act_step, steps[0])
                for half, src in enumerate(halves):
                    before = 2 * T * k + 2 * t + half
                    if before:
                        act.wait_ge(half_squared, before)
                    if units is not None:
                        act.wait_ge(unit_used, units if half else left_units)
                    A(sq[:, 0:BANK], src, ACT.Square, accum_out=half_ssq[:, t, half:half + 1]).then_inc(half_squared, 1)
                    if half == 0:
                        act.wait_ge(half_squared, before + 1)
                        link(A(half_ssq[:, t, 2:3], half_ssq[:, t, 0:1], ACT.Identity, bias=eps[:, :], scale=1.0 / D))
                act.wait_ge(half_squared, 2 * T * k + 2 * t + 2)
                A(std[:, POST + t:POST + t + 1], half_ssq[:, t, 1:2], ACT.Sqrt, bias=half_ssq[:, t, 2:3],
                  scale=1.0 / D).then_inc(std_ready, 1)

            def mixer(layer, m):
                if layer == 0:
                    entry_squares(0, PRE_MIX, 0)
                    for i in range(2):
                        split(m + i)
                        act_high(0, PRE_MIX + i, 1)
                    entry_squares(0, PRE_MIX, 1)
                    splits(m + 2, m + 4)
                    act_high(0, PRE_MIX + 2, 2)
                    splits(m + 4, m + 6)
                    root(PRE, T, D)
                else:
                    entry(layer, PRE_MIX, m, 0, dense_squares)
                if layer == 0:
                    act.wait_ge(angle_ready, 1)
                    A(sin[:, :, :], ang[:, :, :], ACT.Sin).then_inc(sincos_ready, 1)
                    A(cos[:, :, :], turns[:, :, :], ACT.Sin, scale=-1.0, bias=half_pi[:, :]).then_inc(sincos_ready, 1)
                    act.wait_ge(small_loaded, 48)
                    A(wr_split[:, :, 0, :], wr[:, :, :], ACT.Copy).then_inc(router_rounded, 1)
                splits(m + 6, m + 10)
                act.wait_ge(rstd_ready, 2 * layer + 1)
                act.wait_ge(unit_used, m + 4)
                for t in range(T):
                    A(qk[:, t, 0:NQ, :].rearrange("p (i j) d -> p j i d", j=NKV),
                      ps[:, 4 + t, :].rearrange("p (j i d) -> p j i d", j=NKV, i=QPK), ACT.Identity,
                      scale=q_scale[:, t:t + 1]).then_inc(qkv_copied, 1)
                splits(m + 10, m + 12)
                act.wait_ge(unit_used, m + 6)
                for t in range(T):
                    scale = rstd[:, PRE + t:PRE + t + 1]
                    A(qk[:, t, NQ:, :].rearrange("p j d -> p (j d)"), ps[:, 6 + t, 0:KVW], ACT.Identity,
                      scale=scale).then_inc(qkv_copied, 1)
                    A(vv[:, t, :], ps[:, 6 + t, KVW:2 * KVW], ACT.Identity, scale=scale).then_inc(qkv_copied, 1)
                splits(m + 12, m + 15)
                for b in (0, 2):
                    act.wait_ge(qk_turned, 3 * layer + b + 1)
                    n = 2 if b == 0 else 1
                    A(qk_t[:, 2 * b:2 * b + n, :], ps[:, 4 + b, 0:n * S].rearrange("p (k t) -> p k t", k=n),
                      ACT.Copy).then_inc(qk_t_act, 1)
                act.wait_ge(unit_used, m + 10)
                for t in range(T):
                    A(vg[:, t, :], ps[:, 2 + t, :], ACT.Gelu_apprx_tanh,
                      scale=rstd[:, PRE + t:PRE + t + 1]).then_inc(gelu_done, 1)
                split(m + 15)
                for t in range(T):
                    act.wait_ge(max_ready, T * layer + t + 1)
                    for hh in range(NQ):
                        A(sc[t][:, hh, :], sc[t][:, hh, :], ACT.Exp, bias=nmx[:, t, hh:hh + 1],
                          accum_out=rsum[:, t, hh:hh + 1]).then_inc(probs_ready, 1)
                A(sink_e[:, :, :], sink_d[:, :, :], ACT.Exp).then_inc(sink_ready, 1)
                act.wait_ge(var_ready, layer + 1)
                A(ln_std[:, :], ln_var[:, :], ACT.Sqrt, bias=eps[:, :], scale=1.0 / GD).then_inc(ln_std_ready, 1)
                for b, bank in enumerate(PROB_BANKS):
                    act.wait_ge(probs_turned, 6 * layer + b + 1)
                    A(pt[:, 4 * b:4 * b + 4, :], ps[:, bank, :].rearrange("p (n q) -> p n q", n=4),
                      ACT.Copy).then_inc(pt_ready, 1)
                for t in range(T):
                    act.wait_ge(attn_ready, T * layer + t + 1)
                    square(ATTN + t, tok[:, t, 0:AW], AW, sq_mix)
                root(ATTN, T, AW)
                split(m + 16)
                act_high(layer, ATTN_HALF, 2)
                split(m + 17)
                act.wait_ge(unit_used, m + 14)
                for t in range(T):
                    A(ug[:, t, :], ps[:, 2 + t, :], ACT.Gelu_apprx_tanh,
                      scale=rstd[:, PRE + t:PRE + t + 1]).then_inc(gelu_done, 1)
                splits(m + 18, m + 20)
                act.wait_ge(sgu_ready, 2 * (layer + 1))
                for t in range(T):
                    square(SGU + t, tok[:, t, AW:], SW, sq_mix)
                root(SGU, T, SW)
                act_high(layer, SGU_HALF, 2)
                splits(m + 20, m + 24)

                def mixed_squares(t):
                    if t == 0:
                        act.wait_ge(first_tile_done, 1 + 2 * layer)
                        post_squares(2 * layer, t, mixed(t))
                    else:
                        post_squares(2 * layer, t, mixed(t), m + MIX_UNITS - 2, m + MIX_UNITS)

                if layer == 0:
                    entry(layer, PRE_FFN, m + MIX_UNITS, 2, mixed_squares)
                else:
                    mixed_squares(0)
                    act_high(1, PRE_FFN, 1)
                    entry_squares(1, PRE_FFN, 0)
                    mixed_squares(1)
                    act_high(1, PRE_FFN + 1, 2)
                    entry_squares(1, PRE_FFN, 1)
                    act_high(1, PRE_FFN + 3, 1)
                    root(PRE, T, D)

            def dense_squares(t):
                act.wait_ge(part_added, 2 + DENSE_PARTS - 2 * (T - 1 - t))
                post_squares(1, t, summed(t))

            def silu(units, tiles, width=BANK, scaled=True):
                act.wait_ge(unit_used, units)
                for t in range(tiles):
                    scale = rstd[:, PRE + t:PRE + t + 1] if scaled else 1.0
                    A(sil[:, t, 0:width], ps[:, 2 * t, 0:width], ACT.Silu, scale=scale).then_inc(sil_ready, 1)

            def turned(n, tiles, chunks=4, dst=ht_hi):
                for t in range(tiles):
                    act.wait_ge(hid_turned, n + t + 1)
                    A(dst[:, 0:chunks, t, :], ps[:, 6 + t, 0:chunks * P].rearrange("p (c j) -> p c j", c=chunks),
                      ACT.Copy).then_inc(ht_hi_ready, 1)

            act.wait_ge(ident_ready, 1)
            mixer(0, 0)

            m = DENSE0
            splits(m + 6, m + 10)
            act.wait_ge(rstd_ready, 2)
            silu(m + 4, T)
            splits(m + 10, m + 14)
            turned(0, T)
            m = DENSE0 + GU_UNITS
            with act.Fori(0, DG - 1) as g:
                splits(m + 6, m + 14, g)
                silu(m + 8 + BODY * g, T)
                splits(m + 14, m + 16, g)
                turned(T * (g + 1), T)
                splits(m + 16, m + 18, g)
            m += BODY * (DG - 1)
            splits(m + 6, m + 10)
            silu(m + 4, T, BANK // 2)
            turned(T * DG, T, 2, late_hi)
            load_root_table()

            mixer(1, MIX1)

            split(MOE0 + 2)
            act.wait_ge(lg_parts_done, 1)
            A(lg_parts, ps[0:2 * NE, 6, 0:S], ACT.Copy).then_inc(lg_parts_ready, 1)
            splits(MOE0 + 3, MOE0 + 5)

            def gathered_high(b, count):
                act.wait_ge(gathered, count)
                A(xe_hi[:, 4 * b:4 * b + 4, :], ps[:, (7, 2)[b], :].rearrange("p (k j) -> p k j", k=4),
                  ACT.Copy).then_inc(xe_hi_ready, 1)

            def output(e):
                act.wait_ge(unit_used, MOE0 + EXPERT_UNITS * e)
                A(y[:, 0:BANK], ps[:, 4, :], ACT.Copy).then_inc(y_act, 1)

            act.wait_ge(top_ready, 1)
            A(e2[:, :], e2[:, :], ACT.Exp).then_inc(e2_ready, 1)
            split(MOE0 + 5)
            for b in range(2):
                gathered_high(b, b + 1)
            act.wait_ge(n_exp_ready, 1)
            n = act.value_load(n_exp[0:1, 0:1], min_val=NE, max_val=2 * NE)
            with act.Fori(0, n) as e:
                done = EG * e
                with act.If(e > 0):
                    splits(MOE0, MOE0 + 4, done)
                    output(e)
                    splits(MOE0 + 4, MOE0 + 6, done)
                splits(MOE0 + 6, MOE0 + 12, done)
                silu(MOE0 + 8 + BODY * done, 1, scaled=False)
                splits(MOE0 + 12, MOE0 + 14, done)
                turned(DENSE_TILES + done, 1)
                m = MOE0 + GU_UNITS
                with act.Fori(0, EG - 2) as g:
                    splits(m + 6, m + 13, done + g)
                    silu(m + 8 + BODY * (done + g), 1, scaled=False)
                    splits(m + 13, m + 18, done + g)
                    turned(DENSE_TILES + done + g + 1, 1)
                last = done + EG - 2
                splits(m + 6, m + 13, last)
                silu(m + 8 + BODY * last, 1, scaled=False)
                split(m + 13, last)
                turned(DENSE_TILES + last + 1, 1)
                split_held(e)
                split(m + 15, last)
                with act.If(e < n - 1):
                    for b in range(2):
                        gathered_high(b, 3 * e + b + 4)
            output(n)
            load_root_table()
            for t in range(T):
                act.wait_ge(part_added, ADDED0 + 4 * n - 2 * (T - 1 - t))
                post_squares(3, t, summed(t))

        @block.vector
        def _(dve):
            steps = [0]
            V = nc.vector

            def link(ins):
                steps[0] += 1
                ins.then_inc(dve_step, 1)
                dve.wait_ge(dve_step, steps[0])

            def split(m, loops=0):
                dve.wait_ge(hi_ready, m + 1 + BODY * loops)
                V.tensor_tensor(w_lo[:, m % NSPL, :], raw[:, m % NRAW, :], w_hi[:, m % NSPL, :].bitcast(F32),
                                ALU.subtract).then_inc(lo_ready, 1)

            def splits(a, b, loops=0):
                for m in range(a, b):
                    split(m, loops)

            def split_held(e):
                dve.wait_ge(hi_ready, HELD + 1 + EXPERT_UNITS * e)
                V.tensor_tensor(w_lo[:, HELD % NSPL, :], mixers[:, bass.ds(e % NE * UW, UW)],
                                w_hi[:, HELD % NSPL, :].bitcast(F32), ALU.subtract).then_inc(lo_ready, 1)

            stds = [0]

            def inverse(col, n):
                stds[0] += 1
                dve.wait_ge(std_ready, stds[0])
                link(V.reciprocal(rstd[:, col:col + n], std[:, col:col + n]))

            def act_low(layer, first, n):
                for i in range(first, first + n):
                    bank, chunks, t = TURNS[i]
                    tt = slice(t * P, (t + 1) * P)
                    dve.wait_ge(act_hi_ready, N_TURNS * layer + i + 1)
                    V.tensor_tensor(act_lo[:, chunks, tt], ps[:, bank, :].rearrange("p (k t) -> p k t", k=4),
                                    act_hi[:, chunks, tt].bitcast(F32), ALU.subtract).then_inc(act_lo_ready, 1)

            def gained(t, half):
                c = slice(half * BANK, (half + 1) * BANK)
                V.tensor_tensor(tok[:, t, c], h[:, t, c], g_pre[:, c], ALU.mult).then_inc(tok_ready, 1)

            def post(k, t, halves):
                dve.wait_ge(post_loaded, 16 * (k + 1))
                for half, src in enumerate(halves):
                    c = slice(half * BANK, (half + 1) * BANK)
                    dve.wait_ge(half_squared, 2 * T * k + 2 * t + half + 1)
                    ins = V.tensor_tensor(tok[:, t, c], src, g_post[:, c], ALU.mult)
                link(ins)
                inverse(POST + t, 1)
                for half in range(2):
                    c = slice(half * BANK, (half + 1) * BANK)
                    V.scalar_tensor_tensor(out=h[:, t, c], in0=tok[:, t, c], scalar=rstd[:, POST + t:POST + t + 1],
                                           in1=h[:, t, c], op0=ALU.mult, op1=ALU.add).then_inc(h_updated, 1)
                    if k < 2 * DEPTH - 1:
                        dve.wait_ge(h_updated, 2 * (T * k + t) + half + 1)
                        dve.wait_ge(pre_loaded, 16 * (k + 1))
                        gained(t, half)

            def entry(layer, first, m, early, source):
                source(0)
                if early:
                    splits(m + early, m + 3)
                    act_low(layer, first, 2)
                else:
                    for i in range(2):
                        split(m + i)
                        act_low(layer, first + i, 1)
                    split(m + 2)
                source(1)
                split(m + 3)
                act_low(layer, first + 2, 2)
                splits(m + 4, m + 6)
                scales()

            def scales():
                inverse(PRE, T)
                V.tensor_scalar(q_scale[:, :], rstd[:, PRE:PRE + T], HD ** -0.5, None, ALU.mult).then_inc(rstd_ready, 1)

            def rope(layer):
                dve.wait_ge(qkv_copied, 3 * T * (layer + 1))
                H = NQ + NKV
                a, b = qk[:, :, :, 0:HALF], qk[:, :, :, HALF:2 * HALF]

                def bc(f):
                    return f[:, :, :].unsqueeze(2).to_broadcast([P, T, H, HALF])
                for t in range(T):
                    a, b = qk[:, t, :, 0:HALF], qk[:, t, :, HALF:2 * HALF]
                    c = cos[:, t, :].unsqueeze(1).to_broadcast([P, H, HALF])
                    s = sin[:, t, :].unsqueeze(1).to_broadcast([P, H, HALF])
                    V.tensor_tensor(rot[:, 0, t], a, c, ALU.mult)
                    V.tensor_tensor(rot[:, 1, t], b, s, ALU.mult)
                    V.tensor_tensor(rot[:, 2, t], b, c, ALU.mult)
                    link(V.tensor_tensor(rot[:, 3, t], a, s, ALU.mult))
                    V.tensor_tensor(a, rot[:, 0, t], rot[:, 1, t], ALU.subtract)
                    V.tensor_tensor(b, rot[:, 2, t], rot[:, 3, t], ALU.add).then_inc(qk_roped, 1)

            def mixer(layer, m):
                if layer == 0:
                    for i in range(2):
                        split(m + i)
                        act_low(0, PRE_MIX + i, 1)
                    dve.wait_ge(x_loaded[1], 16)
                    for half in range(2):
                        gained(1, half)
                    splits(m + 2, m + 4)
                    act_low(0, PRE_MIX + 2, 2)
                    splits(m + 4, m + 6)
                    scales()
                else:
                    entry(layer, PRE_MIX, m, 0, dense_sum)
                if layer == 0:
                    angles()
                splits(m + 6, m + 10)
                dve.wait_ge(ws_turned, 3 * layer + 1)
                V.tensor_copy(sb_t[:, :], ps[:, 2, 0:NG]).then_inc(ws_copied, 1)
                for b in range(2):
                    dve.wait_ge(ws_turned, 3 * layer + b + 2)
                    V.tensor_copy(ws_t[:, 4 * b:4 * b + 4, :],
                                  ps[:, b, :].rearrange("p (g t) -> p g t", g=4)).then_inc(ws_copied, 1)
                splits(m + 10, m + 12)
                if layer == 0:
                    dve.wait_ge(sincos_ready, 2)
                rope(layer)
                if layer == 0:
                    dve.wait_ge(router_rounded, 1)
                    V.tensor_tensor(wr_split[:, :, 1, :], wr[:, :, :], wr_split[:, :, 0, :].bitcast(F32), ALU.subtract
                                    ).then_inc(router_split, 1)
                splits(m + 12, m + 15)
                dve.wait_ge(qk_turned, 3 * layer + 2)
                V.tensor_copy(qk_t[:, 2:4, :], ps[:, 5, :].rearrange("p (k t) -> p k t", k=2)).then_inc(qk_t_dve, 1)
                split(m + 15)
                for t in range(T):
                    keys = (t + 1) * P
                    per = BANK // keys
                    own = mask[:, (T - 1 - t) * P:].unsqueeze(1).to_broadcast([P, per, keys])
                    for b in range(NQ // per):
                        dve.wait_ge(scores_done, 6 * layer + 2 * t + b + 1)
                        ins = V.tensor_tensor(sc[t][:, per * b:per * (b + 1), :],
                                              ps[:, PROB_BANKS[2 * t + b], :].rearrange("p (h k) -> p h k", h=per),
                                              own, ALU.add)
                    link(ins)
                    link(V.tensor_reduce(mx[:, t, :], sc[t], AX.X, ALU.max))
                    link(V.tensor_tensor(mx[:, t, :], mx[:, t, :], sinks[:, layer, :], ALU.max))
                    link(V.tensor_tensor(sink_d[:, t, :], sinks[:, layer, :], mx[:, t, :], ALU.subtract))
                    V.tensor_scalar(nmx[:, t, :], mx[:, t, :], -1.0, None, ALU.mult).then_inc(max_ready, 1)
                dve.wait_ge(gelu_done, 4 * layer + 2)
                v3 = vg[:, :, :].rearrange("p t (g d) -> p (t g) d", g=NG)
                for t in range(T):
                    vt = vg[:, t, :].rearrange("p (g d) -> p g d", g=NG)
                    ins = V.tensor_reduce(ln_mu[:, t * NG:(t + 1) * NG], vt, AX.X, ALU.add)
                link(ins)
                link(V.tensor_scalar(ln_mu[:, :], ln_mu[:, :], 1.0 / GD, None, ALU.mult))
                link(V.tensor_tensor(v3, v3, ln_mu[:, :].unsqueeze(2).to_broadcast([P, T * NG, GD]), ALU.subtract))
                link(V.tensor_tensor(ln_sq, vg[:, :, :], vg[:, :, :], ALU.mult))
                for t in range(T):
                    ins = V.tensor_reduce(ln_var[:, t * NG:(t + 1) * NG],
                                          ln_sq[:, t, :].rearrange("p (g d) -> p g d", g=NG), AX.X, ALU.add)
                ins.then_inc(var_ready, 1)
                dve.wait_ge(ln_std_ready, layer + 1)
                link(V.reciprocal(ln_std[:, :], ln_std[:, :]))
                link(V.tensor_tensor(v3, v3, ln_std[:, :].unsqueeze(2).to_broadcast([P, T * NG, GD]), ALU.mult))
                dve.wait_ge(ln_loaded, 32 * (layer + 1))
                link(V.tensor_tensor(vg[:, :, :], vg[:, :, :], g_ln[:, 0:1, :].to_broadcast([P, T, SW]), ALU.mult))
                V.tensor_tensor(vg[:, :, :], vg[:, :, :], g_ln[:, 1:2, :].to_broadcast([P, T, SW]),
                                ALU.add).then_inc(vn_ready, 1)
                dve.wait_ge(sink_ready, layer + 1)
                link(V.tensor_tensor(rsum[:, :, :], rsum[:, :, :], sink_e[:, :, :], ALU.add))
                link(V.reciprocal(rinv[:, :, :], rsum[:, :, :]))
                for t in range(T):
                    dve.wait_ge(pv_done, T * layer + t + 1)
                    V.tensor_tensor(tok[:, t, 0:AW].rearrange("p (h d) -> p h d", h=NQ),
                                    ps[:, 4 + t, :].rearrange("p (h d) -> p h d", h=NQ),
                                    rinv[:, t, :].unsqueeze(2).to_broadcast([P, NQ, HD]), ALU.mult
                                    ).then_inc(attn_ready, 1)

                def out_norm(col, c0, loaded):
                    dve.wait_ge(out_loaded, 32 * (layer + 1))
                    inverse(col, T)
                    for t in range(T):
                        V.scalar_tensor_tensor(out=tok[:, t, c0:c0 + AW], in0=tok[:, t, c0:c0 + AW],
                                               scalar=rstd[:, col + t:col + t + 1], in1=g_out[:, c0:c0 + AW],
                                               op0=ALU.mult, op1=ALU.mult).then_inc(tok_ready, 1)

                dve.wait_ge(attn_ready, T * (layer + 1))
                out_norm(ATTN, 0, 1)
                act_low(layer, ATTN_HALF, 1)
                split(m + 16)
                act_low(layer, ATTN_HALF + 1, 1)
                split(m + 17)
                dve.wait_ge(gelu_done, 4 * (layer + 1))
                for b in range(2):
                    dve.wait_ge(sgu_done, 2 * layer + b + 1)
                    for i in range(4):
                        g = 4 * b + i
                        ins = V.scalar_tensor_tensor(
                            out=tok[:, :, AW + g * GD:AW + (g + 1) * GD],
                            in0=ps[:, b, i * P:(i + 1) * P].rearrange("p (t d) -> p t d", t=T),
                            scalar=sb_t[:, g:g + 1], in1=ug[:, :, g * GD:(g + 1) * GD], op0=ALU.add, op1=ALU.mult)
                    ins.then_inc(sgu_ready, 1)
                splits(m + 18, m + 20)
                dve.wait_ge(sgu_ready, 2 * (layer + 1))
                out_norm(SGU, AW, 2)
                clear_sums()
                act_low(layer, SGU_HALF, 2)
                splits(m + 20, m + 24)

                def mixed_post(t):
                    if t == 0:
                        dve.wait_ge(first_tile_done, 1 + 2 * layer)
                    post(2 * layer, t, mixed(t))

                if layer == 0:
                    entry(layer, PRE_FFN, m + MIX_UNITS, 2, mixed_post)
                else:
                    mixed_post(0)
                    act_low(1, PRE_FFN, 1)
                    mixed_post(1)
                    act_low(1, PRE_FFN + 1, 3)

            def hidden(n, tiles, width=BANK, scaled=True):
                for t in tiles:
                    dve.wait_ge(sil_ready, n + t + 1)
                    up = ps[:, 2 * t + 1, 0:width]
                    if scaled:
                        V.scalar_tensor_tensor(out=hid[:, t, 0:width], in0=up, scalar=rstd[:, PRE + t:PRE + t + 1],
                                               in1=sil[:, t, 0:width], op0=ALU.mult, op1=ALU.mult
                                               ).then_inc(hid_ready, 1)
                    else:
                        V.tensor_tensor(hid[:, t, 0:width], sil[:, t, 0:width], up, ALU.mult).then_inc(hid_ready, 1)

            def turned(n, tiles, chunks=4, hi=ht_hi, lo=ht_lo):
                for t in range(tiles):
                    dve.wait_ge(ht_hi_ready, n + t + 1)
                    V.tensor_tensor(lo[:, 0:chunks, t, :],
                                    ps[:, 6 + t, 0:chunks * P].rearrange("p (c j) -> p c j", c=chunks),
                                    hi[:, 0:chunks, t, :].bitcast(F32), ALU.subtract).then_inc(ht_lo_ready, 1)

            def add_parts(n, banks, units=None, tiles=range(T)):
                for t in tiles:
                    for half in range(2):
                        if units is not None and (t, half) == (T - 1, 1):
                            dve.wait_ge(unit_used, units)
                        else:
                            dve.wait_ge(part_done, n + 2 * t + half + 1)
                        cols = slice(half * BANK, (half + 1) * BANK)
                        bank = banks[(2 * t + half) % len(banks)]
                        V.tensor_tensor(facc[:, t, cols], facc[:, t, cols], ps[:, bank, :],
                                        ALU.add).then_inc(part_added, 1)

            def dense_sum(t):
                if t == 0:
                    add_parts(3 * (DG - 1), (4, 5), None, (0,))
                else:
                    dve.wait_ge(unit_used, MIX1)
                    for half in range(2):
                        c = slice(half * BANK, (half + 1) * BANK)
                        V.tensor_tensor(facc[:, t, c], facc[:, t, c], ps[:, 6 + half, :],
                                        ALU.add).then_inc(part_added, 1)
                dve.wait_ge(part_added, 2 + DENSE_PARTS - 2 * (T - 1 - t))
                post(1, t, summed(t))

            def clear_sums():
                for t in range(T):
                    V.memset(facc[:, t, :], 0.0).then_inc(part_added, 1)

            def angles():
                dve.wait_ge(consts_ready, 1)
                dve.wait_ge(small_loaded, 48)
                V.tensor_tensor(fold[:, :], ident[0:2 * NE, 0:NE], ident[0:2 * NE, NE:2 * NE], ALU.add)
                V.tensor_copy(iota[:, :], iota_i[:, :])
                link(V.tensor_copy(pos[:, :], pos_i[:, :]))
                for t in range(T):
                    ins = V.tensor_scalar(ang[:, t, :], inv_freq[:, :], pos[:, t:t + 1], None, ALU.mult)
                link(ins)
                big = 1.5 * 2 ** 23
                link(V.tensor_scalar(turns[:, :, :], ang[:, :, :], 1 / (2 * np.pi), big, ALU.mult, ALU.add))
                link(V.tensor_scalar(turns[:, :, :], turns[:, :, :], -big, None, ALU.add))
                c1 = 6.28125
                c2 = float(np.float32(np.round((2 * np.pi - c1) * 2 ** 20) / 2 ** 20))
                for c in (c1, c2, 2 * np.pi - c1 - c2):
                    link(V.scalar_tensor_tensor(out=ang[:, :, :], in0=turns[:, :, :], scalar=-float(c),
                                                in1=ang[:, :, :],
                                                op0=ALU.mult, op1=ALU.add))
                link(V.tensor_scalar(ang[:, :, :], ang[:, :, :], 3.1415925, -3.1415925, ALU.min, ALU.max))
                V.scalar_tensor_tensor(out=turns[:, :, :], in0=ang[:, :, :], scalar=-1.0, in1=ang[:, :, :],
                                       op0=ALU.mult, op1=ALU.max).then_inc(angle_ready, 1)

            dve.wait_ge(first_gain_loaded, 16)
            dve.wait_ge(x_loaded[0], 16)
            for half in range(2):
                gained(0, half)
            dve.wait_ge(ident_ready, 1)
            mixer(0, 0)

            m = DENSE0
            splits(m + 6, m + 10)
            dve.wait_ge(first_tile_done, 2)
            hidden(0, (0,))
            splits(m + 10, m + 12)
            dve.wait_ge(unit_used, m + 8)
            hidden(0, (1,))
            splits(m + 12, m + 14)
            turned(0, T)
            m = DENSE0 + GU_UNITS
            with dve.Fori(0, DG - 1) as g:
                splits(m + 6, m + 14, g)
                hidden(T * (g + 1), range(T))
                add_parts(3 * g, (4, 5), m + BODY * (g + 1))
                splits(m + 14, m + 16, g)
                turned(T * (g + 1), T)
                splits(m + 16, m + 18, g)
            m += BODY * (DG - 1)
            splits(m + 6, m + 10)
            hidden(T * DG, range(T), BANK // 2)
            turned(T * DG, T, 2, late_hi, late_lo)

            mixer(1, MIX1)

            inverse(PRE, T)
            dve.wait_ge(tok_turned, N_TURNS * DEPTH)
            for t in range(T):
                V.tensor_scalar(tok[:, t, :], tok[:, t, :], rstd[:, PRE + t:PRE + t + 1], None,
                                ALU.mult).then_inc(tokens_ready, 1)
            split(MOE0 + 2)
            dve.wait_ge(logits_done, 1)
            for t in range(T):
                ins = V.tensor_scalar(lg[:, t, :], ps[:, 5, t * NE:(t + 1) * NE], rstd[:, PRE + t:PRE + t + 1], None,
                                      ALU.mult)
            link(ins)
            experts_iota = iota[:, 0:NE].unsqueeze(1).to_broadcast([P, T, NE])

            def wide(a):
                return a.unsqueeze(2).to_broadcast([P, T, NE])

            for r in range(2):
                link(V.tensor_reduce(top[:, r, :], lg[:, :, :], AX.X, ALU.max))
                link(V.tensor_tensor(cand[:, :, :], lg[:, :, :], wide(top[:, r, :]), ALU.is_lt))
                link(V.scalar_tensor_tensor(out=cand[:, :, :], in0=cand[:, :, :], scalar=100.0, in1=experts_iota,
                                            op0=ALU.mult, op1=ALU.add))
                link(V.tensor_reduce(at[:, :], cand[:, :, :], AX.X, ALU.min))
                link(V.tensor_tensor(pick[:, r], experts_iota, wide(at[:, :]), ALU.is_equal))
                if r == 0:
                    link(V.scalar_tensor_tensor(out=lg[:, :, :], in0=pick[:, 0], scalar=-3e38, in1=lg[:, :, :],
                                                op0=ALU.mult, op1=ALU.add))
            link(V.tensor_tensor(chosen[:, :, :], pick[:, 0], pick[:, 1], ALU.add))
            V.tensor_tensor(e2[:, :], top[:, 1, :], top[:, 0, :], ALU.subtract).then_inc(top_ready, 1)
            split(MOE0 + 3)
            dve.wait_ge(counts_done, 1)
            link(V.tensor_tensor(rank[:, :, 0:NE], ps[:, 4, 0:T * NE].rearrange("p (t e) -> p t e", t=T),
                                 chosen[:, :, :], ALU.mult))
            link(V.tensor_scalar(rank[:, :, 0:NE], rank[:, :, 0:NE], -1.0, None, ALU.add))
            V.memset(rank[:, :, 2 * NE:], -1.0)
            link(V.tensor_scalar(rank[:, :, NE:2 * NE], rank[:, :, 0:NE], -float(P), None, ALU.add))

            def select(e):
                for t in range(T):
                    V.tensor_scalar(sel[:, t, :], iota[:, :], rank[:, t, bass.ds(e, 1)], None,
                                    ALU.is_equal).then_inc(sel_ready, 1)

            def gathered_low(b, count):
                dve.wait_ge(xe_hi_ready, count)
                c = slice(4 * b, 4 * b + 4)
                V.tensor_tensor(xe_lo[:, c, :], ps[:, (7, 2)[b], :].rearrange("p (k j) -> p k j", k=4),
                                xe_hi[:, c, :].bitcast(F32), ALU.subtract).then_inc(xe_lo_ready, 1)

            def output(e):
                dve.wait_ge(unit_used, MOE0 + EXPERT_UNITS * e)
                V.tensor_copy(y[:, BANK:], ps[:, 5, :]).then_inc(y_dve, 1)

            select(0)
            dve.wait_ge(totals_done, 1)
            link(V.tensor_reduce(cnt[:, :], ps[:, 5, 0:NE], AX.X, ALU.max))
            link(V.tensor_scalar(n_exp_f[:, :], cnt[:, :], P + 0.5, float(NE), ALU.is_gt, ALU.mult))
            link(V.tensor_scalar(n_exp_f[:, :], n_exp_f[:, :], float(NE), None, ALU.add))
            V.tensor_copy(n_exp[:, :], n_exp_f[:, :]).then_inc(n_exp_ready, 1)
            dve.wait_ge(n_exp_ready, 1)
            n = dve.value_load(n_exp[0:1, 0:1], min_val=NE, max_val=2 * NE)
            split(MOE0 + 4)
            dve.wait_ge(e2_ready, 1)
            link(V.tensor_scalar(g12[:, 0, :], e2[:, :], 1.0, None, ALU.add))
            link(V.reciprocal(g12[:, 0, :], g12[:, 0, :]))
            link(V.tensor_tensor(g12[:, 1, :], g12[:, 0, :], e2[:, :], ALU.mult))
            for r in range(2):
                link(V.tensor_tensor(pick[:, r], pick[:, r], wide(g12[:, r, :]), ALU.mult))
            for r in range(2):
                V.tensor_tensor(gate[:, :, r * NE:(r + 1) * NE], pick[:, 0], pick[:, 1], ALU.add)
            for b in range(2):
                gathered_low(b, b + 1)
            split(MOE0 + 5)
            with dve.Fori(0, n) as e:
                done = EG * e
                with dve.If(e > 0):
                    splits(MOE0, MOE0 + 4, done)
                    output(e)
                    splits(MOE0 + 4, MOE0 + 6, done)
                splits(MOE0 + 6, MOE0 + 12, done)
                hidden(DENSE_TILES + done, range(1), scaled=False)
                with dve.If(e > 0):
                    add_parts(DENSE_SIGNALLED + 4 * (e - 1), PART_BANKS)
                splits(MOE0 + 12, MOE0 + 14, done)
                turned(DENSE_TILES + done, 1)
                select(e + 1)
                for t in range(T):
                    V.tensor_scalar(sel_g[:, t, :], iota[:, :], rank[:, t, bass.ds(e, 1)], gate[:, t, bass.ds(e, 1)],
                                    ALU.is_equal, ALU.mult).then_inc(sel_ready, 1)
                m = MOE0 + GU_UNITS
                with dve.Fori(0, EG - 2) as g:
                    splits(m + 6, m + 13, done + g)
                    hidden(DENSE_TILES + done + g + 1, range(1), scaled=False)
                    splits(m + 13, m + 18, done + g)
                    turned(DENSE_TILES + done + g + 1, 1)
                last = done + EG - 2
                splits(m + 6, m + 13, last)
                hidden(DENSE_TILES + last + 1, range(1), scaled=False)
                split(m + 13, last)
                turned(DENSE_TILES + last + 1, 1)
                split_held(e)
                split(m + 15, last)
                dve.wait_ge(gathered, 3 * e + 3)
                V.tensor_copy(sel_t, ps[:, 3, 0:S].rearrange("p (t j) -> p t j", t=T)).then_inc(sel_t_ready, 1)
                with dve.If(e < n - 1):
                    for b in range(2):
                        gathered_low(b, 2 * e + b + 3)
            output(n)
            add_parts(DENSE_SIGNALLED + 4 * (n - 1), PART_BANKS)
            for t in range(T):
                dve.wait_ge(part_added, ADDED0 + 4 * n - 2 * (T - 1 - t))
                post(3, t, summed(t))

        @block.tensor
        def _(pe):
            mm = nc.tensor.matmul

            def product(o, a_hi, a_lo, b_hi, b_lo, first, last):
                mm(o, a_hi, b_hi, start=first, stop=False)
                mm(o, a_lo, b_hi, start=False, stop=False)
                return mm(o, a_hi, b_lo, start=False, stop=last)

            def unit(m, k, loops=0):
                pe.wait_ge(lo_ready, m + 1 + BODY * loops)
                return unit_view(w_hi, m % NSPL, k), unit_view(w_lo, m % NSPL, k)

            def turn(layer, first, n):
                for i in range(first, first + n):
                    bank, chunks, t = TURNS[i]
                    pe.wait_ge(tok_ready, N_TURNS * layer + i + 1)
                    for c in range(4):
                        k = chunks.start + c
                        ins = nc.tensor.transpose(ps[:, bank, c * P:(c + 1) * P], tok[:, t, k * P:(k + 1) * P],
                                                  ident[:, :])
                    ins.then_inc(tok_turned, 1)

            def group(units, k, width, tiles=T, loops=0, a=(act_hi, act_lo), before=None, after=None):
                a_hi, a_lo = a
                for t in range(tiles):
                    tt = slice(t * P, (t + 1) * P)
                    for u, (m, row, bank) in enumerate(units):
                        if before is not None:
                            before(t, u)
                        if t == 0:
                            pe.wait_ge(lo_ready, m + 1 + BODY * loops)
                        hi, lo = unit_view(w_hi, m % NSPL, k), unit_view(w_lo, m % NSPL, k)
                        for i in range(k):
                            r = row + i
                            ins = product(ps[:, bank(t), 0:width], a_hi[:, r, tt], a_lo[:, r, tt],
                                          hi[:, i, :], lo[:, i, :], r == 0, r == KC - 1)
                        if t == tiles - 1:
                            ins.then_inc(unit_used, 1)
                    if after is not None and t < tiles - 1:
                        ins.then_inc(after, 1)

            def columns(m, n, k, bank0, width, before=None):
                group([(m + u, u * k, lambda t: bank0 + t) for u in range(n)], k, width, before=before)

            def entry(layer, first):
                def before(t, u):
                    if (t, u) == (0, 3):
                        turn(layer, first + 2, 2)
                    if u % 2 == 0:
                        pe.wait_ge(act_lo_ready, N_TURNS * layer + first + 2 * t + u // 2 + 1)
                return before

            def mixer(layer, m):
                if layer == 0:
                    turn(layer, PRE_MIX, 2)
                columns(m, 4, 2, 4, BANK, entry(layer, PRE_MIX))
                columns(m + 4, 2, 4, 6, 2 * KVW)
                pe.wait_ge(ws_masked, layer + 1)
                pe.wait_ge(sb_loaded, 16 * (layer + 1))
                nc.tensor.transpose(ps[:, 2, 0:NG], sb_rows[:, :], ident[0:NG, 0:NG]).then_inc(ws_turned, 1)
                for b in range(2):
                    for i in range(4):
                        ins = nc.tensor.transpose(ps[:, b, i * P:(i + 1) * P], ws_raw[:, 4 * b + i, :], ident[:, :])
                    ins.then_inc(ws_turned, 1)
                pe.wait_ge(ws_copied, 3 * layer + 1)
                columns(m + 6, 4, 2, 2, BANK)
                pe.wait_ge(qk_roped, T * (layer + 1))
                for c in range((NQ + NKV) // 2):
                    for t in range(T):
                        ins = nc.tensor.transpose(ps[:, 4 + c // 2, (c % 2) * S + t * P:(c % 2) * S + (t + 1) * P],
                                                  qk[:, t, 2 * c:2 * c + 2, :].rearrange("p j d -> p (j d)"),
                                                  ident[:, :])
                    if c in (1, 3, 4):
                        ins.then_inc(qk_turned, 1)
                pe.wait_ge(qk_t_act, 2 * (layer + 1))
                pe.wait_ge(qk_t_dve, layer + 1)
                pe.wait_ge(ws_copied, 3 * (layer + 1))
                for t in range(T):
                    keys = (t + 1) * P
                    per = BANK // keys
                    for hh in range(NQ):
                        j, i = hh // QPK, hh % QPK
                        rows = slice(HD * j, HD * (j + 1))
                        bank = PROB_BANKS[2 * t + hh // per]
                        ins = mm(ps[:, bank, (hh % per) * keys:(hh % per + 1) * keys],
                                 qk_t[rows, i, t * P:(t + 1) * P], qk_t[rows, QPK, 0:keys], start=True, stop=True)
                        if hh % per == per - 1:
                            ins.then_inc(scores_done, 1)
                pe.wait_ge(gelu_done, 4 * layer + 2)
                columns(m + 10, 4, 2, 2, BANK)
                for b, bank in enumerate(PROB_BANKS):
                    for i in range(4):
                        n = 4 * b + i
                        if n < NQ:
                            pe.wait_ge(probs_ready, T * NQ * layer + n + 1)
                            src = sc[0][:, n, :]
                        else:
                            hh, blk = (n - NQ) // 2, n % 2
                            pe.wait_ge(probs_ready, T * NQ * layer + NQ + hh + 1)
                            src = sc[1][:, hh, blk * P:(blk + 1) * P]
                        ins = nc.tensor.transpose(ps[:, bank, i * P:(i + 1) * P], src, ident[:, :])
                    ins.then_inc(probs_turned, 1)
                for t in range(T):
                    pe.wait_ge(pt_ready, 6 * layer + (2 if t == 0 else 6))
                    for hh in range(NQ):
                        j = hh // QPK
                        for blk in range(t + 1):
                            n = hh if t == 0 else NQ + 2 * hh + blk
                            ins = mm(ps[:, 4 + t, hh * HD:(hh + 1) * HD], pt[:, n, :],
                                     vv[:, blk, j * HD:(j + 1) * HD], start=(blk == 0), stop=(blk == t))
                    ins.then_inc(pv_done, 1)
                pe.wait_ge(vn_ready, layer + 1)
                for g in range(NG):
                    ins = mm(ps[:, g // 4, (g % 4) * P:(g % 4 + 1) * P].rearrange("p (t d) -> p t d", t=T),
                             ws_t[:, g, :], vg[:, :, g * GD:(g + 1) * GD], start=True, stop=True)
                    if g % 4 == 3:
                        ins.then_inc(sgu_done, 1)
                turn(layer, ATTN_HALF, 2)
                for part, first in enumerate((ATTN_HALF, SGU_HALF)):
                    units = [(m + Z_UNITS + u, OUT_ORDER[u][0],
                              lambda t, half=OUT_ORDER[u][1] // BANK: 4 + 2 * t + half)
                             for u in range(4 * part, 4 * part + 4)]

                    def before(t, u):
                        if u == 0:
                            pe.wait_ge(act_lo_ready, N_TURNS * layer + first + t + 1)
                        if part and (t, u) == (T - 1, 3):
                            turn(layer, PRE_FFN, 1)

                    if part:
                        turn(layer, SGU_HALF, 2)
                    group(units, 2, BANK, before=before, after=first_tile_done if part else None)
                turn(layer, PRE_FFN + 1, 1)

            def gate_up(m, a, tiles, loops=0, width=BANK, before=None, after=None):
                k = UW // width
                per = KC // k
                for w in range(2):
                    group([(m + w * per + u, u * k, lambda t, w=w: 2 * t + w) for u in range(per)], k, width, tiles,
                          loops, a, before if w == 0 else None, after if w == 1 else None)

            def turn_hidden(n, tiles, chunks=4):
                for t in range(tiles):
                    pe.wait_ge(hid_ready, n + t + 1)
                    for c in range(chunks):
                        ins = nc.tensor.transpose(ps[:, 6 + t, c * P:(c + 1) * P], hid[:, t, c * P:(c + 1) * P],
                                                  ident[:, :])
                    ins.then_inc(hid_turned, 1)

            def dense_down(m, n, parts, loops=0):
                pe.wait_ge(ht_lo_ready, n)
                hl = [unit(m + c, 1, loops) for c in range(4)]
                for t in range(T):
                    for half in range(2):
                        pe.wait_ge(part_added, parts + 2 * t + half + 1)
                        for c in range(4):
                            cols = slice(half * BANK, (half + 1) * BANK)
                            ins = product(ps[:, 4 + half, :], ht_hi[:, c, t, :], ht_lo[:, c, t, :],
                                          hl[c][0][:, 0, cols], hl[c][1][:, 0, cols], c == 0, c == 3)
                            if (t, half) == (T - 1, 1):
                                ins.then_inc(unit_used, 1)
                        if (t, half) != (T - 1, 1):
                            ins.then_inc(part_done, 1)

            def expert_down(m, n, first, last, loops=0):
                pe.wait_ge(ht_lo_ready, n)
                for c in range(4):
                    hi, lo = unit(m + c, 1, loops)
                    for half in range(2):
                        cols = slice(half * BANK, (half + 1) * BANK)
                        ins = product(ps[:, 4 + half, :], ht_hi[:, c, 0, :], ht_lo[:, c, 0, :],
                                      hi[:, 0, cols], lo[:, 0, cols], first and c == 0, last and c == 3)
                    ins.then_inc(unit_used, 1)

            pe.wait_ge(ident_ready, 1)
            mixer(0, 0)
            dense = (act_hi, act_lo)
            gate_up(DENSE0, dense, T, before=entry(0, PRE_FFN), after=first_tile_done)
            turn_hidden(0, T)
            m = DENSE0 + GU_UNITS
            with pe.Fori(0, DG - 1) as g:
                gate_up(m, dense, T, g)
                dense_down(m + GU_UNITS, T * (g + 1), 4 * g, g)
                turn_hidden(T * (g + 1), T)
            m += BODY * (DG - 1)
            gate_up(m, dense, T, width=BANK // 2)
            m += 4
            hl = [unit(m + c, 1) for c in range(4)]
            pe.wait_ge(ht_lo_ready, T * DG)
            for half in range(2):
                pe.wait_ge(part_added, 4 * (DG - 1) + half + 1)
                cols = slice(half * BANK, (half + 1) * BANK)
                for c in range(4):
                    product(ps[:, 4 + half, :], ht_hi[:, c, 0, :], ht_lo[:, c, 0, :], hl[c][0][:, 0, cols],
                            hl[c][1][:, 0, cols], c == 0, False)
            turn_hidden(T * DG, T, 2)
            hl += [unit(m + c, 1) for c in range(4, 6)]
            chunks = [(ht_hi, ht_lo, c) for c in range(4)] + [(late_hi, late_lo, c) for c in range(2)]
            pe.wait_ge(ht_lo_ready, T * DG + 1)
            for half in range(2):
                cols = slice(half * BANK, (half + 1) * BANK)
                for u in range(4, 6):
                    a_hi, a_lo, c = chunks[u]
                    ins = product(ps[:, 4 + half, :], a_hi[:, c, 0, :], a_lo[:, c, 0, :], hl[u][0][:, 0, cols],
                                  hl[u][1][:, 0, cols], False, u == 5)
                ins.then_inc(part_done, 1)
            pe.wait_ge(ht_lo_ready, T * (DG + 1))
            for u, (a_hi, a_lo, c) in enumerate(chunks):
                if u == 5:
                    turn(1, PRE_MIX, 2)
                for half in range(2):
                    cols = slice(half * BANK, (half + 1) * BANK)
                    ins = product(ps[:, 6 + half, :], a_hi[:, c, 1, :], a_lo[:, c, 1, :], hl[u][0][:, 0, cols],
                                  hl[u][1][:, 0, cols], u == 0, u == 5)
                ins.then_inc(unit_used, 1)

            mixer(1, MIX1)

            turn(1, PRE_FFN + 2, 2)
            pe.wait_ge(act_lo_ready, N_TURNS * DEPTH)
            pe.wait_ge(router_split, 1)
            for k in range(KC):
                for a in (act_hi, act_lo):
                    ins = mm(ps[0:2 * NE, 6, 0:S], wr_split[:, k, :, :].rearrange("p a e -> p (a e)"), a[:, k, :],
                             start=(k == 0 and a is act_hi), stop=(k == KC - 1 and a is act_lo))
            ins.then_inc(lg_parts_done, 1)
            pe.wait_ge(lg_parts_ready, 1)
            for t in range(T):
                ins = mm(ps[:, 5, t * NE:(t + 1) * NE], lg_parts[:, t * P:(t + 1) * P], fold[:, :], start=True,
                         stop=True)
            ins.then_inc(logits_done, 1)
            pe.wait_ge(top_ready, 1)
            c0, c1 = chosen[:, 0, :], chosen[:, 1, :]
            mm(ps[:, 4, 0:NE], upper[:, :], c0, start=True, stop=True)
            mm(ps[:, 4, NE:2 * NE], upper[:, :], c1, start=True, stop=False)
            mm(ps[:, 4, NE:2 * NE], ones[:, :], c0, start=False, stop=True).then_inc(counts_done, 1)
            mm(ps[:, 5, 0:NE], ones[:, :], c0, start=True, stop=False)
            mm(ps[:, 5, 0:NE], ones[:, :], c1, start=False, stop=True).then_inc(totals_done, 1)

            def gather():
                for b in range(2):
                    for i in range(4):
                        k = 4 * b + i
                        for t in range(T):
                            ins = mm(ps[:, (7, 2)[b], i * P:(i + 1) * P], tok[:, t, k * P:(k + 1) * P], sel[:, t, :],
                                     start=(t == 0), stop=(t == T - 1))
                    ins.then_inc(gathered, 1)

            def scatter(e):
                pe.wait_ge(sel_t_ready, e)
                pe.wait_ge(y_act, e)
                pe.wait_ge(y_dve, e)
                for t in range(T):
                    for half in range(2):
                        if t == 0:
                            pe.wait_ge(part_added, ADDED0 - 5 + 4 * e + half)
                        mm(ps[:, PART_BANKS[2 * t + half], :], sel_t[:, t, :], y[:, half * BANK:(half + 1) * BANK],
                           start=True, stop=True).then_inc(part_done, 1)

            pe.wait_ge(tokens_ready, T)
            pe.wait_ge(sel_ready, T)
            gather()
            pe.wait_ge(n_exp_ready, 1)
            n = pe.value_load(n_exp[0:1, 0:1], min_val=NE, max_val=2 * NE)
            picked = (xe_hi, xe_lo)
            with pe.Fori(0, n) as e:
                done = EG * e

                def chunks_ready(t, u):
                    if u % 2 == 0:
                        pe.wait_ge(xe_lo_ready, 2 * e + u // 2 + 1)

                gate_up(MOE0, picked, 1, done, before=chunks_ready)
                with pe.If(e > 0):
                    scatter(e)
                turn_hidden(DENSE_TILES + done, 1)
                m = MOE0 + GU_UNITS
                gate_up(m, picked, 1, done)
                pe.wait_ge(part_added, ADDED0 + 4 * e)
                expert_down(m + GU_UNITS, DENSE_TILES + done + 1, True, False, done)
                turn_hidden(DENSE_TILES + done + 1, 1)
                with pe.Fori(1, EG - 1) as g:
                    gate_up(m, picked, 1, done + g)
                    expert_down(m + GU_UNITS, DENSE_TILES + done + g + 1, False, False, done + g)
                    turn_hidden(DENSE_TILES + done + g + 1, 1)
                pe.wait_ge(sel_ready, T + 2 * T * (e + 1))
                for t in range(T):
                    ins = nc.tensor.transpose(ps[:, 3, t * P:(t + 1) * P], sel_g[:, t, :], ident[:, :])
                ins.then_inc(gathered, 1)
                with pe.If(e < n - 1):
                    gather()
                expert_down(m, DENSE_TILES + done + EG, False, True, done + EG - 1)
            scatter(n)


_INS = ["x", "positions", "pre_mix_norm", "w_in", "attn_sinks", "sgu_ln_g", "sgu_ln_b", "sgu_w", "sgu_b",
        "attn_out_norm", "sgu_out_norm", "w_out", "post_mix_norm", "pre_ffn_norm", "post_ffn_norm", "ffn_w_gate",
        "ffn_w_up", "ffn_w_down", "moe_router", "moe_w_gate", "moe_w_up", "moe_w_down"]


def kernel(**inputs):
    import numpy as _np
    import concourse.bacc as _bacc
    from concourse import mybir as _mybir
    from concourse.bass_utils import run_bass_kernel_spmd as _run

    nc = _bacc.Bacc("TRN2", target_bir_lowering=False, num_devices=1)
    arrays, args = {}, []
    for name in _INS:
        a = _np.ascontiguousarray(inputs[name])
        arrays[f"in_{name}"] = a
        args.append(nc.dram_tensor(f"in_{name}", a.shape, _mybir.dt.from_np(a.dtype), kind="ExternalInput").ap())
    out = nc.dram_tensor("out_0", (1, S, D), _mybir.dt.float32, kind="ExternalOutput").ap()
    trunk(nc, *args, out)
    r = _run(nc, [arrays], core_ids=[0])
    return r.results[0]["out_0"]
```
